# Optimizing a Trainium2 kernel written in Bass

```python
import jax
import jax.numpy as jnp
from jax import lax
import numpy as np
import jax, jax.numpy as jnp

D_MODEL = 1024
BATCH = 1
SEQ = 512
DEPTH = 1

CHUNK = 64
N_MEM = 256
D_MIX = D_MODEL
D_RNN = D_MIX // 2
D_ATT = D_MIX - D_RNN
N_RNN_BLOCKS = 8
RNN_BLOCK = D_RNN // N_RNN_BLOCKS
CONV_WIDTH = 4
RG_LRU_C = 8.0
N_ATT_HEADS = 8
ATT_HEAD_DIM = D_ATT // N_ATT_HEADS
LEFT_CHUNKS = 8
BAND = (LEFT_CHUNKS + 1) * CHUNK
REL_CLIP = 128
N_XHEADS = 4
XHEAD_DIM = D_MODEL // N_XHEADS
N_GROUPS = 4
EXPERTS_PER_GROUP = 8
N_EXPERTS = N_GROUPS * EXPERTS_PER_GROUP
TOP_K = 2
D_EXPERT = D_MODEL // 2
MOE_BLOCK = 128
D_IN_PROJ = 2 * D_RNN + 3 * D_ATT
EPS = 1e-6
NEG_INF = -1e30


def rms_norm(x, w):
    xf = x.astype(jnp.float32)
    y = xf * lax.rsqrt(jnp.mean(xf * xf, axis=-1, keepdims=True) + EPS)
    return (y * w.astype(jnp.float32)).astype(x.dtype)

def _linear_recurrence_combine(left, right):
    a1, b1 = left
    a2, b2 = right
    return a1 * a2, a2 * b1 + b2

def recurrent_group(xr, xg, conv_w, conv_b, w_a, b_a, w_x, b_x, lam):
    b, s, _ = xr.shape
    xc = lax.conv_general_dilated(
        xr, conv_w[:, None, :].astype(xr.dtype), window_strides=(1,),
        padding=[(CONV_WIDTH - 1, 0)], dimension_numbers=('NWC', 'WIO', 'NWC'),
        feature_group_count=D_RNN) + conv_b
    xb = xc.reshape(b, s, N_RNN_BLOCKS, RNN_BLOCK)
    r = jax.nn.sigmoid((jnp.einsum('bsnc,ncd->bsnd', xb, w_a).reshape(b, s, D_RNN) + b_a).astype(jnp.float32))
    i = jax.nn.sigmoid((jnp.einsum('bsnc,ncd->bsnd', xb, w_x).reshape(b, s, D_RNN) + b_x).astype(jnp.float32))
    log_a = -RG_LRU_C * r * jax.nn.softplus(-lam.astype(jnp.float32))
    a = jnp.exp(log_a)
    u = jnp.sqrt(-jnp.expm1(2.0 * log_a)) * (i * xc.astype(jnp.float32))
    _, h = lax.associative_scan(_linear_recurrence_combine, (a, u), axis=1)
    return (jax.nn.gelu(xg.astype(jnp.float32)) * h).astype(xr.dtype)

def rel_bias_band(rel_bias):
    qi = np.arange(CHUNK)[:, None]
    kj = np.arange(BAND)[None, :]
    dist = LEFT_CHUNKS * CHUNK + qi - kj
    idx = np.clip(dist, -REL_CLIP, REL_CLIP) + REL_CLIP
    return rel_bias[:, idx]

def chunk_band_attention(q, k, v, rel_bias):
    b, s, _ = q.shape
    nc = s // CHUNK
    qc = q.reshape(b, nc, CHUNK, N_ATT_HEADS, ATT_HEAD_DIM)
    kc = k.reshape(b, nc, CHUNK, N_ATT_HEADS, ATT_HEAD_DIM)
    vc = v.reshape(b, nc, CHUNK, N_ATT_HEADS, ATT_HEAD_DIM)
    pad = ((0, 0), (LEFT_CHUNKS, 0), (0, 0), (0, 0), (0, 0))
    kp = jnp.pad(kc, pad)
    vp = jnp.pad(vc, pad)
    kb = jnp.concatenate([kp[:, j:j + nc] for j in range(LEFT_CHUNKS + 1)], axis=2)
    vb = jnp.concatenate([vp[:, j:j + nc] for j in range(LEFT_CHUNKS + 1)], axis=2)
    chunk_id = np.arange(nc)[:, None] - LEFT_CHUNKS + np.arange(LEFT_CHUNKS + 1)[None, :]
    valid = np.repeat(chunk_id >= 0, CHUNK, axis=1)
    scores = jnp.einsum('bnqhd,bnkhd->bhnqk', qc, kb, preferred_element_type=jnp.float32)
    scores = scores * (ATT_HEAD_DIM ** -0.5) + rel_bias_band(rel_bias).astype(jnp.float32)[None, :, None]
    scores = jnp.where(valid[None, None, :, None, :], scores, NEG_INF)
    probs = jax.nn.softmax(scores, axis=-1).astype(v.dtype)
    out = jnp.einsum('bhnqk,bnkhd->bnqhd', probs, vb)
    return out.reshape(b, s, D_ATT)

def memory_cross_attention(h, mem_n, wq, wk, wv, wo):
    b, s, _ = h.shape
    m = mem_n.shape[1]
    q = (h @ wq).reshape(b, s, N_XHEADS, XHEAD_DIM)
    k = (mem_n @ wk).reshape(b, m, N_XHEADS, XHEAD_DIM)
    v = (mem_n @ wv).reshape(b, m, N_XHEADS, XHEAD_DIM)
    scores = jnp.einsum('bshd,bmhd->bhsm', q, k, preferred_element_type=jnp.float32) * (XHEAD_DIM ** -0.5)
    probs = jax.nn.softmax(scores, axis=-1).astype(v.dtype)
    out = jnp.einsum('bhsm,bmhd->bshd', probs, v).reshape(b, s, D_MODEL)
    return out @ wo

def routed_experts(ht, expert_idx, combine_w, w_gate, w_up, w_down):
    t, d = ht.shape
    n_slots = t * TOP_K
    flat_e = expert_idx.reshape(-1)
    flat_tok = jnp.repeat(jnp.arange(t, dtype=jnp.int32), TOP_K)
    order = jnp.argsort(flat_e)
    e_sorted = flat_e[order]
    tok_sorted = flat_tok[order]
    w_sorted = combine_w.reshape(-1)[order]
    counts = jnp.bincount(flat_e, length=N_EXPERTS)
    padded = (counts + MOE_BLOCK - 1) // MOE_BLOCK * MOE_BLOCK
    pad_end = jnp.cumsum(padded)
    pad_start = pad_end - padded
    start = jnp.cumsum(counts) - counts
    dest = pad_start[e_sorted] + (jnp.arange(n_slots) - start[e_sorted])
    n_blocks = (n_slots + MOE_BLOCK - 1) // MOE_BLOCK + N_EXPERTS
    n_rows = n_blocks * MOE_BLOCK
    src_tok = jnp.full((n_rows,), t, dtype=jnp.int32).at[dest].set(tok_sorted)
    x_pad = jnp.concatenate([ht, jnp.zeros((1, d), ht.dtype)], axis=0)
    xs = x_pad[src_tok].reshape(n_blocks, MOE_BLOCK, d)
    block_expert = jnp.minimum(
        jnp.searchsorted(pad_end, jnp.arange(n_blocks) * MOE_BLOCK, side='right'), N_EXPERTS - 1)

    def expert_block(args):
        xb, e = args
        g = xb @ w_gate[e]
        u = xb @ w_up[e]
        return (jax.nn.silu(g) * u) @ w_down[e]

    ys = lax.map(expert_block, (xs, block_expert)).reshape(n_rows, d)
    contrib = (ys[dest].astype(jnp.float32) * w_sorted[:, None]).astype(ht.dtype)
    return jnp.zeros((t, d), ht.dtype).at[tok_sorted].add(contrib)

def hierarchical_moe(h, w_group, b_group, w_router, b_router, w_gate, w_up, w_down):
    b, s, d = h.shape
    t = b * s
    ht = h.reshape(t, d)
    g_logits = (ht @ w_group).astype(jnp.float32) + b_group.astype(jnp.float32)
    g_probs = jax.nn.softmax(g_logits, axis=-1)
    g_p, g_idx = lax.top_k(g_probs, 1)
    e_all = jnp.einsum('td,gde->tge', ht, w_router).astype(jnp.float32) + b_router.astype(jnp.float32)
    sel = jnp.broadcast_to(g_idx[:, :, None], (t, 1, EXPERTS_PER_GROUP))
    e_logits = jnp.take_along_axis(e_all, sel, axis=1)[:, 0]
    e_probs = jax.nn.softmax(e_logits, axis=-1)
    e_p, e_idx = lax.top_k(e_probs, TOP_K)
    e_p = e_p / jnp.sum(e_p, axis=-1, keepdims=True)
    combine_w = g_p * e_p
    expert_idx = g_idx * EXPERTS_PER_GROUP + e_idx
    y = routed_experts(ht, expert_idx, combine_w, w_gate, w_up, w_down)
    return y.reshape(b, s, d)

def first_inputs(seed: int = 0) -> dict:
    key = jax.random.key(seed)
    ks = jax.random.split(key, 32)
    f32 = jnp.float32

    def nrm(k, shape, scale):
        return jax.random.normal(k, shape, f32) * scale

    def gain(k, shape):
        return 1.0 + 0.02 * jax.random.normal(k, shape, f32)

    a0 = jax.random.uniform(ks[10], (DEPTH, D_RNN), f32, 0.9, 0.999)
    lam = jnp.log(a0) - jnp.log1p(-a0)
    return {
        'x': nrm(ks[0], (BATCH, SEQ, D_MODEL), 1.0),
        'mem': nrm(ks[1], (BATCH, N_MEM, D_MODEL), 1.0),
        'ln1_w': gain(ks[2], (DEPTH, D_MODEL)),
        'w_in': nrm(ks[3], (DEPTH, D_MODEL, D_IN_PROJ), D_MODEL ** -0.5),
        'conv_w': nrm(ks[4], (DEPTH, CONV_WIDTH, D_RNN), CONV_WIDTH ** -0.5),
        'conv_b': nrm(ks[5], (DEPTH, D_RNN), 0.02),
        'rnn_wa': nrm(ks[6], (DEPTH, N_RNN_BLOCKS, RNN_BLOCK, RNN_BLOCK), RNN_BLOCK ** -0.5),
        'rnn_ba': nrm(ks[7], (DEPTH, D_RNN), 0.02),
        'rnn_wx': nrm(ks[8], (DEPTH, N_RNN_BLOCKS, RNN_BLOCK, RNN_BLOCK), RNN_BLOCK ** -0.5),
        'rnn_bx': nrm(ks[9], (DEPTH, D_RNN), 0.02),
        'rnn_lambda': lam,
        'rel_bias': nrm(ks[11], (DEPTH, N_ATT_HEADS, 2 * REL_CLIP + 1), 0.2),
        'gn_rnn_w': gain(ks[12], (DEPTH, D_RNN)),
        'gn_att_w': gain(ks[13], (DEPTH, D_ATT)),
        'w_out': nrm(ks[14], (DEPTH, D_MIX, D_MODEL), D_MIX ** -0.5),
        'ln2_w': gain(ks[15], (DEPTH, D_MODEL)),
        'mem_norm_w': gain(ks[16], (D_MODEL,)),
        'xq_w': nrm(ks[17], (DEPTH, D_MODEL, D_MODEL), D_MODEL ** -0.5),
        'xk_w': nrm(ks[18], (DEPTH, D_MODEL, D_MODEL), D_MODEL ** -0.5),
        'xv_w': nrm(ks[19], (DEPTH, D_MODEL, D_MODEL), D_MODEL ** -0.5),
        'xo_w': nrm(ks[20], (DEPTH, D_MODEL, D_MODEL), D_MODEL ** -0.5),
        'ln3_w': gain(ks[21], (DEPTH, D_MODEL)),
        'router_group_w': nrm(ks[22], (DEPTH, D_MODEL, N_GROUPS), D_MODEL ** -0.5),
        'router_group_b': nrm(ks[23], (DEPTH, N_GROUPS), 0.01),
        'router_expert_w': nrm(ks[24], (DEPTH, N_GROUPS, D_MODEL, EXPERTS_PER_GROUP), D_MODEL ** -0.5),
        'router_expert_b': nrm(ks[25], (DEPTH, N_GROUPS, EXPERTS_PER_GROUP), 0.01),
        'expert_gate_w': nrm(ks[26], (DEPTH, N_EXPERTS, D_MODEL, D_EXPERT), D_MODEL ** -0.5),
        'expert_up_w': nrm(ks[27], (DEPTH, N_EXPERTS, D_MODEL, D_EXPERT), D_MODEL ** -0.5),
        'expert_down_w': nrm(ks[28], (DEPTH, N_EXPERTS, D_EXPERT, D_MODEL), D_EXPERT ** -0.5),
        'final_norm_w': gain(ks[29], (D_MODEL,)),
    }

def first_block(x, mem, ln1_w, w_in, conv_w, conv_b, rnn_wa, rnn_ba, rnn_wx, rnn_bx, rnn_lambda,
              rel_bias, gn_rnn_w, gn_att_w, w_out, ln2_w, mem_norm_w, xq_w, xk_w, xv_w, xo_w,
              ln3_w, router_group_w, router_group_b, router_expert_w, router_expert_b,
              expert_gate_w, expert_up_w, expert_down_w, final_norm_w):
    mem_n = rms_norm(mem, mem_norm_w)
    for l in range(DEPTH):
        h = rms_norm(x, ln1_w[l])
        proj = h @ w_in[l]
        xr = proj[..., :D_RNN]
        xg = proj[..., D_RNN:2 * D_RNN]
        q = proj[..., 2 * D_RNN:2 * D_RNN + D_ATT]
        k = proj[..., 2 * D_RNN + D_ATT:2 * D_RNN + 2 * D_ATT]
        v = proj[..., 2 * D_RNN + 2 * D_ATT:]
        y_rnn = recurrent_group(xr, xg, conv_w[l], conv_b[l], rnn_wa[l], rnn_ba[l],
                                rnn_wx[l], rnn_bx[l], rnn_lambda[l])
        y_att = chunk_band_attention(q, k, v, rel_bias[l])
        mixed = jnp.concatenate([rms_norm(y_rnn, gn_rnn_w[l]), rms_norm(y_att, gn_att_w[l])], axis=-1)
        x = x + mixed @ w_out[l]
        h = rms_norm(x, ln2_w[l])
        x = x + memory_cross_attention(h, mem_n, xq_w[l], xk_w[l], xv_w[l], xo_w[l])
        h = rms_norm(x, ln3_w[l])
        x = x + hierarchical_moe(h, router_group_w[l], router_group_b[l], router_expert_w[l],
                                 router_expert_b[l], expert_gate_w[l], expert_up_w[l], expert_down_w[l])
    return rms_norm(x, final_norm_w)


DEPTH_2 = 2

GRID_W = 64
D_MIX_2 = D_MODEL
GROUP_W = D_MIX_2 // 4
HEAD_DIM = 64
CONV_A_WIDTH = 31
GQA_HEADS = GROUP_W // HEAD_DIM
GQA_KV_HEADS = 2
CHUNK_2 = 128
SGU_GROUPS = GROUP_W // HEAD_DIM
SGU_GROUP_DIM = GROUP_W // SGU_GROUPS
MLA_HEADS = GROUP_W // HEAD_DIM
MLA_Q_LORA = 3 * D_MODEL // 16
MLA_KV_LORA = D_MODEL // 8
MLA_NOPE = 64
MLA_ROPE = 32
MLA_V = GROUP_W // MLA_HEADS
Q_BLOCK = 128
ROPE_THETA = 10000.0
D_FF = 2816
FFN_CONV_WIDTH = 3
DEEPNORM_ALPHA = (2 * DEPTH_2) ** 0.25
DEEPNORM_BETA = (8 * DEPTH_2) ** -0.25
LN_EPS = 1e-5
RMS_EPS = 1e-6

SPLIT_SIZES = (2 * GROUP_W,
               GQA_HEADS * HEAD_DIM,
               GQA_KV_HEADS * HEAD_DIM,
               GQA_KV_HEADS * HEAD_DIM,
               2 * GROUP_W,
               MLA_Q_LORA,
               MLA_KV_LORA,
               MLA_ROPE)
D_IN_PROJ_2 = sum(SPLIT_SIZES)
SPLIT_POINTS = [sum(SPLIT_SIZES[:i + 1]) for i in range(len(SPLIT_SIZES) - 1)]


def layer_norm(x, g, b):
    xf = x.astype(jnp.float32)
    mu = jnp.mean(xf, axis=-1, keepdims=True)
    xc = xf - mu
    var = jnp.mean(xc * xc, axis=-1, keepdims=True)
    return (xc * lax.rsqrt(var + LN_EPS) * g + b).astype(x.dtype)

def rms_norm_2(x, g):
    xf = x.astype(jnp.float32)
    ms = jnp.mean(xf * xf, axis=-1, keepdims=True)
    return (xf * lax.rsqrt(ms + RMS_EPS) * g).astype(x.dtype)

def depthwise_conv(x, w, b):
    k = w.shape[0]
    c = x.shape[-1]
    y = lax.conv_general_dilated(x, w[:, None, :], window_strides=(1,),
                                 padding=[(k // 2, k // 2)],
                                 dimension_numbers=('NWC', 'WIO', 'NWC'),
                                 feature_group_count=c)
    return y + b

def rope_1d(x, pos):
    d = x.shape[-1]
    half = d // 2
    inv_freq = ROPE_THETA ** (-jnp.arange(half, dtype=jnp.float32) / half)
    ang = pos[:, None] * inv_freq[None, :]
    cos = jnp.cos(ang)[:, None, :]
    sin = jnp.sin(ang)[:, None, :]
    xf = x.astype(jnp.float32)
    x1, x2 = xf[..., :half], xf[..., half:]
    return jnp.concatenate([x1 * cos - x2 * sin, x2 * cos + x1 * sin], axis=-1).astype(x.dtype)

def rope_2d(x, row, col):
    h = x.shape[-1] // 2
    return jnp.concatenate([rope_1d(x[..., :h], row), rope_1d(x[..., h:], col)], axis=-1)

def blocked_attention(q, k, v, scale):
    bsz, seq, hk, g, dk = q.shape
    nb = seq // Q_BLOCK
    qb = q.reshape(bsz, nb, Q_BLOCK, hk, g, dk).transpose(1, 0, 2, 3, 4, 5)

    def one_block(qi):
        s = jnp.einsum('bqhgd,bshd->bhgqs', qi, k, preferred_element_type=jnp.float32) * scale
        p = jax.nn.softmax(s, axis=-1).astype(v.dtype)
        return jnp.einsum('bhgqs,bshd->bqhgd', p, v)

    out = lax.map(one_block, qb)
    return out.transpose(1, 0, 2, 3, 4, 5).reshape(bsz, seq, hk, g, v.shape[-1])

def second_inputs(seed: int = 0) -> dict:
    key = jax.random.key(seed)
    ks = iter(jax.random.split(key, 32))

    def nrm(shape, scale):
        return scale * jax.random.normal(next(ks), shape, dtype=jnp.float32)

    L = DEPTH_2
    return {
        'x': nrm((BATCH, SEQ, D_MODEL), 1.0),
        'ln_in_g': 1.0 + nrm((D_MODEL,), 0.02),
        'ln_in_b': nrm((D_MODEL,), 0.02),
        'w_in': nrm((L, D_MODEL, D_IN_PROJ_2), D_MODEL ** -0.5),
        'conv_a_w': nrm((L, CONV_A_WIDTH, GROUP_W), CONV_A_WIDTH ** -0.5),
        'conv_a_b': nrm((L, GROUP_W), 0.02),
        'ln_a_g': 1.0 + nrm((L, GROUP_W), 0.02),
        'ln_a_b': nrm((L, GROUP_W), 0.02),
        'qk_norm_q': 1.0 + nrm((L, HEAD_DIM), 0.02),
        'qk_norm_k': 1.0 + nrm((L, HEAD_DIM), 0.02),
        'sgu_ln_g': 1.0 + nrm((L, GROUP_W), 0.02),
        'sgu_ln_b': nrm((L, GROUP_W), 0.02),
        'sgu_w': nrm((L, SGU_GROUPS, CHUNK_2, CHUNK_2), CHUNK_2 ** -0.5),
        'sgu_b': 1.0 + nrm((L, SGU_GROUPS, CHUNK_2), 0.02),
        'mla_q_norm': 1.0 + nrm((L, MLA_Q_LORA), 0.02),
        'mla_w_uq': nrm((L, MLA_Q_LORA, MLA_HEADS * (MLA_NOPE + MLA_ROPE)), MLA_Q_LORA ** -0.5),
        'mla_kv_norm': 1.0 + nrm((L, MLA_KV_LORA), 0.02),
        'mla_w_ukv': nrm((L, MLA_KV_LORA, MLA_HEADS * (MLA_NOPE + MLA_V)), MLA_KV_LORA ** -0.5),
        'w_out': nrm((L, D_MIX_2, D_MODEL), DEEPNORM_BETA * D_MIX_2 ** -0.5),
        'ln_mix_g': 1.0 + nrm((L, D_MODEL), 0.02),
        'ln_mix_b': nrm((L, D_MODEL), 0.02),
        'ffn_w_up': nrm((L, D_MODEL, 2 * D_FF), D_MODEL ** -0.5),
        'ffn_conv_w': nrm((L, FFN_CONV_WIDTH, 2 * D_FF), FFN_CONV_WIDTH ** -0.5),
        'ffn_conv_b': nrm((L, 2 * D_FF), 0.02),
        'ffn_w_down': nrm((L, D_FF, D_MODEL), DEEPNORM_BETA * D_FF ** -0.5),
        'ln_ffn_g': 1.0 + nrm((L, D_MODEL), 0.02),
        'ln_ffn_b': nrm((L, D_MODEL), 0.02),
    }

def second_block(x, ln_in_g, ln_in_b, w_in, conv_a_w, conv_a_b, ln_a_g, ln_a_b,
              qk_norm_q, qk_norm_k, sgu_ln_g, sgu_ln_b, sgu_w, sgu_b,
              mla_q_norm, mla_w_uq, mla_kv_norm, mla_w_ukv, w_out, ln_mix_g, ln_mix_b,
              ffn_w_up, ffn_conv_w, ffn_conv_b, ffn_w_down, ln_ffn_g, ln_ffn_b):
    bsz, seq, _ = x.shape
    rows = seq // GRID_W
    row = jnp.repeat(jnp.arange(rows, dtype=jnp.float32), GRID_W)
    col = jnp.tile(jnp.arange(GRID_W, dtype=jnp.float32), rows)

    h = layer_norm(x, ln_in_g, ln_in_b)
    for l in range(DEPTH_2):
        proj = h @ w_in[l]
        a_in, b_q, b_k, b_v, c_in, d_cq, d_ckv, d_kr = jnp.split(proj, SPLIT_POINTS, axis=-1)

        a = a_in[..., :GROUP_W] * jax.nn.sigmoid(a_in[..., GROUP_W:])
        a = depthwise_conv(a, conv_a_w[l], conv_a_b[l])
        o_a = jax.nn.silu(layer_norm(a, ln_a_g[l], ln_a_b[l]))

        q = rms_norm_2(b_q.reshape(bsz, seq, GQA_HEADS, HEAD_DIM), qk_norm_q[l])
        k = rms_norm_2(b_k.reshape(bsz, seq, GQA_KV_HEADS, HEAD_DIM), qk_norm_k[l])
        v = b_v.reshape(bsz, seq, GQA_KV_HEADS, HEAD_DIM)
        q = rope_2d(q, row, col).reshape(bsz, seq, GQA_KV_HEADS, GQA_HEADS // GQA_KV_HEADS, HEAD_DIM)
        k = rope_2d(k, row, col)
        o_b = blocked_attention(q, k, v, HEAD_DIM ** -0.5).reshape(bsz, seq, GROUP_W)

        c = jax.nn.gelu(c_in)
        u, sv = c[..., :GROUP_W], c[..., GROUP_W:]
        sv = layer_norm(sv, sgu_ln_g[l], sgu_ln_b[l])
        sv = sv.reshape(bsz, seq // CHUNK_2, CHUNK_2, SGU_GROUPS, SGU_GROUP_DIM)
        sv = jnp.einsum('gpq,bnqgc->bnpgc', sgu_w[l], sv) + sgu_b[l].T[:, :, None]
        o_c = u * sv.reshape(bsz, seq, GROUP_W)

        qd = (rms_norm_2(d_cq, mla_q_norm[l]) @ mla_w_uq[l]).reshape(bsz, seq, MLA_HEADS, MLA_NOPE + MLA_ROPE)
        kvd = (rms_norm_2(d_ckv, mla_kv_norm[l]) @ mla_w_ukv[l]).reshape(bsz, seq, MLA_HEADS, MLA_NOPE + MLA_V)
        q_nope, q_rope = qd[..., :MLA_NOPE], qd[..., MLA_NOPE:]
        k_nope, v_d = kvd[..., :MLA_NOPE], kvd[..., MLA_NOPE:]
        k_rope = rope_2d(d_kr[:, :, None, :], row, col)
        q_full = jnp.concatenate([q_nope, rope_2d(q_rope, row, col)], axis=-1)
        k_full = jnp.concatenate([k_nope, jnp.broadcast_to(k_rope, (bsz, seq, MLA_HEADS, MLA_ROPE))], axis=-1)
        o_d = blocked_attention(q_full[:, :, :, None, :], k_full, v_d,
                                (MLA_NOPE + MLA_ROPE) ** -0.5).reshape(bsz, seq, GROUP_W)

        mix = jnp.concatenate([o_a, o_b, o_c, o_d], axis=-1) @ w_out[l]
        h = layer_norm(DEEPNORM_ALPHA * h + mix, ln_mix_g[l], ln_mix_b[l])

        up = depthwise_conv(h @ ffn_w_up[l], ffn_conv_w[l], ffn_conv_b[l])
        f = (jax.nn.silu(up[..., :D_FF]) * up[..., D_FF:]) @ ffn_w_down[l]
        h = layer_norm(DEEPNORM_ALPHA * h + f, ln_ffn_g[l], ln_ffn_b[l])
    return h


def setup_inputs(seed=0):
    out = dict(first_inputs(seed))
    for name, value in second_inputs(seed + 1).items():
        if name != "x":
            out[name + "_2"] = value
    return out


def reference(
    x, mem, ln1_w, w_in, conv_w, conv_b, rnn_wa, rnn_ba, rnn_wx, rnn_bx, rnn_lambda, rel_bias,
    gn_rnn_w, gn_att_w, w_out, ln2_w, mem_norm_w, xq_w, xk_w, xv_w, xo_w, ln3_w, router_group_w,
    router_group_b, router_expert_w, router_expert_b, expert_gate_w, expert_up_w, expert_down_w,
    final_norm_w, ln_in_g_2, ln_in_b_2, w_in_2, conv_a_w_2, conv_a_b_2, ln_a_g_2, ln_a_b_2,
    qk_norm_q_2, qk_norm_k_2, sgu_ln_g_2, sgu_ln_b_2, sgu_w_2, sgu_b_2, mla_q_norm_2,
    mla_w_uq_2, mla_kv_norm_2, mla_w_ukv_2, w_out_2, ln_mix_g_2, ln_mix_b_2, ffn_w_up_2,
    ffn_conv_w_2, ffn_conv_b_2, ffn_w_down_2, ln_ffn_g_2, ln_ffn_b_2,
):
    x = first_block(
        x, mem, ln1_w, w_in, conv_w, conv_b, rnn_wa, rnn_ba, rnn_wx, rnn_bx, rnn_lambda,
        rel_bias, gn_rnn_w, gn_att_w, w_out, ln2_w, mem_norm_w, xq_w, xk_w, xv_w, xo_w, ln3_w,
        router_group_w, router_group_b, router_expert_w, router_expert_b, expert_gate_w,
        expert_up_w, expert_down_w, final_norm_w,
    )
    return second_block(
        x, ln_in_g_2, ln_in_b_2, w_in_2, conv_a_w_2, conv_a_b_2, ln_a_g_2, ln_a_b_2,
        qk_norm_q_2, qk_norm_k_2, sgu_ln_g_2, sgu_ln_b_2, sgu_w_2, sgu_b_2, mla_q_norm_2,
        mla_w_uq_2, mla_kv_norm_2, mla_w_ukv_2, w_out_2, ln_mix_g_2, ln_mix_b_2, ffn_w_up_2,
        ffn_conv_w_2, ffn_conv_b_2, ffn_w_down_2, ln_ffn_g_2, ln_ffn_b_2,
    )


_drawn_inputs = setup_inputs


def setup_inputs(seed=0):
    import zlib

    import numpy as np

    out = dict(_drawn_inputs(seed))
    spreads = {}
    factors = {'rnn_ba': 5.763,
     'rnn_bx': 4.884,
     'gn_rnn_w': 2.887,
     'gn_att_w': 2.697,
     'ln2_w': 8.0,
     'mem_norm_w': 5.959,
     'router_group_b': 4.363,
     'router_expert_b': 5.729,
     'final_norm_w': 2.753,
     'conv_a_b_2': 8.0,
     'ln_a_g_2': 8.0,
     'ln_a_b_2': 8.0,
     'qk_norm_q_2': 8.0,
     'qk_norm_k_2': 8.0,
     'sgu_ln_g_2': 8.0,
     'sgu_ln_b_2': 8.0,
     'sgu_b_2': 8.0,
     'mla_q_norm_2': 8.0,
     'mla_kv_norm_2': 8.0,
     'ffn_conv_b_2': 6.622}
    for name, (base, spread) in spreads.items():
        noise = np.random.default_rng([zlib.crc32(name.encode()), seed]).standard_normal(out[name].shape)
        drawn = base * np.exp(spread * noise) if base else spread * noise
        out[name] = jnp.asarray(drawn.astype(out[name].dtype))
    for name, factor in factors.items():
        out[name] = (out[name] * factor).astype(out[name].dtype)
    return out
```

```python
from contextlib import ExitStack

import numpy as np
import concourse.bass as bass
from concourse import mybir

F32 = mybir.dt.float32
U32 = mybir.dt.uint32
ALU = mybir.AluOpType
ACT = mybir.ActivationFunctionType
AX = mybir.AxisListType

P = 128
T = 512
TT = T // P
D = 1024
DC = D // P
MEM = 256
HALF = 512
HC = HALF // P
CONV = 4
HEADS, HD = 8, 64
CLIP = 128
CHUNK = 64
XHEADS = 4
GROUPS, EPG = 4, 8
EXPERTS = GROUPS * EPG
FE = 512
SLOTS = 2 * T
MAXB = EXPERTS + (SLOTS - EXPERTS) // P
TABLE = MAXB + 1
NEG = -1e30
EPS = 1e-6
LN_EPS = 1e-5
L2 = 2
GW = 256
GC = GW // P
CONVA = 31
DFF = 2816
FC = DFF // P
QL, KVL, ROPE = 192, 128, 32
HM = 96
ALPHA = float((2 * L2) ** 0.25)
RING = 3


def layout(fields):
    at, n = {}, 0
    for name, width in fields:
        at[name] = n
        n += width
    return at, n


COLS1 = [("ln1", DC), ("conv_w", CONV * HC), ("conv_b", HC), ("ba", HC), ("bx", HC), ("lam", HC),
         ("gn_rnn", HC), ("gn_att", HC), ("ln2", DC), ("mem", DC), ("ln3", DC), ("final", DC),
         ("lnin_g", DC), ("lnin_b", DC)]
COLS2 = [("ca_w", CONVA * GC), ("ca_b", GC), ("la_g", GC), ("la_b", GC), ("qn", 1), ("kn", 1),
         ("sg_g", GC), ("sg_b", GC), ("mq", 2), ("mkv", 1), ("mix_g", DC), ("mix_b", DC),
         ("fc_w", 3 * 2 * FC), ("fc_b", 2 * FC), ("ffn_g", DC), ("ffn_b", DC)]
C1, N1 = layout(COLS1)
C2, N2 = layout(COLS2)
CONSTS = [("ident", P), ("ones", P), ("lower", P), ("pair", P), ("perm", P), ("perm96", P), ("desc", EPG), ("block", TABLE)]
CK, NK = layout(CONSTS)
NORMS = [("mem", DC), ("ln1", DC), ("gn_rnn", HC), ("gn_att", HC), ("ln2", DC), ("ln3", DC), ("final", DC)]


class Steps:

    def __init__(self, eng, own):
        self.eng, self.own, self.n, self.last, self.told = eng, own, 0, None, {}

    def do(self, ins):
        self.n += 1
        ins.then_inc(self.own, 1)
        self.last = (self.own, self.n)
        return self.last

    def tell(self, ins, sem, base=0):
        self.told[sem.name] = self.told.get(sem.name, 0) + 1
        ins.then_inc(sem, 1)
        self.last = (sem, base + self.told[sem.name])
        return self.last

    def wait(self, step=None):
        sem, n = step or self.last
        self.eng.wait_ge(sem, n)


def build(nc, A, out):
    with ExitStack() as ctx:
        def sb(name, shape, dt=F32):
            return ctx.enter_context(nc.sbuf_tensor(name, shape, dt))

        def sem(name):
            return ctx.enter_context(nc.semaphore(name))

        bank = [ctx.enter_context(nc.psum_tensor(f"bank{i}", [P, T], F32)) for i in range(8)]

        X = sb("X", [P, DC, T])
        H = sb("H", [P, DC, T])
        ring = [sb(f"ring{i}", [P, 8, 512]) for i in range(RING)]
        S = sb("S", [P, FC, T])
        QKVG = sb("QKVG", [P, 16, T])
        MKV = sb("MKV", [P, 8, T])
        AUX = sb("AUX", [P, 8, T])
        cols = sb("cols", [P, N1])
        cols2 = sb("cols2", [P, N2])
        konst = sb("konst", [P, NK])
        eps = sb("eps", [P, 4])
        rstd = sb("rstd", [P, T])
        stats = sb("stats", [P, 4, 32])
        small = sb("small", [P, 64])

        def const(name, n=P):
            return konst[:, CK[name]:CK[name] + n]

        def col(name, i=0, p=P):
            return cols[0:p, C1[name] + i:C1[name] + i + 1]

        ident = const("ident")
        ones = const("ones")

        Q, K, G = QKVG[:, 0:4, :], QKVG[:, 4:8, :], QKVG[:, 12:16, :]
        V = QKVG[:, 8:12, :]
        KM = MKV[:, 0:4, :].rearrange("p a (b m) -> p (a b) m", m=MEM)
        VM = MKV[:, 4:8, :].rearrange("p (a b) n -> p a (b n)", a=2)
        XR, XC, RG, IG, AD = (S[:, 4 * i:4 * i + 4, :] for i in range(5))
        MT = S[:, 16:20, :].rearrange("p a (b m) -> p (a b) m", m=MEM)

        s_const = sem("const_landed")
        s_x = sem("x_landed")
        s_mem = sem("mem_landed")
        s_gates = sem("gate_weights_landed")
        s_ext = sem("bias_steps")
        s_biasd = sem("bias_dma")
        s_bias = sem("bias_ready")
        w_landed = [sem(f"weights_landed{i}") for i in range(RING)]
        act_own, dve_own, pool_own = sem("act_steps"), sem("dve_steps"), sem("pool_steps")
        sq_done, stat_done, rstd_done, h_done = sem("squares"), sem("stat"), sem("rstd_done"), sem("h_chunks")
        tile_done, tile_free = sem("tile_done"), sem("tile_free")
        xc_done, gate_done, gate_free = sem("conv_done"), sem("gates_done"), sem("gates_free")
        y_rnn = sem("y_rnn")
        rg_done, ia_done, nh_done = sem("r_i_done"), sem("decay_done"), sem("root_done")
        att = {k: sem(k) for k in ("scored", "shifted", "shifted_max", "expd", "normed", "turned", "laid", "summed", "att_out")}
        res_done, res_free = sem("res_done"), sem("res_free")

        chunks_before = {}
        n = 0
        for i, (name, c) in enumerate(NORMS):
            chunks_before[name] = (i, n, c)
            n += c

        def wblock(w, j, n=512):
            return w.rearrange("(k p) n -> p k n", p=P)[:, :, j * n:(j + 1) * n]

        first_uses = [(wblock(A["xk_w"], j), tile_done, 4 * j + 4) for j in range(2)]
        first_uses += [(wblock(A["xv_w"], j), tile_done, 8 + 2 * j + 2) for j in range(2)]
        first_uses += [(wblock(A["w_in"], j), tile_done, 12 + 4 * j + 4) for j in range(5)]
        first_uses += [(wblock(A["w_out"], j), res_done, 4 * j + 4) for j in range(2)]
        first_uses += [(wblock(A["xq_w"], j), tile_done, 32 + 4 * j + 4) for j in range(2)]
        first_uses += [(wblock(A["xo_w"], j), res_done, 8 + 4 * j + 4) for j in range(2)]
        assert len(first_uses) % RING == 0

        gatew = small_gates = sb("gatew", [P, 2, HC, P])
        NEXT = P + T - 1
        ext = sb("ext", [HEADS, NEXT])
        ext_dram = nc.dram_tensor("ext_scratch", (HEADS, NEXT), F32).ap()
        ext_copies = nc.dram_tensor("ext_copies", (P, HEADS, NEXT), F32).ap()

        att_cfg = []
        units = []
        for h in range(HEADS):
            r = slice(64 * (h % 2), 64 * (h % 2) + 64)
            for t in range(TT):
                keys = (t + 1) * P
                units.append(dict(
                    scores=[(Q[r, h // 2, t * P:(t + 1) * P], K[r, h // 2, 0:keys])], keys=keys, t=t,
                    bias=(AUX, h), pt=h % 2,
                    values=[(5 + (h // 2) % 2, r, lambda kt, h=h: V[:, kt, h * 64:(h + 1) * 64])],
                    out=[(h // 2, 5 + (h // 2) % 2)] if h % 2 and t == TT - 1 else []))
        att_cfg.append(dict(units=units, sems=att, base=(0, 0), dest=lambda c: S[:, 12 + c, :], scale=1.0))
        units = []
        QX = QKVG[:, 0:8, :]
        for h in range(XHEADS):
            for t in range(TT):
                units.append(dict(
                    scores=[(QX[:, 2 * h + c, t * P:(t + 1) * P], KM[:, 2 * h + c, :]) for c in range(2)],
                    keys=MEM, t=t, bias=None, pt=h % 2,
                    values=[(5 + c, slice(0, P), lambda kt, f=(2 * h + c) * P: VM[:, kt, f:f + P]) for c in range(2)],
                    out=[(2 * h, 5), (2 * h + 1, 6)] if t == TT - 1 else []))
        att_cfg.append(dict(units=units, sems=att, base=(HEADS * TT, HEADS // 2), dest=lambda c: H[:, c, :], scale=float(D // XHEADS) ** -0.5))

        SS = S[:, 0:3, :]
        PT = S[:, 4:12, :].rearrange("p (a k) t -> p a k t", a=2)

        def outs_before(cfg, u):
            return sum(len(x["out"]) for x in cfg["units"][:u])


        NR = GROUPS + EXPERTS
        routw = sb("routw", [P, DC, NR])
        routb = sb("routb", [P, NR])
        route = sb("route", [P, 6, TT])
        slots = sb("slots", [P, 2, TT], U32)
        ids = sb("ids", [P, TT], U32)
        zero = sb("zero", [P, TABLE], U32)
        table = sb("table", [1, 64])
        table_u = sb("table_u", [1, 64], U32)
        idx = sb("idx", [P, 1], U32)
        rows_dram = nc.dram_tensor("rows_scratch", (T, D), F32).ap()
        slot_dram = nc.dram_tensor("slot_tokens", (TABLE * P, 1), U32).ap()
        y_dram = nc.dram_tensor("expert_rows", (TABLE * P, D), F32).ap()
        HT = S[:, 0:8, :].rearrange("p (t a) n -> p t (a n)", t=TT)
        LG = S[:, 12, 0:TT * NR].rearrange("p (t n) -> p t n", t=TT)

        def rt(i, *dims):
            n = TT * int(np.prod(dims))
            a = S[:, 13 + i // 4, (i % 4) * P:(i % 4) * P + n]
            if len(dims) == 2:
                return a.rearrange("p (t g e) -> p t g e", t=TT, e=dims[1])
            return a.rearrange("p (t g) -> p t g", t=TT)

        XB = QKVG[:, 0:2, :].rearrange("p a n -> p (a n)")
        XBT = QKVG[:, 2:4, :].rearrange("p a (c s) -> p (a c) s", s=P)
        SG, PR = QKVG[:, 4, :], QKVG[:, 5, :]
        AT = QKVG[:, 6, :].rearrange("p (c s) -> p c s", s=P)
        YB = QKVG[:, 7:9, :]

        s_rout = sem("router_landed")
        lg_done, lg_read = sem("logits"), sem("logits_read")
        rows_turned, rows_laid, rows_stored = sem("rows_turned"), sem("rows_laid"), sem("rows_stored")
        r_exp, r_d, mask_done, rank_done, slots_done = (sem(f"route_{n}") for n in ("exp", "dve", "mask", "rank", "slots"))
        ids_stored, scattered = sem("ids_stored"), sem("slot_tokens_stored")
        spare = sem("spare_rows_zeroed")
        sp_waits, pool_waits = sem("sync_counted_waits"), sem("gpsimd_counted_waits")
        idx_landed, xb_landed = sem("idx_landed"), sem("rows_gathered")
        g_landed, u_landed, d_landed = sem("gate_w_landed"), sem("up_w_landed"), sem("down_w_landed")
        x_turned, xbt_a, xbt_v = sem("x_turned"), sem("x_laid_act"), sem("x_laid_dve")
        g_done, u_done, sg_done, pr_done = sem("gate_done"), sem("up_done"), sem("silu_done"), sem("product_done")
        a_turned, at_ready, y_done, y_a, y_v, y_stored = (sem(n) for n in ("a_turned", "a_laid", "down_done", "y_laid_act", "y_laid_dve", "y_stored"))
        y_all, y_got, y_sum, y_back, x3 = sem("experts_done"), sem("y_gathered"), sem("y_weighted"), sem("y_turned_back"), sem("x3_tiles")

        def expert_w(w, e):
            return w[bass.ds(e, 1)].rearrange("o (k p) n -> p (o k) n", p=P)

        def wait_counted(eng, sem_, value):
            eng.wait_ge(sem_, value)
            eng.sem_inc(sp_waits if eng is nc.sync else pool_waits, 1)

        def moe_sync(sp):
            sp.wait_ge(*first_uses[-3][1:])
            sp.wait_ge(*first_uses[-2][1:])
            sp.wait_ge(*first_uses[-1][1:])
            sp.wait_ge(slots_done, 1)
            nb = sp.value_load(table_u[0:1, 63:64], min_val=2, max_val=MAXB)

            def gate_up(b, e):
                wait_counted(sp, g_done, b)
                sp.dma_start(ring[0][:, :, :], expert_w(A["expert_gate_w"], e)).then_inc(g_landed, 16)
                wait_counted(sp, u_done, b)
                sp.dma_start(ring[1][:, :, :], expert_w(A["expert_up_w"], e)).then_inc(u_landed, 16)

            def down(b, e):
                wait_counted(sp, y_done, b)
                sp.dma_start(ring[2][:, :, :].rearrange("p (k a) n -> p k (a n)", a=2),
                             expert_w(A["expert_down_w"], e)).then_inc(d_landed, 16)

            e = sp.value_load(table_u[0:1, 0:1], min_val=0, max_val=EXPERTS - 1)
            gate_up(0, e)
            with sp.Fori(1, nb) as b:
                e = sp.value_load(table_u[0:1, bass.ds(b, 1)], min_val=0, max_val=EXPERTS - 1)
                gate_up(b, e)
                e0 = sp.value_load(table_u[0:1, bass.ds(b - 1, 1)], min_val=0, max_val=EXPERTS - 1)
                down(b - 1, e0)
            final = sp.value_load(table_u[0:1, 62:63], min_val=1, max_val=MAXB - 1)
            e = sp.value_load(table_u[0:1, bass.ds(final, 1)], min_val=0, max_val=EXPERTS - 1)
            down(final, e)

        def moe_gpsimd(pool, st):
            st.do(pool.iota(ids[:, :], [[P, TT]], base=0, channel_multiplier=1))
            st.do(pool.memset(zero[:, :], 0))
            st.wait()
            pool.dma_start(slot_dram.rearrange("(p n) o -> p (n o)", p=P), zero[:, :]).then_inc(ids_stored, 16)
            pool.dma_start(routw[:, :, :], A["router_w"].rearrange("(k p) n -> p k n", p=P)).then_inc(s_rout, 16)
            pool.dma_start(routb[:, :], bass.AP(A["router_b"].tensor, 0, [[0, P], [1, NR]])).then_inc(s_rout, 16)
            pool.wait_ge(ids_stored, 16)
            pool.wait_ge(y_rnn, 8)
            pool.wait_ge(att["summed"], 8 * TT)
            st.do(pool.memset(S[:, 10:12, :], 0.0)); st.wait()
            pool.wait_ge(slots_done, 1)
            nb = pool.value_load(table_u[0:1, 63:64], min_val=2, max_val=MAXB)
            for w in range(2):
                for t in range(TT):
                    pool.indirect_dma_start(slot_dram, bass.IndirectOffsetOnAxis(slots[:, w, t:t + 1], 0),
                                            ids[:, t:t + 1], None).then_inc(scattered, 16)
            with pool.Fori(nb, TABLE) as b:
                pool.dma_start(y_dram[bass.ds(b * P, P), :], S[:, 10:12, :].rearrange("p a n -> p (a n)")).then_inc(spare, 16)
            pool.wait_ge(scattered, 16 * 2 * TT)
            pool.wait_ge(rows_stored, 16 * TT)

            def gather(b):
                pool.dma_start(idx[:, :], slot_dram[bass.ds(b * P, P), :]).then_inc(idx_landed, 16)
                wait_counted(pool, idx_landed, b * 16 + 16)
                wait_counted(pool, x_turned, b)
                pool.indirect_dma_start(XB, None, rows_dram, bass.IndirectOffsetOnAxis(idx[:, 0:1], 0)).then_inc(xb_landed, 16)
                wait_counted(pool, xb_landed, b * 16 + 16)

            with pool.Fori(0, nb + 1) as b:
                gather(b)
            pool.wait_ge(y_all, 1)
            wait_counted(pool, spare, pool.value_load(table_u[0:1, 61:62], min_val=1, max_val=TABLE - 2) * 16)
            for t in range(TT):
                for w in range(2):
                    pool.indirect_dma_start(S[:, 4 * t + 2 * w:4 * t + 2 * w + 2, :].rearrange("p a n -> p (a n)"), None, y_dram,
                                            bass.IndirectOffsetOnAxis(slots[:, w, t:t + 1], 0)).then_inc(y_got, 16)
                pool.wait_ge(y_got, 32 * (t + 1))

        def moe_tensor(pe):
            h3 = lambda k: H[:, k, :]
            first = chunks_before["ln3"][1]
            pe.wait_ge(s_rout, 32)
            pe.wait_ge(tile_free, 40)
            pe.wait_ge(h_done, first + DC)
            for t in range(TT):
                for k in range(DC):
                    mm = pe.matmul(bank[5][:, t * NR:(t + 1) * NR], H[:, k, t * P:(t + 1) * P], routw[:, k, :], start=(k == 0), stop=(k == DC - 1))
            mm.then_inc(lg_done, 1)
            pe.wait_ge(res_free, 16)
            for t in range(TT):
                if t >= 2:
                    pe.wait_ge(rows_laid, 2 * (t - 1))
                for j in range(2):
                    for c in range(4):
                        mm = pe.transpose(bank[2 * (t % 2) + j][:, c * P:(c + 1) * P], H[:, 4 * j + c, t * P:(t + 1) * P], ident)
                mm.then_inc(rows_turned, 1)
            pe.wait_ge(mask_done, 1)
            M = rt(9, GROUPS, EPG).rearrange("p t g e -> p t (g e)")
            for t in range(TT):
                for o in range(t + 1):
                    pe.matmul(bank[6][:, t * EXPERTS:(t + 1) * EXPERTS], const("lower") if o == t else ones, M[:, o, :], start=(o == 0), stop=(o == t))
            for t in range(TT):
                mm = pe.matmul(bank[4][:, 0:EXPERTS], ones, M[:, t, :], start=(t == 0), stop=(t == TT - 1))
            mm.then_inc(rank_done, 1)
            pe.wait_ge(slots_done, 1)
            nb = pe.value_load(table_u[0:1, 63:64], min_val=2, max_val=MAXB)
            pe.wait_ge(rows_laid, 2 * TT)

            def turn_x(b):
                pe.wait_ge(xb_landed, b * 16 + 16)
                for j in range(2):
                    for c in range(4):
                        mm = pe.transpose(bank[4 + j][:, c * P:(c + 1) * P], XB[:, (4 * j + c) * P:(4 * j + c + 1) * P], ident)
                mm.then_inc(x_turned, 1)

            def block_in(b):
                for i, (landed, done) in enumerate(((g_landed, g_done), (u_landed, u_done))):
                    pe.wait_ge(landed, b * 16 + 16)
                    if i == 0:
                        pe.wait_ge(xbt_a, b + 1)
                        pe.wait_ge(xbt_v, b + 1)
                    pe.wait_ge((sg_done, pr_done)[i], b)
                    for k in range(DC):
                        mm = pe.matmul(bank[i][:, :], XBT[:, k, :], ring[i][:, k, :], start=(k == 0), stop=(k == DC - 1))
                    mm.then_inc(done, 1)
                turn_x(b + 1)

            def turn_a(b):
                pe.wait_ge(pr_done, b + 1)
                for c in range(4):
                    mm = pe.transpose(bank[6][:, c * P:(c + 1) * P], PR[:, c * P:(c + 1) * P], ident)
                mm.then_inc(a_turned, 1)

            def block_out(b):
                pe.wait_ge(d_landed, b * 16 + 16)
                pe.wait_ge(at_ready, b + 1)
                pe.wait_ge(y_a, b)
                pe.wait_ge(y_v, b)
                for k in range(4):
                    for j in range(2):
                        mm = pe.matmul(bank[2 + j][:, :], AT[:, k, :], ring[2][:, 2 * k + j, :], start=(k == 0), stop=(k == 3))
                mm.then_inc(y_done, 1)

            turn_x(0)
            block_in(0)
            turn_a(0)
            with pe.Fori(1, nb) as b:
                block_in(b)
                block_out(b - 1)
                turn_a(b)
            block_out(pe.value_load(table_u[0:1, 62:63], min_val=1, max_val=MAXB - 1))
            for t in range(TT):
                pe.wait_ge(y_sum, t + 1)
                if t >= 2:
                    pe.wait_ge(x3, t - 1)
                for j in range(2):
                    for c in range(4):
                        mm = pe.transpose(bank[2 * (t % 2) + j][:, c * P:(c + 1) * P], S[:, 4 * t + j, c * P:(c + 1) * P], ident)
                mm.then_inc(y_back, 1)
            pe_stats(pe, "final", lambda c: H[:, c, :])
            pe_layernorm(pe, lnin, lambda c: X[:, c, :], lambda c: pe.wait_ge(h_done, 40 + c + 1))
            layer_tensor(pe)

        def moe_vector(dve, st):
            dve.wait_ge(lg_done, 1)
            st.tell(dve.tensor_tensor(LG, bank[5][:, 0:TT * NR].rearrange("p (t n) -> p t n", t=TT),
                                      routb[:, None, :].to_broadcast([P, TT, NR]), ALU.add), lg_read)
            gl = LG[:, :, 0:GROUPS]
            el = LG[:, :, GROUPS:NR].rearrange("p t (g e) -> p t g e", e=EPG)

            def step(ins):
                st.do(ins)
                st.wait()

            def first_of_max(vals, n, mx, tmp, hot):
                step(dve.tensor_reduce(mx, vals, AX.X, ALU.max))
                step(dve.tensor_tensor(tmp, vals, mx.to_broadcast([P, TT, n]), ALU.is_equal))
                desc = konst[:, CK["desc"] + EPG - n:CK["desc"] + EPG]
                step(dve.tensor_tensor(tmp, tmp, desc[:, None, :].to_broadcast([P, TT, n]), ALU.mult))
                step(dve.tensor_reduce(hot[:, :, 0:1], tmp, AX.X, ALU.max))
                step(dve.tensor_tensor(tmp, tmp, hot[:, :, 0:1].to_broadcast([P, TT, n]), ALU.is_equal))
                step(dve.tensor_copy(hot, tmp))

            st.wait()
            gmax, m1, m2 = rt(0, 1), rt(1, 1), rt(2, 1)
            g_hot, tmp4 = rt(3, GROUPS), rt(4, GROUPS)
            first_of_max(gl, GROUPS, gmax, tmp4, g_hot)
            gd = rt(5, GROUPS)
            st.tell(dve.tensor_tensor(gd, gl, gmax.to_broadcast([P, TT, GROUPS]), ALU.subtract), r_d)
            big = rt(6, GROUPS, EPG)
            esel, tmp8, hot1, hot2 = rt(7, EPG), rt(8, EPG), rt(10, EPG), rt(11, EPG)
            step(dve.tensor_tensor(big, el, g_hot[:, :, :, None].to_broadcast([P, TT, GROUPS, EPG]), ALU.mult))
            step(dve.tensor_reduce(esel, big.rearrange("p t g e -> p t e g"), AX.X, ALU.add))
            first_of_max(esel, EPG, m1, tmp8, hot1)
            step(dve.scalar_tensor_tensor(esel, hot1, -3e38, esel, ALU.mult, ALU.add))
            first_of_max(esel, EPG, m2, tmp8, hot2)
            st.tell(dve.tensor_tensor(m2, m2, m1, ALU.subtract), r_d)
            hots = [rt(12, GROUPS, EPG), rt(13, GROUPS, EPG)]
            for dst, hot in zip(hots, (hot1, hot2)):
                step(dve.tensor_copy(dst, g_hot[:, :, :, None].to_broadcast([P, TT, GROUPS, EPG])))
                step(dve.tensor_tensor(dst, dst, hot[:, :, None, :].to_broadcast([P, TT, GROUPS, EPG]), ALU.mult))
            st.tell(dve.tensor_tensor(rt(9, GROUPS, EPG), hots[0], hots[1], ALU.add), mask_done)
            dve.wait_ge(r_exp, 2)
            gsum, ex = rt(14, 1), rt(15, 1)
            w1, w2 = route[:, 0:1, :].rearrange("p o t -> p t o"), route[:, 1:2, :].rearrange("p o t -> p t o")
            step(dve.tensor_reduce(gsum, gd, AX.X, ALU.add))
            step(dve.tensor_copy(ex, m2))
            step(dve.tensor_scalar(m1, ex, 1.0, None, ALU.add))
            step(dve.tensor_tensor(m1, m1, gsum, ALU.mult))
            step(dve.reciprocal(w1, m1))
            step(dve.tensor_tensor(w2, w1, ex, ALU.mult))
            dve.wait_ge(rank_done, 1)
            cnt, nblk, end, begin = (rt(i, 8)[:, 0:TT, :].rearrange("p t g -> p (t g)") for i in (16, 17, 18, 19))
            step(dve.tensor_copy(cnt, bank[4][:, 0:EXPERTS]))
            step(dve.tensor_scalar(nblk, cnt, 0.0, None, ALU.is_gt))
            for m in range(1, TT):
                step(dve.scalar_tensor_tensor(nblk, cnt, float(m * P), nblk, ALU.is_gt, ALU.add))
            step(dve.tensor_tensor_scan(end, ones[:, 0:EXPERTS], nblk, 0.0, ALU.mult, ALU.add))
            step(dve.tensor_tensor(begin, end, nblk, ALU.subtract))
            step(dve.tensor_scalar(begin, begin, float(P), None, ALU.mult))
            pos = rt(20, EXPERTS)
            step(dve.tensor_tensor(pos, bank[6][:, 0:TT * EXPERTS].rearrange("p (t e) -> p t e", e=EXPERTS),
                                   begin[:, None, :].to_broadcast([P, TT, EXPERTS]), ALU.add))
            for w in range(2):
                hot = hots[w].rearrange("p t g e -> p t (g e)")
                step(dve.tensor_tensor(hot, hot, pos, ALU.mult))
                step(dve.tensor_reduce(route[:, 2 + w:3 + w, :].rearrange("p o t -> p t o"), hot, AX.X, ALU.add))
                step(dve.tensor_copy(slots[:, w, :], route[:, 2 + w, :]))
            cmp = S[0:1, 19:22, :].rearrange("p a n -> p (a n)")[:, 0:TABLE * EXPERTS].rearrange("p (b e) -> p b e", e=EXPERTS)
            blk = konst[0:1, CK["block"]:CK["block"] + TABLE]
            step(dve.tensor_tensor(cmp, end[0:1, None, :].to_broadcast([1, TABLE, EXPERTS]), blk[:, :, None].to_broadcast([1, TABLE, EXPERTS]), ALU.is_le))
            step(dve.tensor_reduce(table[0:1, 0:TABLE, None], cmp, AX.X, ALU.add))
            step(dve.tensor_scalar(table[0:1, 0:TABLE], table[0:1, 0:TABLE], float(EXPERTS - 1), None, ALU.min))
            step(dve.tensor_copy(table_u[0:1, 0:TABLE], table[0:1, 0:TABLE]))
            nblocks = end[0:1, EXPERTS - 1:EXPERTS]
            step(dve.tensor_scalar(table_u[0:1, 62:63], nblocks, -1.0, None, ALU.add))
            step(dve.tensor_scalar(table_u[0:1, 61:62], nblocks, -1.0, float(TABLE), ALU.mult, ALU.add))
            st.tell(dve.tensor_copy(table_u[0:1, 63:64], nblocks), slots_done)
            st.wait()
            nb = dve.value_load(table_u[0:1, 63:64], min_val=2, max_val=MAXB)

            def lay_x(b):
                dve.wait_ge(x_turned, b + 1)
                dve.wait_ge(u_done, b)
                dve.tensor_copy(XBT[:, 4:8, :], bank[5][:, :].rearrange("p (c s) -> p c s", s=P)).then_inc(xbt_v, 1)

            def product(b):
                dve.wait_ge(u_done, b + 1)
                dve.wait_ge(sg_done, b + 1)
                dve.wait_ge(a_turned, b)
                dve.tensor_tensor(PR, SG, bank[1][:, :], ALU.mult).then_inc(pr_done, 1)

            def lay_y(b):
                dve.wait_ge(y_done, b + 1)
                dve.wait_ge(y_stored, b * 16)
                dve.tensor_copy(YB[:, 1, :], bank[3][:, :]).then_inc(y_v, 1)

            lay_x(0)
            product(0)
            lay_x(1)
            with dve.Fori(1, nb) as b:
                product(b)
                lay_x(b + 1)
                lay_y(b - 1)
            lay_y(dve.value_load(table_u[0:1, 62:63], min_val=1, max_val=MAXB - 1))
            for t in range(TT):
                dve.wait_ge(y_got, 32 * (t + 1))
                a, b2 = S[:, 4 * t:4 * t + 2, :], S[:, 4 * t + 2:4 * t + 4, :]
                step(dve.tensor_scalar(a, a, route[:, 0, t:t + 1], None, ALU.mult))
                st.tell(dve.scalar_tensor_tensor(a, b2, route[:, 1, t:t + 1], a, ALU.mult, ALU.add), y_sum)
            for t in range(TT):
                dve.wait_ge(y_back, t + 1)
                for j in range(2):
                    xs = X[:, 4 * j:4 * j + 4, t * P:(t + 1) * P]
                    ins = dve.tensor_tensor(xs, xs, bank[2 * (t % 2) + j][:, :].rearrange("p (c s) -> p c s", s=P), ALU.add)
                    st.tell(ins, x3) if j else st.do(ins)
            dve_norm(dve, st, "final", lambda c: X[:, c, :], lambda c: X[:, c, :])
            dve_layernorm(dve, st, lnin, lambda c: X[:, c, :], lambda c: col("lnin_g", c))
            layer_vector(dve)

        def moe_scalar(act, st):
            for t in range(TT):
                act.wait_ge(rows_turned, t + 1)
                for j in range(2):
                    st.tell(act.activation(HT[:, t, j * 512:(j + 1) * 512], bank[2 * (t % 2) + j][:, :], ACT.Copy), rows_laid)
                st.wait()
                act.dma_start(rows_dram[t * P:(t + 1) * P, :], HT[:, t, :]).then_inc(rows_stored, 16)
            for i, a in enumerate((rt(5, GROUPS), rt(2, 1))):
                act.wait_ge(r_d, i + 1)
                st.tell(act.activation(a, a, ACT.Exp), r_exp)
            act.wait_ge(slots_done, 1)
            nb = act.value_load(table_u[0:1, 63:64], min_val=2, max_val=MAXB)

            def lay_x(b):
                act.wait_ge(x_turned, b + 1)
                act.wait_ge(u_done, b)
                act.activation(XBT[:, 0:4, :], bank[4][:, :].rearrange("p (c s) -> p c s", s=P), ACT.Copy).then_inc(xbt_a, 1)

            def silu(b):
                act.wait_ge(g_done, b + 1)
                act.wait_ge(pr_done, b)
                act.activation(SG, bank[0][:, :], ACT.Silu).then_inc(sg_done, 1)

            def lay_a(b):
                act.wait_ge(a_turned, b + 1)
                act.wait_ge(y_done, b)
                act.activation(AT, bank[6][:, :].rearrange("p (c s) -> p c s", s=P), ACT.Copy).then_inc(at_ready, 1)

            def lay_y(b):
                act.wait_ge(y_done, b + 1)
                act.wait_ge(y_stored, b * 16)
                act.activation(YB[:, 0, :], bank[2][:, :], ACT.Copy).then_inc(y_a, 1)
                act.wait_ge(y_a, b + 1)
                act.wait_ge(y_v, b + 1)
                act.dma_start(y_dram[bass.ds(b * P, P), :], YB[:, :, :].rearrange("p a n -> p (a n)")).then_inc(y_stored, 16)

            lay_x(0)
            silu(0)
            lay_x(1)
            with act.Fori(1, nb) as b:
                lay_a(b - 1)
                silu(b)
                lay_x(b + 1)
                lay_y(b - 1)
            final = act.value_load(table_u[0:1, 62:63], min_val=1, max_val=MAXB - 1)
            lay_a(final)
            lay_y(final)
            act.wait_ge(y_stored, nb * 16)
            act.sem_inc(y_all, 1)
            act.wait_ge(x3, TT)
            for c in range(DC):
                st.tell(act.activation(H[:, c, :], X[:, c, :], ACT.Square), sq_done)
            act_rstd(act, st, "final")
            act_layernorm(act, st, lnin, lambda c: X[:, c, :], lambda c: H[:, c, :], lambda c: X[:, c, :], lambda c: col("lnin_b", c))
            layer_scalar(act)
        def ln_sems(name, chunks, banks=(7, 5)):
            return dict({k: sem(f"{name}_{k}") for k in ("mean", "centred", "squared", "var", "rstd", "scaled", "ready")},
                        chunks=chunks, banks=banks, use=0)

        def pe_layernorm(pe, l, src, ready, sq=lambda c: H[:, c, :]):
            n = l["chunks"]
            for c in range(n):
                ready(c)
                mm = pe.matmul(bank[l["banks"][0]][:, :], ones, src(c), start=(c == 0), stop=(c == n - 1))
            mm.then_inc(l["mean"], 1)
            for c in range(n):
                pe.wait_ge(l["squared"], l["use"] * n + c + 1)
                mm = pe.matmul(bank[l["banks"][1]][:, :], ones, sq(c), start=(c == 0), stop=(c == n - 1))
            mm.then_inc(l["var"], 1)

        def dve_centre(dve, st, l, src):
            dve.wait_ge(l["mean"], l["use"] + 1)
            for c in range(l["chunks"]):
                st.tell(dve.scalar_tensor_tensor(src(c), bank[l["banks"][0]][:, :], -1.0 / (l["chunks"] * P), src(c), ALU.mult, ALU.add), l["centred"])

        def dve_scale(dve, st, l, src, g, r=None):
            r = rstd if r is None else r
            dve.wait_ge(l["rstd"], l["use"] + 1)
            for c in range(l["chunks"]):
                st.tell(dve.scalar_tensor_tensor(src(c), src(c), g(c), r[:, :], ALU.mult, ALU.mult), l["scaled"])

        def dve_layernorm(dve, st, l, src, g, r=None):
            dve_centre(dve, st, l, src)
            dve_scale(dve, st, l, src, g, r)

        def act_variance(act, st, l, src, sq, r=None):
            r = rstd if r is None else r
            for c in range(l["chunks"]):
                act.wait_ge(l["centred"], l["use"] * l["chunks"] + c + 1)
                st.tell(act.activation(sq(c), src(c), ACT.Square), l["squared"])
            act.wait_ge(l["var"], l["use"] + 1)
            st.do(act.activation(r[:, :], bank[l["banks"][1]][:, :], ACT.Ln, scale=1.0 / (l["chunks"] * P), bias=eps[:, 1:2])); st.wait()
            st.tell(act.activation(r[:, :], r[:, :], ACT.Exp, scale=-0.5), l["rstd"])

        def act_shift(act, st, l, src, dst, b, func=ACT.Identity):
            for c in range(l["chunks"]):
                act.wait_ge(l["scaled"], l["use"] * l["chunks"] + c + 1)
                st.tell(act.activation(dst(c), src(c), func, bias=b(c)), l["ready"])

        def act_layernorm(act, st, l, src, sq, dst, b, func=ACT.Identity, r=None):
            act_variance(act, st, l, src, sq, r)
            act_shift(act, st, l, src, dst, b, func)

        lnin = ln_sems("ln_in", DC)

        cos64, sin64, cos96, sin96 = (AUX[:, i, :] for i in range(4))
        UQ = AUX[:, 4:6, :].rearrange("p a n -> p (a n)")[:, 0:2 * 4 * HM].rearrange("p (k n) -> p k n", k=2)
        UKV = AUX[:, 6, :]
        SGW = AUX[:, 7, :].rearrange("p (g q) -> p g q", g=4)
        sgb = sb("sgu_bias", [P, GC, P])
        r_conv, r_sgu = (gatew[:, i, :, :].rearrange("p a n -> p (a n)") for i in range(2))
        AA, SGA, CV, CSQ = (MKV[:, 2 * i:2 * i + 2, :] for i in range(4))
        QG, KG, K2, VG = QKVG[:, 0:2, :], QKVG[:, 2, :], QKVG[:, 3:5, :], QKVG[:, 5, :].rearrange("p (t n) -> p t n", t=TT)
        CQ, CKV, KR, QF = QKVG[:, 6:8, :], QKVG[:, 8, :], QKVG[:, 9, :], QKVG[:, 10:14, :]
        SVT = QKVG[:, 14:16, :].rearrange("p a n -> p (a n)").rearrange("p (t n) -> p t n", t=TT)
        KF, VF = S[:, 12:16, :], S[:, 16:18, :].rearrange("p a n -> p (a n)").rearrange("p (t n) -> p t n", t=TT)
        U, SV = S[:, 18:20, :], S[:, 20:22, :]
        GR = S[:, 7:12, :]
        ROT = S[:, 0:3, :]

        s_tab, s_out = sem("rotary_landed"), sem("out_stored")
        layer_done, layer_go = sem("layer_done"), sem("layer_go")
        lw = [sem(f"layer_weights_landed{i}") for i in range(RING)]
        first_cleared = lw[0].num
        s_small = sem("layer_small_landed")
        l_act, l_dve, l_pool = sem("layer_act_steps"), sem("layer_dve_steps"), sem("layer_pool_steps")
        t_done, t_free = sem("layer_tiles"), sem("layer_tiles_read")
        glu_done, conv_ready = sem("glu_done"), sem("conv_a_done")
        g_sq, g_stat, g_rstd, g_n, g_turned, g_rot = (sem(f"gqa_{n}") for n in ("squared", "stat", "rstd", "normed", "turned", "rotated"))
        m_sq, m_stat, m_rstd, m_n, m_turned, m_rot = (sem(f"mla_{n}") for n in ("squared", "stat", "rstd", "normed", "turned", "rotated"))
        svt_done, svt_laid, mix_done, oc_done = sem("sgu_turned"), sem("sgu_laid"), sem("sgu_mixed"), sem("o_c_done")
        r_done, r_free = sem("layer_res_done"), sem("layer_res_added")
        f_done, f_free, f_conv, f_silu, f_act = sem("up_tiles"), sem("up_tiles_read"), sem("gate_up_ready"), sem("silu_ready"), sem("ffn_product")
        latt = {k: sem(f"{k}_layer") for k in ("scored", "shifted", "expd", "normed", "turned", "laid", "summed", "att_out")}
        ln_a, ln_s = ln_sems("ln_a", GC, (7, 4)), ln_sems("ln_sgu", GC, (5, 5))
        ln_m = ln_sems("ln_out", DC)
        ln_f = dict(ln_m, use=1)
        last_cleared = ln_m["ready"].num

        def col2(name, i=0, p=P):
            return cols2[0:p, C2[name] + i:C2[name] + i + 1]

        def up_block(l, j):
            w = A["ffn_w_up"][bass.ds(l, 1)].rearrange("o (k p) (h n) -> h p (o k) n", p=P, h=2)
            return [w[h, :, :, j * 256:(j + 1) * 256] for h in range(2)]

        def layer_uses(l):
            w_in = A["w_in_2"][bass.ds(l, 1)].rearrange("o (k p) n -> p (o k) n", p=P)
            w_out = A["w_out_2"][bass.ds(l, 1)].rearrange("o (k p) n -> p (o k) n", p=P)
            down = A["ffn_w_down"][bass.ds(l, 1)].rearrange("o (k p) n -> p (o k) n", p=P)
            whole = lambda r: r[:, :, :]
            uses = [([(whole, w_in[:, :, 512 * j:512 * (j + 1)])], t_done, 4 * j + 4) for j in range(3)]
            uses += [([(lambda r: r[:, :, 0:QL + KVL + ROPE], w_in[:, :, 1536:1536 + QL + KVL + ROPE])], t_done, 16)]
            uses += [([(whole, w_out[:, :, 512 * j:512 * (j + 1)])], r_done, 4 * j + 4) for j in range(2)]
            uses += [([(lambda r, h=h: r[:, :, 256 * h:256 * (h + 1)], up_block(l, j)[h]) for h in range(2)], f_done, 4 * j + 4)
                     for j in range(FC // 2)]
            uses += [([(down_slot, down[:, :, P * m:P * (m + 1)])], r_done, DC + m + 1) for m in range(DC)]
            return uses

        def down_slot(r):
            return r[:, :, :].rearrange("p a n -> p (a n)")[:, 0:FC * P].rearrange("p (k n) -> p k n", n=P)

        N_USES = 4 + 2 + FC // 2 + DC

        def end_of_layer(eng, l):
            eng.sem_inc(layer_done, 1)
            if eng is nc.sync:
                wait_counted(eng, layer_go, l + 1)
            else:
                eng.wait_ge(layer_go, l + 1)

        l_units = []
        for h in range(8):
            r = slice(64 * (h % 2), 64 * (h % 2) + 64)
            for t in range(TT):
                tt = slice(t * P, (t + 1) * P)
                if h < 4:
                    sc = (QG[r, h // 2, tt], K2[r, h // 2, :])
                    val = lambda kt, h=h: VG[:, kt, 64 * (h // 2):64 * (h // 2) + 64]
                else:
                    sc = (QF[0:HM, h - 4, tt], KF[0:HM, h - 4, :])
                    val = lambda kt, h=h: VF[:, kt, 64 * (h - 4):64 * (h - 4) + 64]
                l_units.append(dict(scores=[sc], keys=T, t=t, bias=None, pt=h % 2, scale=float(64 if h < 4 else HM) ** -0.5,
                                    values=[(5 + (h // 2) % 2, r, val)],
                                    out=[(h // 2, 5 + (h // 2) % 2)] if h % 2 and t == TT - 1 else []))
        l_cfg = dict(units=l_units, sems=latt, base=(0, 0), dest=lambda c: H[:, (2, 3, 6, 7)[c], :], scale=1.0)

        def layer_sync(sp):
            sp.wait_ge(att["shifted_max"], 8 * TT)
            sp.dma_start(AUX[:, 0:4, :], A["rotary"]).then_inc(s_tab, 16)
            wait_counted(sp, y_done, sp.value_load(table_u[0:1, 63:64], min_val=2, max_val=MAXB))
            with sp.Fori(0, L2) as l:
                sp.dma_start(cols2[:, :], A["cols2"][bass.ds(l, 1)].rearrange("o p n -> p (o n)")).then_inc(s_small, 16)
                sp.dma_start(UKV, A["w_ukv"][bass.ds(l, 1)].rearrange("o p n -> p (o n)")).then_inc(s_small, 16)
                sp.dma_start(UQ[:, 0, :], A["w_uq"][bass.ds(l, 1), 0:P, :].rearrange("o p n -> p (o n)")).then_inc(s_small, 16)
                sp.dma_start(UQ[0:QL - P, 1, :], A["w_uq"][bass.ds(l, 1), P:QL, :].rearrange("o p n -> p (o n)")).then_inc(s_small, 16)
                sp.dma_start(SGW, A["sgu_wT"][bass.ds(l, 1)].rearrange("o q g p -> q (o g) p")).then_inc(s_small, 16)
                for g in range(4):
                    src = A["sgu_b"][bass.ds(l, 1), g:g + 1, :].rearrange("o g p -> o (g p)")
                    sp.dma_start(sgb[64 * (g % 2):64 * (g % 2) + 64, g // 2, :], src.to_broadcast([64, P])).then_inc(s_small, 16)
                uses = layer_uses(l)
                assert len(uses) == N_USES
                for n, (parts, _, _) in enumerate(uses):
                    if n >= RING:
                        sp.wait_ge(*uses[n - RING][1:])
                    for place, src in parts:
                        sp.dma_start(place(ring[n % RING]), src).then_inc(lw[n % RING], 16)
                end_of_layer(sp, l)

        def layer_gpsimd(pool):
            with pool.Fori(0, L2) as l:
                st = Steps(pool, l_pool)
                for j in range(FC // 2):
                    for i in range(2):
                        pool.wait_ge(f_silu, 2 * j + i + 1)
                        pool.wait_ge(f_conv, 4 * j + 2 + i + 1)
                        b = 2 * (j % 2) + i
                        st.tell(pool.tensor_tensor(S[:, 2 * j + i, :], QKVG[:, b, :], QKVG[:, 4 + b, :], ALU.mult), f_act)
                st.wait()
                wait_counted(pool, layer_done, 4 * l + 4)
                pool.sem_clear(range(first_cleared, last_cleared + 1))
                pool.sem_inc(layer_go, 1)

        def layer_tensor(pe):
            h = lambda k: H[:, k, :]
            x = lambda k: X[:, k, :]
            pe.wait_ge(s_tab, 16)
            pe.wait_ge(lnin["ready"], DC)
            with pe.Fori(0, L2) as l:
                use = [0]
                landed = [0] * RING

                def slot():
                    n = use[0]
                    use[0] += 1
                    landed[n % RING] += 32 if 6 <= n < 6 + FC // 2 else 16
                    pe.wait_ge(lw[n % RING], landed[n % RING])
                    return ring[n % RING]

                read = {}

                def take(b):
                    if b in read:
                        pe.wait_ge(*read[b])

                tiles = [0]

                def tile(mms, count=tiles, done=t_done, free=t_free):
                    n = count[0]
                    if n >= 4:
                        pe.wait_ge(free, n - 3)
                    mms(bank[n % 4]).then_inc(done, 1)
                    count[0] += 1

                def products(w, m0, m, src, rows=slice(0, P), k_tiles=DC):
                    def mms(b):
                        for k in range(k_tiles):
                            mm = pe.matmul(b[rows, :], w[:, k, m0:m0 + m], src(k), start=(k == 0), stop=(k == k_tiles - 1))
                        return mm
                    return mms

                pe.wait_ge(s_small, 16 * 9)
                w = slot()
                for m in range(4):
                    tile(products(w, m * P, P, x))
                w = slot()
                for m in range(3):
                    tile(products(w, m * P, P, x))

                def values(b):
                    for t in range(TT):
                        for k in range(DC):
                            mm = pe.matmul(b[:, t * P:(t + 1) * P], X[:, k, t * P:(t + 1) * P], w[:, k, 3 * P:4 * P], start=(k == 0), stop=(k == DC - 1))
                    return mm
                tile(values)
                w = slot()
                for m in range(4):
                    tile(products(w, m * P, P, x))
                for i in range(3):
                    pe.wait_ge(g_sq, i + 1)
                    pe.matmul(bank[4 + i][:, :], const("pair"), S[:, 4 + i, :], start=True, stop=True).then_inc(g_stat, 1)
                    read[4 + i] = (g_rstd, i + 1)
                w = slot()
                tile(products(w, 0, P, x))
                tile(products(w, P, QL - P, x, slice(0, QL - P)))
                tile(products(w, QL, KVL, x))
                tile(products(w, QL + KVL, ROPE, x, slice(64, HM)))
                pe.wait_ge(m_sq, 2)
                pe.matmul(bank[7][:, :], ones, H[:, 2, :], start=True, stop=False)
                pe.matmul(bank[7][:, :], ones[0:QL - P, :], H[0:QL - P, 3, :], start=False, stop=True).then_inc(m_stat, 1)
                read[7] = (m_rstd, 1)
                pe.wait_ge(m_sq, 3)
                take(4)
                pe.matmul(bank[4][:, :], ones, H[:, 6, :], start=True, stop=True).then_inc(m_stat, 1)
                read[4] = (m_rstd, 2)
                take(5)
                for c in range(GC):
                    pe.wait_ge(t_free, 11 + c)
                    mm = pe.matmul(bank[5][:, :], ones, SV[:, c, :], start=(c == 0), stop=(c == GC - 1))
                mm.then_inc(ln_s["mean"], 1)
                read[5] = (ln_s["centred"], GC)
                for i, b in enumerate((6, 7, 4)):
                    pe.wait_ge(g_n, i + 1)
                    take(b)
                    pe.matmul(bank[b][:, :], const("perm"), (QG[:, 0, :], QG[:, 1, :], KG)[i], start=True, stop=True).then_inc(g_turned, 1)
                    read[b] = (g_rot, i + 1)
                take(5)
                for c in range(GC):
                    pe.wait_ge(ln_s["squared"], c + 1)
                    mm = pe.matmul(bank[5][:, :], ones, H[:, 4 + c, :], start=(c == 0), stop=(c == GC - 1))
                mm.then_inc(ln_s["var"], 1)
                read[5] = (ln_s["rstd"], 1)
                for hh in range(4):
                    def mms(b):
                        pe.wait_ge(m_n, 2)
                        pe.matmul(b[0:HM, :], UQ[:, 0, hh * HM:(hh + 1) * HM], CQ[:, 0, :], start=True, stop=False)
                        return pe.matmul(b[0:HM, :], UQ[0:QL - P, 1, hh * HM:(hh + 1) * HM], CQ[0:QL - P, 1, :], start=False, stop=True)
                    tile(mms)
                for hh in range(4):
                    def mms(b):
                        pe.wait_ge(m_n, 3)
                        return pe.matmul(b[0:64, :], UKV[:, hh * P:hh * P + 64], CKV, start=True, stop=True)
                    tile(mms)
                for half in range(2):
                    def mms(b):
                        for t in range(2):
                            tok = slice((2 * half + t) * P, (2 * half + t + 1) * P)
                            mm = pe.matmul(b[:, t * 256:(t + 1) * 256], CKV[:, tok],
                                           UKV.rearrange("p (h n) -> p h n", h=4)[:, :, 64:128], start=True, stop=True)
                        return mm
                    tile(mms)
                take(6)
                pe.wait_ge(t_free, 16)
                pe.matmul(bank[6][64:HM, :], const("perm96")[64:HM, 64:HM], KR[64:HM, :], start=True, stop=True).then_inc(m_turned, 1)
                read[6] = (m_rot, 1)
                for hh, b in enumerate((7, 4, 5, 6)):
                    take(b)
                    pe.wait_ge(t_free, 17 + hh)
                    pe.matmul(bank[b][0:HM, :], const("perm96")[0:HM, 0:HM], QF[0:HM, hh, :], start=True, stop=True).then_inc(m_turned, 1)
                    read[b] = (m_rot, 2 + hh)
                take(7)
                take(4)
                pe_layernorm(pe, ln_a, lambda c: CV[:, c, :], lambda c: pe.wait_ge(conv_ready, c + 1), lambda c: CSQ[:, c, :])
                read[7], read[4] = (ln_a["centred"], GC), (ln_a["rstd"], 1)
                for c, b in enumerate((5, 6)):
                    take(b)
                    pe.wait_ge(ln_s["ready"], c + 1)
                    for t in range(TT):
                        mm = pe.transpose(bank[b][:, t * P:(t + 1) * P], SV[:, c, t * P:(t + 1) * P], ident)
                    mm.then_inc(svt_done, 1)
                    read[b] = (svt_laid, c + 1)
                pe.wait_ge(svt_laid, GC)
                for c, b in enumerate((7, 4)):
                    take(b)
                    for g in (2 * c, 2 * c + 1):
                        for t in range(TT):
                            mm = pe.matmul(bank[b][64 * (g % 2):64 * (g % 2) + 64, t * P:(t + 1) * P], SVT[:, t, g * 64:(g + 1) * 64],
                                           SGW[:, g, :], start=True, stop=True)
                    mm.then_inc(mix_done, 1)
                    read[b] = (oc_done, c + 1)
                pe.wait_ge(t_free, 26)
                for b in (4, 5, 6):
                    take(b)
                pe.wait_ge(m_rot, 5)
                pe_attention(pe, l_cfg)
                pe.wait_ge(latt["att_out"], 4)
                pe.wait_ge(ln_a["ready"], GC)
                pe.wait_ge(oc_done, 2)
                rt_ = [0]
                res = dict(count=rt_, done=r_done, free=r_free)
                for j in range(2):
                    w = slot()
                    for m in range(4):
                        tile(products(w, m * P, P, h), **res)
                pe_layernorm(pe, ln_m, x, lambda c: pe.wait_ge(r_free, c + 1))
                ft = [0]
                for j in range(FC // 2):
                    w = slot()
                    for m in range(4):
                        def mms(b):
                            for k in range(DC):
                                if j == 0 and m == 0:
                                    pe.wait_ge(ln_m["ready"], k + 1)
                                mm = pe.matmul(b[:, :], w[:, k, m * P:(m + 1) * P], X[:, k, :], start=(k == 0), stop=(k == DC - 1))
                            return mm
                        tile(mms, count=ft, done=f_done, free=f_free)
                pe.wait_ge(f_free, 2 * FC)
                for m in range(DC):
                    w = down_slot(slot())

                    def mms(b):
                        for k in range(FC):
                            if m == 0:
                                pe.wait_ge(f_act, k + 1)
                            mm = pe.matmul(b[:, :], w[:, k, :], S[:, k, :], start=(k == 0), stop=(k == FC - 1))
                        return mm
                    tile(mms, **res)
                pe_layernorm(pe, ln_f, x, lambda c: pe.wait_ge(r_free, DC + c + 1))
                pe.wait_ge(ln_f["ready"], 2 * DC)
                end_of_layer(pe, l)

        def layer_vector(dve):
            with dve.Fori(0, L2) as l:
                st = Steps(dve, l_dve)
                x = lambda k: X[:, k, :]

                def step(ins):
                    st.do(ins)
                    st.wait()

                dve.wait_ge(s_small, 16 * 9)
                for c in range(GC):
                    dve.wait_ge(t_free, 3 + c)
                    st.do(dve.tensor_tensor(AA[:, c, :], AA[:, c, :], SGA[:, c, :], ALU.mult))
                st.wait()
                last = [None] * GC
                for n, i in enumerate([CONVA // 2] + [i for i in range(CONVA) if i != CONVA // 2]):
                    for c in range(GC):
                        o = i - CONVA // 2
                        w = col2("ca_w", i * GC + c)
                        lo, hi = max(0, -o), T - max(0, o)
                        if n == 0:
                            last[c] = st.do(dve.tensor_scalar(CV[:, c, :], AA[:, c, :], w, col2("ca_b", c), ALU.mult, ALU.add))
                            continue
                        st.wait(last[c])
                        ins = dve.scalar_tensor_tensor(CV[:, c, lo:hi], AA[:, c, lo + o:hi + o], w, CV[:, c, lo:hi], ALU.mult, ALU.add)
                        last[c] = st.tell(ins, conv_ready) if n == CONVA - 1 else st.do(ins)
                qk = (QG[:, 0, :], QG[:, 1, :], KG)
                for i in range(3):
                    dve.wait_ge(g_rstd, i + 1)
                    st.tell(dve.scalar_tensor_tensor(qk[i], qk[i], col2("kn" if i == 2 else "qn"), GR[:, i, :], ALU.mult, ALU.mult), g_n)
                dve_centre(dve, st, ln_s, lambda c: SV[:, c, :])
                for i, (a, p) in enumerate(((CQ[:, 0, :], P), (CQ[:, 1, :], QL - P), (CKV, P))):
                    dve.wait_ge(m_rstd, 1 + i // 2)
                    w = col2("mkv") if i == 2 else col2("mq", i, p)
                    st.tell(dve.scalar_tensor_tensor(a[0:p], a[0:p], w, GR[0:p, 3 + i // 2, :], ALU.mult, ALU.mult), m_n)

                def rotate(a, b, r, cos, sin, done, i):
                    step(dve.tensor_tensor(ROT[r, i % 3, :], bank[b][r, :], sin[r], ALU.mult))
                    step(dve.tensor_tensor(a[r], a[r], cos[r], ALU.mult))
                    ins = dve.tensor_tensor(a[r], a[r], ROT[r, i % 3, :], ALU.add)
                    st.tell(ins, done) if done else st.do(ins)
                    st.wait()

                for i, b in enumerate((6, 7, 4)):
                    dve.wait_ge(g_turned, i + 1)
                    rotate(qk[i], b, slice(0, P), cos64, sin64, g_rot, i)
                for kv in range(2):
                    for half in range(2):
                        st.do(dve.tensor_copy(K2[64 * half:64 * half + 64, kv, :], KG[64 * kv:64 * kv + 64, :]))
                dve_scale(dve, st, ln_s, lambda c: SV[:, c, :], lambda c: col2("sg_g", c), r_sgu)
                dve.wait_ge(m_turned, 1)
                rotate(KR, 6, slice(64, HM), cos96, sin96, None, 0)
                for hh in range(3):
                    st.do(dve.tensor_copy(KF[64:HM, hh, :], KR[64:HM, :]))
                st.tell(dve.tensor_copy(KF[64:HM, 3, :], KR[64:HM, :]), m_rot)
                for hh, b in enumerate((7, 4, 5, 6)):
                    dve.wait_ge(m_turned, 2 + hh)
                    rotate(QF[:, hh, :], b, slice(0, HM), cos96, sin96, m_rot, 1 + hh)
                dve_layernorm(dve, st, ln_a, lambda c: CV[:, c, :], lambda c: col2("la_g", c), r_conv)
                for c, b in enumerate((7, 4)):
                    dve.wait_ge(mix_done, c + 1)
                    hb = H[:, 4 + c, :].rearrange("p (t n) -> p t n", t=TT)
                    step(dve.tensor_tensor(hb, bank[b][:, :].rearrange("p (t n) -> p t n", t=TT),
                                           sgb[:, c, None, :].to_broadcast([P, TT, P]), ALU.add))
                    st.tell(dve.tensor_tensor(H[:, 4 + c, :], H[:, 4 + c, :], U[:, c, :], ALU.mult), oc_done)
                dve_attention(dve, st, l_cfg)

                def residual(first):
                    for m in range(DC):
                        dve.wait_ge(r_done, first + m + 1)
                        st.tell(dve.scalar_tensor_tensor(X[:, m, :], X[:, m, :], ALPHA, bank[m % 4][:, :], ALU.mult, ALU.add), r_free)

                residual(0)
                dve_layernorm(dve, st, ln_m, x, lambda c: col2("mix_g", c))
                for j in range(FC // 2):
                    for m in range(4):
                        n = 4 * j + m
                        b = 4 * (m // 2) + 2 * (j % 2) + m % 2
                        f = FC * (m // 2) + 2 * j + m % 2
                        src, dst = bank[n % 4], QKVG[:, b, :]
                        dve.wait_ge(f_done, n + 1)
                        if j >= 2:
                            dve.wait_ge(f_act, 2 * (j - 2) + m % 2 + 1)
                        tap = lambda i: col2("fc_w", i * 2 * FC + f)
                        step(dve.tensor_scalar(dst, src[:, :], tap(1), col2("fc_b", f), ALU.mult, ALU.add))
                        step(dve.scalar_tensor_tensor(dst[:, 1:T], src[:, 0:T - 1], tap(0), dst[:, 1:T], ALU.mult, ALU.add))
                        st.tell(dve.scalar_tensor_tensor(dst[:, 0:T - 1], src[:, 1:T], tap(2), dst[:, 0:T - 1], ALU.mult, ALU.add), f_free)
                        st.wait()
                        dve.sem_inc(f_conv, 1)
                residual(DC)
                dve_layernorm(dve, st, ln_f, x, lambda c: col2("ffn_g", c))
                st.wait()
                end_of_layer(dve, l)

        def layer_scalar(act):
            with act.Fori(0, L2) as l:
                st = Steps(act, l_act)
                n = [0]
                act.wait_ge(s_small, 16 * 9)

                def evac(dst, rows=slice(0, P), func=ACT.Copy):
                    act.wait_ge(t_done, n[0] + 1)
                    st.tell(act.activation(dst, bank[n[0] % 4][rows, :], func), t_free)
                    n[0] += 1

                def rms(i, b, scale, done):
                    st.do(act.activation(GR[:, i, :], bank[b][:, :], ACT.Ln, scale=scale, bias=eps[:, 0:1])); st.wait()
                    st.tell(act.activation(GR[:, i, :], GR[:, i, :], ACT.Exp, scale=-0.5), done)

                for c in range(2):
                    evac(AA[:, c, :])
                for c in range(2):
                    evac(SGA[:, c, :], func=ACT.Sigmoid)
                qk = (QG[:, 0, :], QG[:, 1, :], KG)
                for i in range(3):
                    evac(qk[i])
                    st.wait()
                    st.tell(act.activation(S[:, 4 + i, :], qk[i], ACT.Square), g_sq)
                evac(VG.rearrange("p t n -> p (t n)"))
                for c in range(2):
                    evac(U[:, c, :], func=ACT.Gelu_apprx_tanh)
                for c in range(2):
                    evac(SV[:, c, :], func=ACT.Gelu_apprx_tanh)
                for i in range(3):
                    act.wait_ge(g_stat, i + 1)
                    rms(i, 4 + i, 1.0 / 64, g_rstd)
                for a, sq, p in ((CQ[:, 0, :], H[:, 2, :], P), (CQ[:, 1, :], H[:, 3, :], QL - P), (CKV, H[:, 6, :], P)):
                    evac(a[0:p], slice(0, p))
                    st.wait()
                    st.tell(act.activation(sq[0:p], a[0:p], ACT.Square), m_sq)
                evac(KR[64:HM, :], slice(64, HM))
                for i in range(2):
                    act.wait_ge(m_stat, i + 1)
                    rms(3 + i, (7, 4)[i], 1.0 / (QL, KVL)[i], m_rstd)
                act_variance(act, st, ln_s, lambda c: SV[:, c, :], lambda c: H[:, 4 + c, :], r_sgu)
                for hh in range(4):
                    evac(QF[0:HM, hh, :], slice(0, HM))
                for hh in range(4):
                    evac(KF[0:64, hh, :], slice(0, 64))
                for half in range(2):
                    evac(VF[:, 2 * half:2 * half + 2, :].rearrange("p t n -> p (t n)"))
                act_variance(act, st, ln_a, lambda c: CV[:, c, :], lambda c: CSQ[:, c, :], r_conv)
                act_shift(act, st, ln_s, lambda c: SV[:, c, :], lambda c: SV[:, c, :], lambda c: col2("sg_b", c))
                for c, b in enumerate((5, 6)):
                    act.wait_ge(svt_done, c + 1)
                    st.tell(act.activation(SVT[:, :, c * P:(c + 1) * P], bank[b][:, :].rearrange("p (t n) -> p t n", t=TT), ACT.Copy), svt_laid)
                act_shift(act, st, ln_a, lambda c: CV[:, c, :], lambda c: H[:, c, :], lambda c: col2("la_b", c), ACT.Silu)
                act_attention(act, st, l_cfg)
                x, h = (lambda k: X[:, k, :]), (lambda k: H[:, k, :])
                act.wait_ge(r_done, DC)
                act_layernorm(act, st, ln_m, x, h, x, lambda c: col2("mix_b", c))
                for j in range(FC // 2):
                    for i in range(2):
                        act.wait_ge(f_conv, 4 * j + i + 1)
                        b = 2 * (j % 2) + i
                        st.tell(act.activation(QKVG[:, b, :], QKVG[:, b, :], ACT.Silu), f_silu)
                act_layernorm(act, st, ln_f, x, h, x, lambda c: col2("ffn_b", c))
                st.wait()
                end_of_layer(act, l)
            act.dma_start(out.rearrange("(k p) t -> p k t", p=P), X[:, :, :]).then_inc(s_out, 16)
            act.wait_ge(s_out, 16)

        block = ctx.enter_context(nc.Block())

        @block.sync
        def _(sp):
            sp.dma_start(konst[:, :], A["konst"]).then_inc(s_const, 16)
            sp.dma_start(cols[:, :], A["cols"]).then_inc(s_const, 16)
            sp.dma_start(MT, A["memT"].rearrange("(k p) m -> p k m", p=P)).then_inc(s_mem, 16)
            for n, (src, _, _) in enumerate(first_uses):
                if n == 2:
                    sp.dma_start(X[:, :, :], A["xT"].rearrange("(k p) t -> p k t", p=P)).then_inc(s_x, 16)
                if n >= RING:
                    sp.wait_ge(*first_uses[n - RING][1:])
                sp.dma_start(ring[n % RING][:, :, :], src).then_inc(w_landed[n % RING], 16)
            moe_sync(sp)
            layer_sync(sp)

        @block.gpsimd
        def _(pool):
            st = Steps(pool, pool_own)
            st.do(pool.memset(gatew[:, :, :, :], 0.0))
            st.do(pool.memset(ext[:, :], 0.0))
            st.wait()
            for g, w in enumerate(("rnn_wa", "rnn_wx")):
                for half in range(2):
                    pool.dma_start(gatew[64 * half:64 * half + 64, g, :, 64 * half:64 * half + 64],
                                   A[w].rearrange("(c h) i o -> h i c o", h=2)[half]).then_inc(s_gates, 16)
            pool.dma_start(ext[:, NEXT - 2 * CLIP:], A["rel_rev"][:, 0:2 * CLIP]).then_inc(s_biasd, 16)
            pool.wait_ge(s_biasd, 16)
            st.do(pool.tensor_copy(ext[:, 0:NEXT - 2 * CLIP],
                                   ext[:, NEXT - 2 * CLIP:NEXT - 2 * CLIP + 1].to_broadcast([HEADS, NEXT - 2 * CLIP])))
            st.wait()
            pool.dma_start(ext_dram, ext[:, :]).then_inc(s_biasd, 16)
            pool.wait_ge(s_biasd, 32)
            pool.dma_start(ext_copies, bass.AP(ext_dram.tensor, 0, [[0, P], [NEXT, HEADS], [1, NEXT]])).then_inc(s_biasd, 16)
            pool.wait_ge(s_biasd, 48)
            pool.dma_start(AUX[:, :, :], bass.AP(ext_copies.tensor, P - 1, [[HEADS * NEXT - 1, P], [NEXT, HEADS], [1, T]])).then_inc(s_biasd, 16)
            pool.wait_ge(s_biasd, 64)
            pool.memset(AUX[0:CHUNK, :, T - CHUNK:T], NEG).then_inc(s_bias, 1)
            moe_gpsimd(pool, st)
            layer_gpsimd(pool)

        def pe_stats(pe, name, src, n=T, acc=bank[7]):
            i, before, chunks = chunks_before[name]
            if i:
                pe.wait_ge(rstd_done, i)
            for c in range(chunks):
                pe.wait_ge(sq_done, before + c + 1)
                mm = pe.matmul(acc[:, 0:n], ones, src(c), start=(c == 0), stop=(c == chunks - 1))
            mm.then_inc(stat_done, 1)

        def pe_attention(pe, cfg):
            s, units = cfg["sems"], cfg["units"]
            before, outs = cfg["base"]
            for step in range(len(units) + 3):
                u = step
                if u < len(units):
                    x = units[u]
                    if u >= 3:
                        pe.wait_ge(s["shifted"], before + u - 2)
                    for i, (q, k) in enumerate(x["scores"]):
                        mm = pe.matmul(bank[u % 3][:, 0:x["keys"]], q, k, start=(i == 0), stop=(i == len(x["scores"]) - 1))
                    mm.then_inc(s["scored"], 1)
                u = step - 2
                if 0 <= u < len(units):
                    x = units[u]
                    pe.wait_ge(s["normed"], before + u + 1)
                    if u >= 2:
                        pe.wait_ge(s["laid"], before + u - 1)
                    for kt in range(x["keys"] // P):
                        mm = pe.transpose(bank[3 + u % 2][:, kt * P:(kt + 1) * P], SS[:, u % 3, kt * P:(kt + 1) * P], ident)
                    mm.then_inc(s["turned"], 1)
                u = step - 3
                if 0 <= u < len(units):
                    x = units[u]
                    t = slice(x["t"] * P, (x["t"] + 1) * P)
                    pe.wait_ge(s["laid"], before + u + 1)
                    need = outs_before(cfg, u)
                    need -= len(x["values"]) == 1
                    if x["t"] == 0 and need > 0:
                        pe.wait_ge(s["att_out"], outs + need)
                    for b, r, v in x["values"]:
                        last = x["keys"] // P - 1
                        for kt in range(last + 1):
                            mm = pe.matmul(bank[b][r, t], v(kt), PT[:, x["pt"], kt, t], start=(kt == 0), stop=(kt == last))
                    mm.then_inc(s["summed"], 1)

        def dve_attention(dve, st, cfg):
            s, units = cfg["sems"], cfg["units"]
            before, outs = cfg["base"]
            for step in range(len(units) + 1):
                u = step
                if u < len(units):
                    x = units[u]
                    n = x["keys"]
                    dve.wait_ge(s["scored"], before + u + 1)
                    if u >= 3:
                        dve.wait_ge(s["turned"], before + u - 2)
                    if x["bias"]:
                        aux, h = x["bias"]
                        st.tell(dve.tensor_tensor(SS[:, u % 3, 0:n], bank[u % 3][:, 0:n], aux[:, h, T - n:T], ALU.add), s["shifted"])
                        st.wait()
                        st.tell(dve.tensor_reduce(stats[:, 0, u:u + 1], SS[:, u % 3, 0:n], AX.X, ALU.max, negate=True), s["shifted_max"])
                    else:
                        st.tell(dve.tensor_scalar(SS[:, u % 3, 0:n], bank[u % 3][:, 0:n], -x.get("scale", cfg["scale"]), None, ALU.mult, ALU.min,
                                                  accum_out=stats[:, 0, u:u + 1]), s["shifted"])
                u = step - 1
                if 0 <= u:
                    n = units[u]["keys"]
                    dve.wait_ge(s["expd"], before + u + 1)
                    st.do(dve.reciprocal(stats[:, 2, u:u + 1], stats[:, 1, u:u + 1]))
                    st.wait()
                    st.tell(dve.tensor_scalar(SS[:, u % 3, 0:n], SS[:, u % 3, 0:n], stats[:, 2, u:u + 1], None, ALU.mult), s["normed"])

        def act_attention(act, st, cfg, extra=lambda u: None):
            s, units = cfg["sems"], cfg["units"]
            before, outs = cfg["base"]
            for step in range(len(units) + 3):
                u = step
                if u < len(units):
                    x = units[u]
                    n = x["keys"]
                    act.wait_ge(s["shifted_max"] if x["bias"] else s["shifted"], before + u + 1)
                    st.tell(act.activation(SS[:, u % 3, 0:n], SS[:, u % 3, 0:n], ACT.Exp, bias=stats[:, 0, u:u + 1],
                                           scale=1.0 if x["bias"] else -1.0, accum_out=stats[:, 1, u:u + 1]), s["expd"])
                u = step - 2
                if 0 <= u < len(units):
                    x = units[u]
                    n = x["keys"]
                    act.wait_ge(s["turned"], before + u + 1)
                    if u >= 2 * TT:
                        act.wait_ge(s["summed"], before + u - 2 * TT + 1)
                    st.tell(act.activation(PT[:, x["pt"], 0:n // P, x["t"] * P:(x["t"] + 1) * P],
                                           bank[3 + u % 2][:, 0:n].rearrange("p (k t) -> p k t", t=P), ACT.Copy), s["laid"])
                u = step - 3
                if 0 <= u and units[u]["out"]:
                    act.wait_ge(s["summed"], before + u + 1)
                    for c, b in units[u]["out"]:
                        st.tell(act.activation(cfg["dest"](c), bank[b][:, :], ACT.Copy), s["att_out"])


        @block.tensor
        def _(pe):
            uses = [0]

            def slot():
                n = uses[0]
                uses[0] += 1
                pe.wait_ge(w_landed[n % RING], 16 * (n // RING + 1))
                return ring[n % RING]


            tiles = [0]

            def tile(mms, done=tile_done, free=tile_free, count=tiles, banks=4):
                n = count[0]
                if n >= banks:
                    pe.wait_ge(free, n - banks + 1)
                mms(bank[n % banks]).then_inc(done, 1)
                count[0] += 1

            def project(src, n=T, hwait=None, chunks=4, after=None, **kw):
                w = slot()
                for m in range(chunks):
                    def mms(b):
                        for k in range(DC):
                            if hwait is not None and m == 0:
                                pe.wait_ge(h_done, hwait + k + 1)
                            mm = pe.matmul(b[:, 0:n], w[:, k, m * P:(m + 1) * P], src(k), start=(k == 0), stop=(k == DC - 1))
                        return mm
                    tile(mms, **kw)
                    if after:
                        after(m)

            def tokens(src, tt):
                w = slot()
                for t in range(tt):
                    def mms(b):
                        for k in range(DC):
                            mm = pe.matmul(b[:, :], src(k)[:, t * P:(t + 1) * P], w[:, k, :], start=(k == 0), stop=(k == DC - 1))
                        return mm
                    tile(mms)

            pe.wait_ge(s_const, 32)
            pe_stats(pe, "mem", lambda c: S[:, 12 + c // 2, (c % 2) * MEM:(c % 2) * MEM + MEM], MEM)
            pe_stats(pe, "ln1", lambda c: H[:, c, :])
            mt = lambda k: MT[:, k, :]
            h = lambda k: H[:, k, :]
            project(mt, MEM, hwait=0)
            project(mt, MEM)
            tokens(mt, 2)
            tokens(mt, 2)
            project(h, hwait=chunks_before["ln1"][1])
            project(h)
            pe.wait_ge(s_gates, 64)

            def gates(m):
                pe.wait_ge(xc_done, m + 1)
                if m:
                    pe.wait_ge(gate_free, 2 * m)
                for g in range(2):
                    pe.matmul(bank[5 + g][:, :], gatew[:, g, m, :], XC[:, m, :], start=True, stop=True).then_inc(gate_done, 1)

            project(h, after=gates)
            project(h)
            tokens(h, TT)
            pe.wait_ge(tile_free, tiles[0])
            pe_attention(pe, att_cfg[0])
            pe_stats(pe, "gn_rnn", lambda c: S[:, c, :])
            pe_stats(pe, "gn_att", lambda c: S[:, 4 + c, :])
            rt = [0]
            res = dict(done=res_done, free=res_free, count=rt)
            project(h, hwait=chunks_before["gn_rnn"][1], **res)
            project(h, **res)
            pe_stats(pe, "ln2", h)
            pe.wait_ge(res_free, rt[0])
            project(h, hwait=chunks_before["ln2"][1])
            project(h)
            pe.wait_ge(tile_free, tiles[0])
            pe_attention(pe, att_cfg[1])
            pe.wait_ge(att["att_out"], HEADS // 2 + 8)
            project(h, **res)
            project(h, **res)
            pe_stats(pe, "ln3", h)
            moe_tensor(pe)

        def dve_norm(dve, st, name, src, dst, w=None, n=T):
            i, before, chunks = chunks_before[name]
            dve.wait_ge(rstd_done, i + 1)
            for c in range(chunks):
                st.tell(dve.scalar_tensor_tensor(dst(c), src(c), col(w or name, c), rstd[:, 0:n], ALU.mult, ALU.mult), h_done)

        def dve_residual(dve, st, first, scale=None):
            for m in range(DC):
                dve.wait_ge(res_done, first + m + 1)
                st.tell(dve.tensor_tensor(X[:, m, :], X[:, m, :], bank[(first + m) % 4][:, :], ALU.add), res_free)

        @block.vector
        def _(dve):
            st = Steps(dve, dve_own)
            st.do(dve.memset(eps[:, 0:1], EPS))
            st.do(dve.memset(eps[:, 1:2], LN_EPS))
            st.do(dve.memset(eps[:, 2:3], 1e-30))
            st.do(dve.memset(eps[:, 3:4], 1.0))
            dve.wait_ge(s_mem, 16)
            dve_norm(dve, st, "mem", lambda c: MT[:, c, :], lambda c: MT[:, c, :], n=MEM)
            dve.wait_ge(s_x, 16)
            dve_norm(dve, st, "ln1", lambda c: X[:, c, :], lambda c: H[:, c, :])
            lam = cols[:, C1["lam"]:C1["lam"] + HC]
            sm = lambda i: small[:, 4 * i:4 * i + 4]
            dve.wait_ge(rg_done, 1)
            dve.wait_ge(rg_done, 2)
            st.do(dve.tensor_scalar(sm(3), sm(1), 1.0, None, ALU.add)); st.wait()
            st.do(dve.reciprocal(sm(4), sm(3)))
            st.do(dve.tensor_scalar(sm(5), sm(3), -1.0, None, ALU.add)); st.wait()
            st.do(dve.tensor_tensor(sm(5), sm(1), sm(5), ALU.subtract)); st.wait()
            st.do(dve.tensor_tensor(sm(5), sm(5), sm(4), ALU.mult)); st.wait()
            st.do(dve.tensor_tensor(sm(5), sm(5), sm(2), ALU.add)); st.wait()
            st.do(dve.tensor_scalar(sm(6), lam, -1.0, 0.0, ALU.mult, ALU.max)); st.wait()
            st.do(dve.tensor_tensor(sm(5), sm(5), sm(6), ALU.add)); st.wait()
            st.do(dve.tensor_scalar(sm(7), sm(5), 8.0, None, ALU.mult))
            st.do(dve.tensor_scalar(sm(8), sm(5), -8.0, None, ALU.mult))
            for c in range(HC):
                dve.wait_ge(tile_free, 12 + c + 1)
                tap = lambda i: col("conv_w", i * HC + c)
                st.do(dve.tensor_scalar(XC[:, c, :], XR[:, c, :], tap(3), col("conv_b", c), ALU.mult, ALU.add))
                for i in (2, 1, 0):
                    o = 3 - i
                    st.wait()
                    ins = dve.scalar_tensor_tensor(XC[:, c, o:T], XR[:, c, 0:T - o], tap(i), XC[:, c, o:T], ALU.mult, ALU.add)
                    st.tell(ins, xc_done) if i == 0 else st.do(ins)
            for c in range(HC):
                dve.wait_ge(rg_done, 2 + 2 * c + 2)
                st.do(dve.tensor_tensor(IG[:, c, :], IG[:, c, :], XC[:, c, :], ALU.mult))
            for c in range(HC):
                dve.wait_ge(ia_done, 2 * c + 2)
                st.do(dve.tensor_tensor(XR[:, c, :], AD[:, c, :], AD[:, c, :], ALU.mult)); st.wait()
                st.tell(dve.scalar_tensor_tensor(RG[:, c, :], XR[:, c, :], 1.0, RG[:, c, :], ALU.add, ALU.mult), y_rnn)
            for c in range(HC):
                dve.wait_ge(nh_done, c + 1)
                st.do(dve.tensor_tensor(IG[:, c, :], IG[:, c, :], RG[:, c, :], ALU.mult)); st.wait()
                st.do(dve.tensor_tensor_scan(XC[:, c, :], AD[:, c, :], IG[:, c, :], 0.0, ALU.mult, ALU.add)); st.wait()
                st.tell(dve.tensor_tensor(G[:, c, :], G[:, c, :], XC[:, c, :], ALU.mult), y_rnn)
            dve.wait_ge(s_bias, 1)
            dve_attention(dve, st, att_cfg[0])
            dve_norm(dve, st, "gn_rnn", lambda c: G[:, c, :], lambda c: H[:, c, :])
            dve_norm(dve, st, "gn_att", lambda c: S[:, 12 + c, :], lambda c: H[:, 4 + c, :])
            dve_residual(dve, st, 0)
            dve_norm(dve, st, "ln2", lambda c: X[:, c, :], lambda c: H[:, c, :])
            dve_attention(dve, st, att_cfg[1])
            dve_residual(dve, st, 8)
            dve_norm(dve, st, "ln3", lambda c: X[:, c, :], lambda c: H[:, c, :])
            moe_vector(dve, st)

        def act_squares(act, st, name, src, dst):
            for c in range(chunks_before[name][2]):
                st.tell(act.activation(dst(c), src(c), ACT.Square), sq_done)

        def act_rstd(act, st, name, n=T, acc=bank[7], size=None, e=0):
            i, before, chunks = chunks_before[name]
            act.wait_ge(stat_done, i + 1)
            if before:
                act.wait_ge(h_done, before)
            st.do(act.activation(rstd[:, 0:n], acc[:, 0:n], ACT.Ln, scale=1.0 / (chunks * P), bias=eps[:, e:e + 1])); st.wait()
            st.tell(act.activation(rstd[:, 0:n], rstd[:, 0:n], ACT.Exp, scale=-0.5), rstd_done)

        @block.scalar
        def _(act):
            st = Steps(act, act_own)
            act.wait_ge(s_mem, 16)
            act_squares(act, st, "mem", lambda c: MT[:, c, :], lambda c: S[:, 12 + c // 2, (c % 2) * MEM:(c % 2) * MEM + MEM])
            act.wait_ge(s_x, 16)
            act_squares(act, st, "ln1", lambda c: X[:, c, :], lambda c: H[:, c, :])
            act.wait_ge(dve_own, 4)
            act_rstd(act, st, "mem", MEM)
            act_rstd(act, st, "ln1")
            act.wait_ge(s_const, 32)
            lam = cols[:, C1["lam"]:C1["lam"] + HC]
            sm = lambda i: small[:, 4 * i:4 * i + 4]
            st.do(act.activation(sm(0), lam, ACT.Abs)); st.wait()
            st.tell(act.activation(sm(1), sm(0), ACT.Exp, scale=-1.0), rg_done); st.wait()
            st.tell(act.activation(sm(2), sm(1), ACT.Ln, bias=eps[:, 3:4]), rg_done)

            n = [0]

            def evac(dst, src, func=ACT.Copy, scale=1.0):
                act.wait_ge(tile_done, n[0] + 1)
                st.tell(act.activation(dst, src(bank[n[0] % 4]), func, scale=scale), tile_free)
                n[0] += 1

            for m in range(DC):
                evac(KM[:, m, :], lambda b: b[:, 0:MEM])
            for j in range(2):
                for t in range(2):
                    evac(VM[:, t, j * 512:(j + 1) * 512], lambda b: b[:, :])
            full = lambda b: b[:, :]
            for c in range(HC):
                evac(XR[:, c, :], full)
            for c in range(HC):
                evac(G[:, c, :], full, ACT.Gelu_apprx_tanh)
            for c in range(HC):
                evac(Q[:, c, :], full, scale=HD ** -0.5)
                for g, (dst, b) in enumerate(((RG, "ba"), (IG, "bx"))):
                    act.wait_ge(gate_done, 2 * c + g + 1)
                    st.tell(act.activation(dst[:, c, :], bank[5 + g][:, :], ACT.Sigmoid, bias=col(b, c)), gate_free)
                st.told.setdefault(rg_done.name, 0)
                st.wait()
                act.sem_inc(rg_done, 2)
            act.wait_ge(dve_own, 4 + 10)
            for c in range(HC):
                evac(K[:, c, :], full)
                st.tell(act.activation(AD[:, c, :], RG[:, c, :], ACT.Exp, scale=small[:, 32 + c:33 + c]), ia_done)
                st.tell(act.activation(RG[:, c, :], RG[:, c, :], ACT.Tanh, scale=small[:, 28 + c:29 + c]), ia_done)
            for t in range(TT):
                evac(V[:, t, :], full)
                act.wait_ge(y_rnn, t + 1)
                st.tell(act.activation(RG[:, t, :], RG[:, t, :], ACT.Sqrt, bias=eps[:, 2:3]), nh_done)
            act.wait_ge(y_rnn, 8)
            act_attention(act, st, att_cfg[0])
            for c in range(HC):
                st.tell(act.activation(S[:, c, :], G[:, c, :], ACT.Square), sq_done)
            act_rstd(act, st, "gn_rnn")
            act.wait_ge(att["summed"], 32)
            act.wait_ge(att["att_out"], 4)
            for c in range(HC):
                st.tell(act.activation(S[:, 4 + c, :], S[:, 12 + c, :], ACT.Square), sq_done)
            act_rstd(act, st, "gn_att")
            act.wait_ge(res_done, 8)
            for c in range(DC):
                act.wait_ge(res_free, c + 1)
                st.tell(act.activation(H[:, c, :], X[:, c, :], ACT.Square), sq_done)
            act_rstd(act, st, "ln2")
            for c in range(DC):
                evac(QX[:, c, :], full)
            act_attention(act, st, att_cfg[1])
            act.wait_ge(res_done, 16)
            for c in range(DC):
                act.wait_ge(res_free, 8 + c + 1)
                st.tell(act.activation(H[:, c, :], X[:, c, :], ACT.Square), sq_done)
            act_rstd(act, st, "ln3")
            moe_scalar(act, st)
def layouts(i):
    f = np.float32

    def column(v):
        v = np.asarray(v, f).reshape(-1)
        if v.size % P:
            v = np.concatenate([v, np.zeros(P - v.size % P, f)])
        return v.reshape(-1, P).T

    r = {}
    r["xT"] = np.asarray(i["x"])[0].T
    r["memT"] = np.asarray(i["mem"])[0].T
    parts = [i["ln1_w"], i["conv_w"], i["conv_b"], i["rnn_ba"], i["rnn_bx"], i["rnn_lambda"], i["gn_rnn_w"],
             i["gn_att_w"], i["ln2_w"], i["mem_norm_w"], i["ln3_w"], i["final_norm_w"], i["ln_in_g_2"], i["ln_in_b_2"]]
    r["cols"] = np.concatenate([column(v) for v in parts], axis=1)
    for w in ("w_in", "w_out", "xq_w", "xk_w", "xv_w", "xo_w", "rnn_wa", "rnn_wx"):
        r[w] = np.asarray(i[w])[0]
    r["router_w"] = np.concatenate([np.asarray(i["router_group_w"])[0], np.asarray(i["router_expert_w"])[0].transpose(1, 0, 2).reshape(D, EXPERTS)], axis=1)
    r["router_b"] = np.concatenate([np.asarray(i["router_group_b"])[0], np.asarray(i["router_expert_b"])[0].reshape(-1)])
    for w in ("expert_gate_w", "expert_up_w", "expert_down_w"):
        r[w] = np.asarray(i[w])[0]
    r["rel_rev"] = np.asarray(i["rel_bias"])[0][:, ::-1]
    k = np.arange(P)
    pair = (k[:, None] // 64 == k[None, :] // 64)

    def perm(rows):
        m = np.zeros((P, P), f)
        for d in rows:
            if d % 32 < 16:
                m[d + 16, d] = -1.0
            else:
                m[d - 16, d] = 1.0
        return m

    half = [d for d in range(P)]
    def perm_mla():
        m = np.zeros((P, P), f)
        for d in range(64, HM):
            if d % 16 < 8:
                m[d + 8, d] = -1.0
            else:
                m[d - 8, d] = 1.0
        return m
    r["konst"] = np.concatenate([np.eye(P), np.ones((P, P)), k[:, None] < k[None, :], pair, perm(half), perm_mla(),
                                 np.tile(np.arange(EPG, 0, -1), (P, 1)), np.tile(np.arange(TABLE), (P, 1))],
                                axis=1).astype(f)
    l2 = {n[:-2]: np.asarray(v) for n, v in i.items() if n.endswith("_2")}
    names = ["conv_a_w", "conv_a_b", "ln_a_g", "ln_a_b", "qk_norm_q", "qk_norm_k", "sgu_ln_g", "sgu_ln_b", "mla_q_norm",
             "mla_kv_norm", "ln_mix_g", "ln_mix_b", "ffn_conv_w", "ffn_conv_b", "ln_ffn_g", "ln_ffn_b"]

    def vectors(l):
        return [np.tile(l2[n][l], 2) if n.startswith("qk_norm") else l2[n][l] for n in names]
    r["cols2"] = np.stack([np.concatenate([column(v) for v in vectors(l)], axis=1) for l in range(L2)])
    r["w_in_2"], r["w_out_2"] = l2["w_in"], l2["w_out"]
    r["ffn_w_up"], r["ffn_w_down"] = l2["ffn_w_up"], l2["ffn_w_down"]
    r["w_uq"], r["w_ukv"] = l2["mla_w_uq"], l2["mla_w_ukv"]
    r["sgu_wT"] = l2["sgu_w"].transpose(0, 3, 1, 2)
    r["sgu_b"] = l2["sgu_b"]
    t = np.arange(T)
    row, colm = (t // 64).astype(f), (t % 64).astype(f)

    def angles(dims, half):
        freq = (f(10000.0) ** (-np.arange(half, dtype=f) / f(half))).astype(f)
        return np.stack([(row if (d % (4 * half)) < 2 * half else colm) * freq[d % half] for d in range(dims)]).astype(f)
    a64 = angles(P, 16)
    a96 = np.zeros((P, T), f)
    a96[64:HM] = angles(ROPE, 8)
    r["rotary"] = np.stack([np.cos(a64), np.sin(a64), np.cos(a96), np.sin(a96)], axis=1).astype(f)
    return r


def kernel(**inputs):
    import numpy as _np
    import concourse.bacc as _bacc
    from concourse import mybir as _mybir
    from concourse.bass_utils import run_bass_kernel_spmd as _run

    nc = _bacc.Bacc("TRN2", target_bir_lowering=False, num_devices=1)
    arrays, A = {}, {}
    for name, a in layouts(inputs).items():
        a = _np.ascontiguousarray(a)
        arrays[f"in_{name}"] = a
        A[name] = nc.dram_tensor(f"in_{name}", a.shape, _mybir.dt.from_np(a.dtype), kind="ExternalInput").ap()
    out = nc.dram_tensor("out_0", (D, T), F32, kind="ExternalOutput").ap()
    build(nc, A, out)
    r = _run(nc, [arrays], core_ids=[0])
    return r.results[0]["out_0"].T.reshape(1, T, D)
```

```python
from contextlib import ExitStack

import numpy as np
import concourse.bass as bass
from concourse import mybir

F32 = mybir.dt.float32
F32R = mybir.dt.float32r
U32 = mybir.dt.uint32
ALU = mybir.AluOpType
ACT = mybir.ActivationFunctionType
AX = mybir.AxisListType

P = 128
T = 512
TT = T // P
D = 1024
DC = D // P
MEM = 256
HALF = 512
HC = HALF // P
CONV = 4
HEADS, HD = 8, 64
CLIP = 128
CHUNK = 64
XHEADS = 4
GROUPS, EPG = 4, 8
EXPERTS = GROUPS * EPG
FE = 512
SLOTS = 2 * T
MAXB = EXPERTS + (SLOTS - EXPERTS) // P
MINB = SLOTS // P
TABLE = MAXB + 1
NEG = -1e30
EPS = 1e-6
LN_EPS = 1e-5
L2 = 2
GW = 256
GC = GW // P
CONVA = 31
DFF = 2816
FC = DFF // P
QL, KVL, ROPE = 192, 128, 32
HM = 96
ALPHA = float((2 * L2) ** 0.25)
RING = 3


def layout(fields):
    at, n = {}, 0
    for name, width in fields:
        at[name] = n
        n += width
    return at, n


COLS1 = [("ln1", DC), ("conv_w", CONV * HC), ("conv_b", HC), ("ba", HC), ("bx", HC), ("lam", HC),
         ("gn_rnn", HC), ("gn_att", HC), ("ln2", DC), ("mem", DC), ("ln3", DC), ("final", DC),
         ("lnin_g", DC), ("lnin_b", DC)]
COLS2 = [("ca_w", CONVA * GC), ("ca_b", GC), ("la_g", GC), ("la_b", GC), ("qn", 1), ("kn", 1),
         ("sg_g", GC), ("sg_b", GC), ("mq", 2), ("mkv", 1), ("mix_g", DC), ("mix_b", DC),
         ("fc_w", 3 * 2 * FC), ("fc_b", 2 * FC), ("ffn_g", DC), ("ffn_b", DC)]
C1, N1 = layout(COLS1)
C2, N2 = layout(COLS2)
CONSTS = [("ident", P), ("ones", P), ("lower", P), ("pair", P), ("perm", P), ("perm96", P), ("desc", EPG), ("block", TABLE)]
CK, NK = layout(CONSTS)
NORMS = [("mem", DC), ("ln1", DC), ("gn_rnn", HC), ("gn_att", HC), ("ln2", DC), ("ln3", DC), ("final", DC)]


class Steps:

    def __init__(self, eng, own):
        self.eng, self.own, self.n, self.last, self.told = eng, own, 0, None, {}

    def do(self, ins):
        self.n += 1
        ins.then_inc(self.own, 1)
        self.last = (self.own, self.n)
        return self.last

    def tell(self, ins, sem, base=0):
        self.told[sem.name] = self.told.get(sem.name, 0) + 1
        ins.then_inc(sem, 1)
        self.last = (sem, base + self.told[sem.name])
        return self.last

    def wait(self, step=None):
        sem, n = step or self.last
        self.eng.wait_ge(sem, n)


def build(nc, A, out):
    with ExitStack() as ctx:
        def sb(name, shape, dt=F32):
            return ctx.enter_context(nc.sbuf_tensor(name, shape, dt))

        def sem(name):
            return ctx.enter_context(nc.semaphore(name))

        bank = [ctx.enter_context(nc.psum_tensor(f"bank{i}", [P, T], F32)) for i in range(8)]

        with ExitStack() as places:
            def place(name, shape):
                return places.enter_context(nc.sbuf_tensor(name, shape, F32R))

            place("raw_place", [P, 8, 512])
            WHL = [place(f"split_weights{i}", [P, 2, 8, 256]) for i in range(2)]
            SP = place("split_products", [P, FC, T])
            XH = place("split_x_high", [P, DC, T])
            XL = place("split_x_low", [P, DC, T])
            QP = place("split_products_low", [P, 16, T])
        ring = [sb(f"ring{i}", [P, 8, 512]) for i in range(RING)]
        S = sb("S", [P, FC, T])
        H = sb("H", [P, DC, T])
        MKV = sb("MKV", [P, 8, T])
        QKVG = sb("QKVG", [P, 16, T])
        X = sb("X", [P, DC, T])
        AUX = sb("AUX", [P, 8, T])
        cols = sb("cols", [P, N1])
        cols2 = sb("cols2", [P, N2])
        konst = sb("konst", [P, NK])
        eps = sb("eps", [P, 4])
        rstd = sb("rstd", [P, T])
        stats = sb("stats", [P, 4, 32])
        small = sb("small", [P, 64])

        def const(name, n=P):
            return konst[:, CK[name]:CK[name] + n]

        def col(name, i=0, p=P):
            return cols[0:p, C1[name] + i:C1[name] + i + 1]

        ident = const("ident")
        ones = const("ones")

        Q, K, G = QKVG[:, 0:4, :], QKVG[:, 4:8, :], QKVG[:, 12:16, :]
        V = QKVG[:, 8:12, :]
        KM = MKV[:, 0:4, :].rearrange("p a (b m) -> p (a b) m", m=MEM)
        VM = MKV[:, 4:8, :].rearrange("p (a b) n -> p a (b n)", a=2)
        XR, XC, RG, IG, AD = (S[:, 4 * i:4 * i + 4, :] for i in range(5))
        MT = S[:, 16:20, :].rearrange("p a (b m) -> p (a b) m", m=MEM)

        s_const = sem("const_landed")
        s_x = sem("x_landed")
        s_mem = sem("mem_landed")
        s_gates = sem("gate_weights_landed")
        s_biasd = sem("bias_dma")
        s_bias = sem("bias_ready")
        w_landed = [sem(f"weights_landed{i}") for i in range(RING)]
        act_own, dve_own, pool_own = sem("act_steps"), sem("dve_steps"), sem("pool_steps")
        sq_done, stat_done, rstd_done, h_done = sem("squares"), sem("stat"), sem("rstd_done"), sem("h_chunks")
        tile_done, tile_free = sem("tile_done"), sem("tile_free")
        xc_done, gate_done, gate_free = sem("conv_done"), sem("gates_done"), sem("gates_free")
        y_rnn = sem("y_rnn")
        rg_done, ia_done, nh_done = sem("r_i_done"), sem("decay_done"), sem("root_done")
        att = {k: sem(k) for k in ("scored", "shifted", "shifted_max", "expd", "normed", "turned", "laid", "summed", "att_out")}
        res_done, res_free = sem("res_done"), sem("res_free")

        chunks_before = {}
        n = 0
        for i, (name, c) in enumerate(NORMS):
            chunks_before[name] = (i, n, c)
            n += c

        def wblock(w, j, n=512):
            return w.rearrange("(k p) n -> p k n", p=P)[:, :, j * n:(j + 1) * n]

        first_uses = [(wblock(A["xk_w"], j), tile_done, 4 * j + 4) for j in range(2)]
        first_uses += [(wblock(A["xv_w"], j), tile_done, 8 + 2 * j + 2) for j in range(2)]
        first_uses += [(wblock(A["w_in"], j), tile_done, 12 + 4 * j + 4) for j in range(5)]
        first_uses += [(wblock(A["w_out"], j), res_done, 4 * j + 4) for j in range(2)]
        first_uses += [(wblock(A["xq_w"], j), tile_done, 32 + 4 * j + 4) for j in range(2)]
        first_uses += [(wblock(A["xo_w"], j), res_done, 8 + 4 * j + 4) for j in range(2)]
        assert len(first_uses) % RING == 0

        gatew = sb("gatew", [P, 2, HC, P])
        NEXT = P + T - 1
        ext = sb("ext", [HEADS, NEXT])
        ext_dram = nc.dram_tensor("ext_scratch", (HEADS, NEXT), F32).ap()
        ext_copies = nc.dram_tensor("ext_copies", (P, HEADS, NEXT), F32).ap()

        att_cfg = []
        units = []
        for h in range(HEADS):
            r = slice(64 * (h % 2), 64 * (h % 2) + 64)
            for t in range(TT):
                keys = (t + 1) * P
                units.append(dict(
                    scores=[(Q[r, h // 2, t * P:(t + 1) * P], K[r, h // 2, 0:keys])], keys=keys, t=t,
                    bias=(AUX, h), pt=h % 2,
                    values=[(5 + (h // 2) % 2, r, lambda kt, h=h: V[:, kt, h * 64:(h + 1) * 64])],
                    out=[(h // 2, 5 + (h // 2) % 2)] if h % 2 and t == TT - 1 else []))
        att_cfg.append(dict(units=units, sems=att, base=(0, 0), dest=lambda c: S[:, 12 + c, :], scale=1.0))
        units = []
        QX = QKVG[:, 0:8, :]
        for h in range(XHEADS):
            for t in range(TT):
                units.append(dict(
                    scores=[(QX[:, 2 * h + c, t * P:(t + 1) * P], KM[:, 2 * h + c, :]) for c in range(2)],
                    keys=MEM, t=t, bias=None, pt=h % 2,
                    values=[(5 + c, slice(0, P), lambda kt, f=(2 * h + c) * P: VM[:, kt, f:f + P]) for c in range(2)],
                    out=[(2 * h, 5), (2 * h + 1, 6)] if t == TT - 1 else []))
        att_cfg.append(dict(units=units, sems=att, base=(HEADS * TT, HEADS // 2), dest=lambda c: H[:, c, :], scale=float(D // XHEADS) ** -0.5))

        SS = S[:, 0:3, :]
        PT = S[:, 4:12, :].rearrange("p (a k) t -> p a k t", a=2)

        def outs_before(cfg, u):
            return sum(len(x["out"]) for x in cfg["units"][:u])


        NR = GROUPS + EXPERTS
        routw = sb("routw", [P, DC, NR])
        routb = sb("routb", [P, NR])
        route = sb("route", [P, 6, TT])
        slots = sb("slots", [P, 2, TT], U32)
        ids = sb("ids", [P, TT], U32)
        zero = sb("zero", [P, TABLE], U32)
        nothing = sb("nothing", [P, 512])
        assert (TABLE - MINB) % 8 == 0
        table = sb("table", [1, 64])
        table_u = sb("table_u", [1, 64], U32)
        idx = sb("idx", [P, 1], U32)
        rows_dram = nc.dram_tensor("rows_scratch", (T, D), F32).ap()
        slot_dram = nc.dram_tensor("slot_tokens", (TABLE * P, 1), U32).ap()
        y_dram = nc.dram_tensor("expert_rows", (TABLE * P, D), F32).ap()
        HT = S[:, 0:8, :].rearrange("p (t a) n -> p t (a n)", t=TT)
        LG = S[:, 12, 0:TT * NR].rearrange("p (t n) -> p t n", t=TT)

        def rt(i, *dims):
            n = TT * int(np.prod(dims))
            a = S[:, 13 + i // 4, (i % 4) * P:(i % 4) * P + n]
            if len(dims) == 2:
                return a.rearrange("p (t g e) -> p t g e", t=TT, e=dims[1])
            return a.rearrange("p (t g) -> p t g", t=TT)

        XB = QKVG[:, 0:2, :].rearrange("p a n -> p (a n)")
        XBT = [QP[:, i:i + 2, :].rearrange("p a (c s) -> p (a c) s", s=P) for i in (2, 10)]
        SG, PR = QKVG[:, 4, :], QKVG[:, 5, :]
        AT = [QP[:, i, :].rearrange("p (c s) -> p c s", s=P) for i in (6, 9)]
        EW = [XH, XL, SP]

        def e_raw(u):
            return ring[u // 2][:, 4 * (u % 2):4 * (u % 2) + 4, :]

        def e_high(u):
            return EW[u % 3][:, 0:4, :]

        def e_low(u):
            return EW[u % 3][:, 4:8, :]

        def as_f32(a):
            return a.bitcast(F32)

        YB = QKVG[:, 7:9, :]

        s_rout = sem("router_landed")
        routed = sem("router_products")
        rows_turned, rows_laid, rows_stored = sem("rows_turned"), sem("rows_laid"), sem("rows_stored")
        r_exp, r_d, mask_done, slots_done = (sem(f"route_{n}") for n in ("exp", "dve", "mask", "slots"))
        scattered = sem("slot_tokens_stored")
        spare = sem("spare_rows_zeroed")
        counted_waits = sem("counted_waits")
        idx_landed, xb_landed = sem("idx_landed"), sem("rows_gathered")
        g_landed, u_landed, d_landed = sem("gate_w_landed"), sem("up_w_landed"), sem("down_w_landed")
        ew_high, ew_low, ew_used = sem("expert_w_high"), sem("expert_w_low"), sem("expert_w_used")
        x_turned, x_high, x_low = sem("x_turned"), sem("expert_x_high"), sem("expert_x_low")
        sg_done, pr_done = sem("silu_done"), sem("product_done")
        a_turned, a_high, a_low, y_a, y_v, y_stored = (sem(n) for n in ("a_turned", "a_high", "a_low", "y_laid_act", "y_laid_dve", "y_stored"))
        y_got, y_sum, y_back, x3 = [sem(f"y_gathered{i}") for i in range(2)], sem("y_weighted"), sem("y_turned_back"), sem("x3_tiles")

        def expert_w(w, e):
            return w[bass.ds(e, 1)].rearrange("o (k p) n -> p (o k) n", p=P)

        def wait_counted(eng, sem_, value):
            eng.wait_ge(sem_, value)
            eng.sem_inc(counted_waits, 1)

        def moe_sync(sp):
            sp.wait_ge(*first_uses[-3][1:])
            sp.wait_ge(*first_uses[-2][1:])
            sp.wait_ge(*first_uses[-1][1:])
            sp.wait_ge(slots_done, 1)
            nb = sp.value_load(table_u[0:1, 63:64], min_val=MINB, max_val=MAXB)

            def gate_up(b, e, first=False):
                for i, (w, landed) in enumerate((("expert_gate_w", g_landed), ("expert_up_w", u_landed))):
                    if not first:
                        wait_counted(sp, ew_low, b * 6 - 4 + 2 * i)
                    sp.dma_start(ring[i][:, :, :], expert_w(A[w], e)).then_inc(landed, 16)

            def down(b, e, first=False):
                if not first:
                    wait_counted(sp, ew_low, b * 6 + 6)
                sp.dma_start(ring[2][:, :, :].rearrange("p (k a) n -> p k (a n)", a=2),
                             expert_w(A["expert_down_w"], e)).then_inc(d_landed, 16)

            e = sp.value_load(table_u[0:1, 0:1], min_val=0, max_val=EXPERTS - 1)
            gate_up(0, e, first=True)
            down(0, e, first=True)
            e1 = sp.value_load(table_u[0:1, 1:2], min_val=0, max_val=EXPERTS - 1)
            gate_up(1, e1)
            with sp.Fori(2, nb) as b:
                e = sp.value_load(table_u[0:1, bass.ds(b, 1)], min_val=0, max_val=EXPERTS - 1)
                gate_up(b, e)
                e0 = sp.value_load(table_u[0:1, bass.ds(b - 1, 1)], min_val=0, max_val=EXPERTS - 1)
                down(b - 1, e0)
            final = sp.value_load(table_u[0:1, 62:63], min_val=MINB - 1, max_val=MAXB - 1)
            e = sp.value_load(table_u[0:1, bass.ds(final, 1)], min_val=0, max_val=EXPERTS - 1)
            down(final, e)

        def moe_gpsimd(pool, st):
            st.do(pool.iota(ids[:, :], [[P, TT]], base=0, channel_multiplier=1))
            st.do(pool.memset(zero[:, :], 0))
            st.wait()
            pool.dma_start(slot_dram.rearrange("(p n) o -> p (n o)", p=P), zero[:, :]).then_inc(scattered, 16)
            pool.dma_start(routw[:, :, :], A["router_w"].rearrange("(k p) n -> p k n", p=P)).then_inc(s_rout, 16)
            pool.dma_start(routb[:, :], bass.AP(A["router_b"].tensor, 0, [[0, P], [1, NR]])).then_inc(s_rout, 16)
            pool.wait_ge(scattered, 16)
            st.do(pool.memset(nothing[:, :], 0.0)); st.wait()
            pool.wait_ge(tile_done, 28)
            for b in range(MINB, TABLE, 8):
                pool.dma_start(y_dram[b * P:(b + 8) * P, :].rearrange("(p b) (a n) -> p (b a) n", p=P, n=512),
                               nothing[:, None, :].to_broadcast([P, 16, 512])).then_inc(spare, 16)
            pool.wait_ge(slots_done, 1)
            nb = pool.value_load(table_u[0:1, 63:64], min_val=MINB, max_val=MAXB)
            for w in range(2):
                for t in range(TT):
                    pool.indirect_dma_start(slot_dram, bass.IndirectOffsetOnAxis(slots[:, w, t:t + 1], 0),
                                            ids[:, t:t + 1], None).then_inc(scattered, 16)
            pool.wait_ge(scattered, 16 * (2 * TT + 1))
            pool.wait_ge(rows_stored, 16 * TT)

            def gather(b):
                pool.dma_start(idx[:, :], slot_dram[bass.ds(b * P, P), :]).then_inc(idx_landed, 16)
                wait_counted(pool, idx_landed, b * 16 + 16)
                wait_counted(pool, x_turned, b)
                pool.indirect_dma_start(XB, None, rows_dram, bass.IndirectOffsetOnAxis(idx[:, 0:1], 0)).then_inc(xb_landed, 16)
                wait_counted(pool, xb_landed, b * 16 + 16)

            with pool.Fori(0, nb) as b:
                gather(b)
            wait_counted(pool, y_stored, nb * 16)
            for t in range(TT):
                for w in range(2):
                    pool.indirect_dma_start(S[:, 4 * t + 2 * w:4 * t + 2 * w + 2, :].rearrange("p a n -> p (a n)"), None, y_dram,
                                            bass.IndirectOffsetOnAxis(slots[:, w, t:t + 1], 0)).then_inc(y_got[t % 2], 16)
                if t:
                    pool.wait_ge(y_got[(t - 1) % 2], 32 * ((t - 1) // 2 + 1))

        def moe_tensor(pe):
            h3 = lambda k: H[:, k, :]
            first = chunks_before["ln3"][1]
            pe.wait_ge(s_rout, 32)
            pe.wait_ge(tile_free, 40)
            pe.wait_ge(h_done, first + DC)
            for t in range(TT):
                for k in range(DC):
                    mm = pe.matmul(bank[5][:, t * NR:(t + 1) * NR], H[:, k, t * P:(t + 1) * P], routw[:, k, :], start=(k == 0), stop=(k == DC - 1))
            mm.then_inc(routed, 1)
            pe.wait_ge(res_free, 16)
            for t in range(TT):
                if t >= 2:
                    pe.wait_ge(rows_laid, 2 * (t - 1))
                for j in range(2):
                    for c in range(4):
                        mm = pe.transpose(bank[2 * (t % 2) + j][:, c * P:(c + 1) * P], H[:, 4 * j + c, t * P:(t + 1) * P], ident)
                mm.then_inc(rows_turned, 1)
            pe.wait_ge(mask_done, 1)
            M = rt(9, GROUPS, EPG).rearrange("p t g e -> p t (g e)")
            for t in range(TT):
                for o in range(t + 1):
                    pe.matmul(bank[6][:, t * EXPERTS:(t + 1) * EXPERTS], const("lower") if o == t else ones, M[:, o, :], start=(o == 0), stop=(o == t))
            for t in range(TT):
                mm = pe.matmul(bank[4][:, 0:EXPERTS], ones, M[:, t, :], start=(t == 0), stop=(t == TT - 1))
            mm.then_inc(routed, 1)
            pe.wait_ge(slots_done, 1)
            nb = pe.value_load(table_u[0:1, 63:64], min_val=MINB, max_val=MAXB)
            pe.wait_ge(rows_laid, 2 * TT)

            def turn_x(b):
                pe.wait_ge(xb_landed, b * 16 + 16)
                for j in range(2):
                    for c in range(4):
                        mm = pe.transpose(bank[4 + j][:, c * P:(c + 1) * P], XB[:, (4 * j + c) * P:(4 * j + c + 1) * P], ident)
                mm.then_inc(x_turned, 1)

            def unit(u, high_low, acc, n_k, last=False):
                xs = high_low
                n_j = 4 // n_k
                for k in range(n_k):
                    for q, (i, w) in enumerate(((0, e_high(u)), (0, e_low(u)), (1, e_high(u)))):
                        for j in range(n_j):
                            mm = pe.matmul(acc[j][:, :], xs[i][:, (u % 2) * n_k + k, :], w[:, n_j * k + j, :],
                                           start=(u % 2 == 0 and k == 0 and q == 0), stop=(u % 2 == 1 and k == n_k - 1 and q == 2))
                mm.then_inc(ew_used, 1)

            def down(base):
                for u in (4, 5):
                    pe.wait_ge(ew_low, base + u - 3)
                    unit(u, AT, (bank[2], bank[3]), 2)

            def block_of_experts(b, before=None, first=False, last=False):
                for u in range(4):
                    pe.wait_ge(ew_low, b * 6 + u + 1)
                    if u == 0:
                        pe.wait_ge(x_low, b * 2 + 2)
                    if u % 2 == 0 and not first:
                        pe.wait_ge((sg_done, pr_done)[u // 2], b)
                    unit(u, XBT, (bank[u // 2],), 4)
                if not last:
                    turn_x(b + 1)
                if first:
                    pe.wait_ge(ew_used, 4)
                    pe.sem_inc(ew_used, 2)
                else:
                    pe.wait_ge(a_low, b)
                    pe.wait_ge(y_a, before)
                    pe.wait_ge(y_v, before)
                    down(b * 6 + 4)
                pe.wait_ge(pr_done, b + 1)
                for c in range(4):
                    mm = pe.transpose(bank[6][:, c * P:(c + 1) * P], PR[:, c * P:(c + 1) * P], ident)
                mm.then_inc(a_turned, 1)

            turn_x(0)
            block_of_experts(0, first=True)
            final = pe.value_load(table_u[0:1, 62:63], min_val=MINB - 1, max_val=MAXB - 1)
            with pe.Fori(1, final) as b:
                block_of_experts(b, b - 1)
            block_of_experts(final, pe.value_load(table_u[0:1, 61:62], min_val=MINB - 2, max_val=MAXB - 2), last=True)
            pe.wait_ge(a_low, nb)
            pe.wait_ge(y_a, final)
            pe.wait_ge(y_v, final)
            down(nb * 6)
            for t in range(TT):
                pe.wait_ge(y_sum, t + 1)
                if t >= 2:
                    pe.wait_ge(x3, t - 1)
                for j in range(2):
                    for c in range(4):
                        mm = pe.transpose(bank[2 * (t % 2) + j][:, c * P:(c + 1) * P], S[:, 4 * t + j, c * P:(c + 1) * P], ident)
                mm.then_inc(y_back, 1)
            pe_stats(pe, "final", lambda c: H[:, c, :])
            pe_layernorm(pe, lnin, lambda c: X[:, c, :], lambda c: pe.wait_ge(h_done, 40 + c + 1))
            layer_tensor(pe)

        def moe_vector(dve, st):
            dve.wait_ge(routed, 1)
            st.do(dve.tensor_tensor(LG, bank[5][:, 0:TT * NR].rearrange("p (t n) -> p t n", t=TT),
                                      routb[:, None, :].to_broadcast([P, TT, NR]), ALU.add))
            gl = LG[:, :, 0:GROUPS]
            el = LG[:, :, GROUPS:NR].rearrange("p t (g e) -> p t g e", e=EPG)

            def step(ins):
                st.do(ins)
                st.wait()

            def first_of_max(vals, n, mx, tmp, hot):
                step(dve.tensor_reduce(mx, vals, AX.X, ALU.max))
                step(dve.tensor_tensor(tmp, vals, mx.to_broadcast([P, TT, n]), ALU.is_equal))
                desc = konst[:, CK["desc"] + EPG - n:CK["desc"] + EPG]
                step(dve.tensor_tensor(tmp, tmp, desc[:, None, :].to_broadcast([P, TT, n]), ALU.mult))
                step(dve.tensor_reduce(hot[:, :, 0:1], tmp, AX.X, ALU.max))
                step(dve.tensor_tensor(tmp, tmp, hot[:, :, 0:1].to_broadcast([P, TT, n]), ALU.is_equal))
                step(dve.tensor_copy(hot, tmp))

            st.wait()
            gmax, m1, m2 = rt(0, 1), rt(1, 1), rt(2, 1)
            g_hot, tmp4 = rt(3, GROUPS), rt(4, GROUPS)
            first_of_max(gl, GROUPS, gmax, tmp4, g_hot)
            gd = rt(5, GROUPS)
            st.tell(dve.tensor_tensor(gd, gl, gmax.to_broadcast([P, TT, GROUPS]), ALU.subtract), r_d)
            big = rt(6, GROUPS, EPG)
            esel, tmp8, hot1, hot2 = rt(7, EPG), rt(8, EPG), rt(10, EPG), rt(11, EPG)
            step(dve.tensor_tensor(big, el, g_hot[:, :, :, None].to_broadcast([P, TT, GROUPS, EPG]), ALU.mult))
            step(dve.tensor_reduce(esel, big.rearrange("p t g e -> p t e g"), AX.X, ALU.add))
            first_of_max(esel, EPG, m1, tmp8, hot1)
            step(dve.scalar_tensor_tensor(esel, hot1, -3e38, esel, ALU.mult, ALU.add))
            first_of_max(esel, EPG, m2, tmp8, hot2)
            st.tell(dve.tensor_tensor(m2, m2, m1, ALU.subtract), r_d)
            hots = [rt(12, GROUPS, EPG), rt(13, GROUPS, EPG)]
            for dst, hot in zip(hots, (hot1, hot2)):
                step(dve.tensor_copy(dst, g_hot[:, :, :, None].to_broadcast([P, TT, GROUPS, EPG])))
                step(dve.tensor_tensor(dst, dst, hot[:, :, None, :].to_broadcast([P, TT, GROUPS, EPG]), ALU.mult))
            st.tell(dve.tensor_tensor(rt(9, GROUPS, EPG), hots[0], hots[1], ALU.add), mask_done)
            dve.wait_ge(r_exp, 2)
            gsum, ex = rt(14, 1), rt(15, 1)
            w1, w2 = route[:, 0:1, :].rearrange("p o t -> p t o"), route[:, 1:2, :].rearrange("p o t -> p t o")
            step(dve.tensor_reduce(gsum, gd, AX.X, ALU.add))
            step(dve.tensor_copy(ex, m2))
            step(dve.tensor_scalar(m1, ex, 1.0, None, ALU.add))
            step(dve.tensor_tensor(m1, m1, gsum, ALU.mult))
            step(dve.reciprocal(w1, m1))
            step(dve.tensor_tensor(w2, w1, ex, ALU.mult))
            dve.wait_ge(routed, 2)
            cnt, nblk, end, begin = (rt(i, 8)[:, 0:TT, :].rearrange("p t g -> p (t g)") for i in (16, 17, 18, 19))
            step(dve.tensor_copy(cnt, bank[4][:, 0:EXPERTS]))
            step(dve.tensor_scalar(nblk, cnt, 0.0, None, ALU.is_gt))
            for m in range(1, TT):
                step(dve.scalar_tensor_tensor(nblk, cnt, float(m * P), nblk, ALU.is_gt, ALU.add))
            step(dve.tensor_tensor_scan(end, ones[:, 0:EXPERTS], nblk, 0.0, ALU.mult, ALU.add))
            step(dve.tensor_tensor(begin, end, nblk, ALU.subtract))
            step(dve.tensor_scalar(begin, begin, float(P), None, ALU.mult))
            pos = rt(20, EXPERTS)
            step(dve.tensor_tensor(pos, bank[6][:, 0:TT * EXPERTS].rearrange("p (t e) -> p t e", e=EXPERTS),
                                   begin[:, None, :].to_broadcast([P, TT, EXPERTS]), ALU.add))
            for w in range(2):
                hot = hots[w].rearrange("p t g e -> p t (g e)")
                step(dve.tensor_tensor(hot, hot, pos, ALU.mult))
                step(dve.tensor_reduce(route[:, 2 + w:3 + w, :].rearrange("p o t -> p t o"), hot, AX.X, ALU.add))
                step(dve.tensor_copy(slots[:, w, :], route[:, 2 + w, :]))
            cmp = S[0:1, 19:22, :].rearrange("p a n -> p (a n)")[:, 0:TABLE * EXPERTS].rearrange("p (b e) -> p b e", e=EXPERTS)
            blk = konst[0:1, CK["block"]:CK["block"] + TABLE]
            step(dve.tensor_tensor(cmp, end[0:1, None, :].to_broadcast([1, TABLE, EXPERTS]), blk[:, :, None].to_broadcast([1, TABLE, EXPERTS]), ALU.is_le))
            step(dve.tensor_reduce(table[0:1, 0:TABLE, None], cmp, AX.X, ALU.add))
            step(dve.tensor_scalar(table[0:1, 0:TABLE], table[0:1, 0:TABLE], float(EXPERTS - 1), None, ALU.min))
            step(dve.tensor_copy(table_u[0:1, 0:TABLE], table[0:1, 0:TABLE]))
            nblocks = end[0:1, EXPERTS - 1:EXPERTS]
            step(dve.tensor_scalar(table_u[0:1, 62:63], nblocks, -1.0, None, ALU.add))
            step(dve.tensor_scalar(table_u[0:1, 61:62], nblocks, -2.0, None, ALU.add))
            st.tell(dve.tensor_copy(table_u[0:1, 63:64], nblocks), slots_done)
            st.wait()
            nb = dve.value_load(table_u[0:1, 63:64], min_val=MINB, max_val=MAXB)

            def weights_low(u, count):
                dve.wait_ge(ew_high, count)
                dve.tensor_tensor(e_low(u), e_raw(u), as_f32(e_high(u)), ALU.subtract).then_inc(ew_low, 1)

            def rows_low(b):
                for j in range(2):
                    dve.wait_ge(x_high, b * 2 + j + 1)
                    x = slice(4 * j, 4 * j + 4)
                    dve.tensor_tensor(XBT[1][:, x, :], bank[4 + j][:, :].rearrange("p (c s) -> p c s", s=P), as_f32(XBT[0][:, x, :]),
                                      ALU.subtract).then_inc(x_low, 1)

            def lay_y(b, used):
                dve.wait_ge(ew_used, used)
                dve.wait_ge(y_stored, b * 16)
                dve.tensor_copy(YB[:, 1, :], bank[3][:, :]).then_inc(y_v, 1)

            def block_of_experts(b, before=None, first=False, last=False):
                weights_low(3, b * 6 + 4)
                if first:
                    dve.wait_ge(ew_low, 4)
                    dve.sem_inc(ew_low, 2)
                else:
                    weights_low(4, b * 6 + 5)
                    weights_low(5, b * 6 + 6)
                dve.wait_ge(ew_used, b * 6 + 4)
                dve.wait_ge(sg_done, b + 1)
                if not first:
                    dve.wait_ge(a_turned, b)
                dve.tensor_tensor(PR, SG, bank[1][:, :], ALU.mult).then_inc(pr_done, 1)
                if not last:
                    rows_low(b + 1)
                    weights_low(0, b * 6 + 7)
                    weights_low(1, b * 6 + 8)
                dve.wait_ge(a_high, b + 1)
                dve.tensor_tensor(AT[1], bank[6][:, :].rearrange("p (c s) -> p c s", s=P), as_f32(AT[0]), ALU.subtract).then_inc(a_low, 1)
                if not first:
                    lay_y(before, b * 6 + 6)
                if not last:
                    weights_low(2, b * 6 + 9)

            for u in range(3):
                weights_low(u, u + 1)
            rows_low(0)
            block_of_experts(0, first=True)
            final = dve.value_load(table_u[0:1, 62:63], min_val=MINB - 1, max_val=MAXB - 1)
            with dve.Fori(1, final) as b:
                block_of_experts(b, b - 1)
            block_of_experts(final, dve.value_load(table_u[0:1, 61:62], min_val=MINB - 2, max_val=MAXB - 2), last=True)
            weights_low(4, nb * 6 + 1)
            weights_low(5, nb * 6 + 2)
            lay_y(final, nb * 6 + 2)
            for t in range(TT):
                dve.wait_ge(y_got[t % 2], 32 * (t // 2 + 1))
                a, b2 = S[:, 4 * t:4 * t + 2, :], S[:, 4 * t + 2:4 * t + 4, :]
                step(dve.tensor_scalar(a, a, route[:, 0, t:t + 1], None, ALU.mult))
                st.tell(dve.scalar_tensor_tensor(a, b2, route[:, 1, t:t + 1], a, ALU.mult, ALU.add), y_sum)
            for t in range(TT):
                dve.wait_ge(y_back, t + 1)
                for j in range(2):
                    xs = X[:, 4 * j:4 * j + 4, t * P:(t + 1) * P]
                    ins = dve.tensor_tensor(xs, xs, bank[2 * (t % 2) + j][:, :].rearrange("p (c s) -> p c s", s=P), ALU.add)
                    st.tell(ins, x3) if j else st.do(ins)
            dve_norm(dve, st, "final", lambda c: X[:, c, :], lambda c: X[:, c, :])
            dve_layernorm(dve, st, lnin, lambda c: X[:, c, :], lambda c: col("lnin_g", c))
            layer_vector(dve)

        def moe_scalar(act, st):
            for t in range(TT):
                act.wait_ge(rows_turned, t + 1)
                for j in range(2):
                    st.tell(act.activation(HT[:, t, j * 512:(j + 1) * 512], bank[2 * (t % 2) + j][:, :], ACT.Copy), rows_laid)
                st.wait()
                act.dma_start(rows_dram[t * P:(t + 1) * P, :], HT[:, t, :]).then_inc(rows_stored, 16)
            for i, a in enumerate((rt(5, GROUPS), rt(2, 1))):
                act.wait_ge(r_d, i + 1)
                st.tell(act.activation(a, a, ACT.Exp), r_exp)
            act.wait_ge(slots_done, 1)
            nb = act.value_load(table_u[0:1, 63:64], min_val=MINB, max_val=MAXB)

            def weights_high(u, landed, used=None):
                act.wait_ge((g_landed, u_landed, d_landed)[u // 2], landed)
                if used is not None:
                    act.wait_ge(ew_used, used)
                act.activation(e_high(u), e_raw(u), ACT.Copy).then_inc(ew_high, 1)

            def rows_high(b, first=False):
                act.wait_ge(x_turned, b + 1)
                if not first:
                    act.wait_ge(ew_used, b * 6 - 2)
                for j in range(2):
                    act.activation(XBT[0][:, 4 * j:4 * j + 4, :], bank[4 + j][:, :].rearrange("p (c s) -> p c s", s=P), ACT.Copy).then_inc(x_high, 1)

            def lay_y(b, used):
                act.wait_ge(ew_used, used)
                act.wait_ge(y_stored, b * 16)
                act.activation(YB[:, 0, :], bank[2][:, :], ACT.Copy).then_inc(y_a, 1)
                act.wait_ge(y_a, b + 1)
                act.wait_ge(y_v, b + 1)
                act.dma_start(y_dram[bass.ds(b * P, P), :], YB[:, :, :].rearrange("p a n -> p (a n)")).then_inc(y_stored, 16)

            def block_of_experts(b, before=None, first=False, last=False):
                weights_high(3, b * 16 + 16, b * 6 + 1)
                act.wait_ge(ew_used, b * 6 + 2)
                if not first:
                    act.wait_ge(pr_done, b)
                act.activation(SG, bank[0][:, :], ACT.Silu).then_inc(sg_done, 1)
                if first:
                    act.wait_ge(ew_high, 4)
                    act.sem_inc(ew_high, 2)
                else:
                    weights_high(4, b * 16, b * 6 + 2)
                    weights_high(5, b * 16, b * 6 + 3)
                if not last:
                    rows_high(b + 1)
                    weights_high(0, b * 16 + 32, b * 6 + 4)
                    weights_high(1, b * 16 + 32, b * 6 + 5)
                act.wait_ge(a_turned, b + 1)
                if not first:
                    act.wait_ge(ew_used, b * 6 + 6)
                act.activation(AT[0], bank[6][:, :].rearrange("p (c s) -> p c s", s=P), ACT.Copy).then_inc(a_high, 1)
                if not first:
                    lay_y(before, b * 6 + 6)
                if not last:
                    weights_high(2, b * 16 + 32, b * 6 + 6)

            act.wait_ge(rows_stored, 16 * TT)
            for u in range(3):
                weights_high(u, 16)
            rows_high(0, first=True)
            act.wait_ge(spare, 16 * (TABLE - MINB) // 8)
            block_of_experts(0, first=True)
            final = act.value_load(table_u[0:1, 62:63], min_val=MINB - 1, max_val=MAXB - 1)
            with act.Fori(1, final) as b:
                block_of_experts(b, b - 1)
            block_of_experts(final, act.value_load(table_u[0:1, 61:62], min_val=MINB - 2, max_val=MAXB - 2), last=True)
            weights_high(4, nb * 16, nb * 6)
            weights_high(5, nb * 16, nb * 6)
            lay_y(final, nb * 6 + 2)
            act.wait_ge(y_stored, nb * 16)
            act.wait_ge(x3, TT)
            for c in range(DC):
                st.tell(act.activation(H[:, c, :], X[:, c, :], ACT.Square), sq_done)
            act_rstd(act, st, "final")
            act_layernorm(act, st, lnin, lambda c: X[:, c, :], lambda c: H[:, c, :], lambda c: X[:, c, :], lambda c: col("lnin_b", c))
            layer_scalar(act)
        def ln_sems(name, chunks, banks=(7, 5)):
            return dict({k: sem(f"{name}_{k}") for k in ("mean", "centred", "squared", "var", "rstd", "scaled", "ready")},
                        chunks=chunks, banks=banks, use=0)

        def pe_layernorm(pe, l, src, ready, sq=lambda c: H[:, c, :]):
            n = l["chunks"]
            for c in range(n):
                ready(c)
                mm = pe.matmul(bank[l["banks"][0]][:, :], ones, src(c), start=(c == 0), stop=(c == n - 1))
            mm.then_inc(l["mean"], 1)
            for c in range(n):
                pe.wait_ge(l["squared"], l["use"] * n + c + 1)
                mm = pe.matmul(bank[l["banks"][1]][:, :], ones, sq(c), start=(c == 0), stop=(c == n - 1))
            mm.then_inc(l["var"], 1)

        def dve_centre(dve, st, l, src):
            dve.wait_ge(l["mean"], l["use"] + 1)
            for c in range(l["chunks"]):
                st.tell(dve.scalar_tensor_tensor(src(c), bank[l["banks"][0]][:, :], -1.0 / (l["chunks"] * P), src(c), ALU.mult, ALU.add), l["centred"])

        def dve_scale(dve, st, l, src, g, r=None):
            r = rstd if r is None else r
            dve.wait_ge(l["rstd"], l["use"] + 1)
            for c in range(l["chunks"]):
                st.tell(dve.scalar_tensor_tensor(src(c), src(c), g(c), r[:, :], ALU.mult, ALU.mult), l["scaled"])

        def dve_layernorm(dve, st, l, src, g, r=None):
            dve_centre(dve, st, l, src)
            dve_scale(dve, st, l, src, g, r)

        def act_variance(act, st, l, src, sq, r=None):
            r = rstd if r is None else r
            for c in range(l["chunks"]):
                act.wait_ge(l["centred"], l["use"] * l["chunks"] + c + 1)
                st.tell(act.activation(sq(c), src(c), ACT.Square), l["squared"])
            act.wait_ge(l["var"], l["use"] + 1)
            st.do(act.activation(r[:, :], bank[l["banks"][1]][:, :], ACT.Ln, scale=1.0 / (l["chunks"] * P), bias=eps[:, 1:2])); st.wait()
            st.tell(act.activation(r[:, :], r[:, :], ACT.Exp, scale=-0.5), l["rstd"])

        def act_shift(act, st, l, src, dst, b, func=ACT.Identity):
            for c in range(l["chunks"]):
                act.wait_ge(l["scaled"], l["use"] * l["chunks"] + c + 1)
                st.tell(act.activation(dst(c), src(c), func, bias=b(c)), l["ready"])

        def act_layernorm(act, st, l, src, sq, dst, b, func=ACT.Identity, r=None):
            act_variance(act, st, l, src, sq, r)
            act_shift(act, st, l, src, dst, b, func)

        lnin = ln_sems("ln_in", DC)

        cos64, sin64, cos96, sin96 = (AUX[:, i, :] for i in range(4))
        UQ = AUX[:, 4:6, :].rearrange("p a n -> p (a n)")[:, 0:2 * 4 * HM].rearrange("p (k n) -> p k n", k=2)
        UKV = AUX[:, 6, :]
        SGW = AUX[:, 7, :].rearrange("p (g q) -> p g q", g=4)
        sgb = sb("sgu_bias", [P, GC, P])
        r_conv, r_sgu = (gatew[:, i, :, :].rearrange("p a n -> p (a n)") for i in range(2))
        AA, SGA, CV, CSQ = (MKV[:, 2 * i:2 * i + 2, :] for i in range(4))
        QG, KG, K2, VG = QKVG[:, 0:2, :], QKVG[:, 2, :], QKVG[:, 3:5, :], QKVG[:, 5, :].rearrange("p (t n) -> p t n", t=TT)
        CQ, CKV, KR, QF = QKVG[:, 6:8, :], QKVG[:, 8, :], QKVG[:, 9, :], QKVG[:, 10:14, :]
        SVT = QKVG[:, 14:16, :].rearrange("p a n -> p (a n)").rearrange("p (t n) -> p t n", t=TT)
        KF, VF = S[:, 12:16, :], S[:, 16:18, :].rearrange("p a n -> p (a n)").rearrange("p (t n) -> p t n", t=TT)
        U, SV = S[:, 18:20, :], S[:, 20:22, :]
        GR = S[:, 7:12, :]
        ROT = S[:, 0:3, :]

        s_tab, s_out = sem("rotary_landed"), sem("out_stored")
        layer_done, layer_go = sem("layer_done"), sem("layer_go")
        lw = [sem(f"layer_weights_landed{i}") for i in range(RING)]
        first_cleared = lw[0].num
        s_small = sem("layer_small_landed")
        l_act, l_dve, l_pool = sem("layer_act_steps"), sem("layer_dve_steps"), sem("layer_pool_steps")
        t_done, t_free = sem("layer_tiles"), sem("layer_tiles_read")
        conv_ready = sem("conv_a_done")
        g_sq, g_stat, g_rstd, g_n, g_turned, g_rot = (sem(f"gqa_{n}") for n in ("squared", "stat", "rstd", "normed", "turned", "rotated"))
        m_sq, m_stat, m_rstd, m_n, m_turned, m_rot = (sem(f"mla_{n}") for n in ("squared", "stat", "rstd", "normed", "turned", "rotated"))
        svt_done, svt_laid, mix_done, oc_done = sem("sgu_turned"), sem("sgu_laid"), sem("sgu_mixed"), sem("o_c_done")
        r_done, r_free = sem("layer_res_done"), sem("layer_res_added")
        half_landed = [sem(f"half_slot_landed{i}") for i in range(2)]
        wh_done, wl_done, xh_done = sem("weights_high"), sem("weights_low"), sem("x_high")
        xl_done, ph_done, pl_done = sem("x_low"), sem("product_high"), sem("product_low")
        f_done, f_free, f_silu, f_act = sem("up_tiles"), sem("up_tiles_convolved"), sem("silu_ready"), sem("ffn_product")
        latt = {k: sem(f"{k}_layer") for k in ("scored", "shifted", "expd", "normed", "turned", "laid", "summed", "att_out")}
        ln_a, ln_s = ln_sems("ln_a", GC, (7, 4)), ln_sems("ln_sgu", GC, (5, 5))
        ln_m = ln_sems("ln_out", DC)
        ln_f = dict(ln_m, use=1, banks=(0, 1))
        last_cleared = ln_m["ready"].num

        def col2(name, i=0, p=P):
            return cols2[0:p, C2[name] + i:C2[name] + i + 1]

        PARTS = ((0, 8), (8, 14), (14, FC))
        units = []
        for p, (lo, hi) in enumerate(PARTS):
            first = 0 if p == 0 else PARTS[p - 1][1] // 2 + 1
            for j in range(first, min(hi // 2 + 1, FC // 2)):
                units += [("up", j, 0), ("up", j, 1)]
            units += [("down", p, m) for m in range(DC // 2)]
        ups = [n for n, x in enumerate(units) if x[0] == "up"]
        downs = [n for n, x in enumerate(units) if x[0] == "down"]
        assert len(ups) == FC

        def unit_used(n):
            if n in ups:
                return f_done, 2 * ups.index(n) + 2
            return r_done, DC + 2 * downs.index(n) + 2

        def unit_source(l, n):
            kind, a, b = units[n]
            if kind == "up":
                w = A["ffn_w_up"][bass.ds(l, 1)].rearrange("o (k p) (h n) -> h p (o k) n", p=P, h=2)
                return w[b, :, :, a * 256:(a + 1) * 256], DC
            lo, hi = PARTS[a]
            w = A["ffn_w_down"][bass.ds(l, 1)].rearrange("o (k p) n -> p (o k) n", p=P)
            return w[:, lo:hi, b * 256:(b + 1) * 256], hi - lo

        def k_chunks(n):
            return DC if units[n][0] == "up" else PARTS[units[n][1]][1] - PARTS[units[n][1]][0]

        def raw_half(n):
            return ring[0][:, 4 * (n % 2):4 * (n % 2) + 4, :].rearrange("p a (b n) -> p (a b) n", n=256)[:, 0:k_chunks(n), :]

        def product_parts(c):
            if PARTS[1][0] <= c < PARTS[1][1]:
                i = c - PARTS[1][0]
                return SP[:, 16 + i, :], QP[:, 8 + i, :]
            i = c - (0 if c < PARTS[1][0] else PARTS[2][0])
            return SP[:, i, :], SP[:, 8 + i, :]

        def layer_uses(l):
            w_in = A["w_in_2"][bass.ds(l, 1)].rearrange("o (k p) n -> p (o k) n", p=P)
            w_out = A["w_out_2"][bass.ds(l, 1)].rearrange("o (k p) n -> p (o k) n", p=P)
            whole = lambda r: r[:, :, :]
            uses = [([(whole, w_in[:, :, 512 * j:512 * (j + 1)])], t_done, 4 * j + 4) for j in range(3)]
            uses += [([(lambda r: r[:, :, 0:QL + KVL + ROPE], w_in[:, :, 1536:1536 + QL + KVL + ROPE])], t_done, 16)]
            uses += [([(whole, w_out[:, :, 512 * j:512 * (j + 1)])], r_done, 4 * j + 4) for j in range(2)]
            return uses

        N_USES = 4 + 2

        def end_of_layer(eng, l):
            eng.sem_inc(layer_done, 1)
            if eng is nc.sync:
                wait_counted(eng, layer_go, l + 1)
            else:
                eng.wait_ge(layer_go, l + 1)

        l_units = []
        for h in range(8):
            r = slice(64 * (h % 2), 64 * (h % 2) + 64)
            for t in range(TT):
                tt = slice(t * P, (t + 1) * P)
                if h < 4:
                    sc = (QG[r, h // 2, tt], K2[r, h // 2, :])
                    val = lambda kt, h=h: VG[:, kt, 64 * (h // 2):64 * (h // 2) + 64]
                else:
                    sc = (QF[0:HM, h - 4, tt], KF[0:HM, h - 4, :])
                    val = lambda kt, h=h: VF[:, kt, 64 * (h - 4):64 * (h - 4) + 64]
                l_units.append(dict(scores=[sc], keys=T, t=t, bias=None, pt=h % 2, scale=float(64 if h < 4 else HM) ** -0.5,
                                    values=[(5 + (h // 2) % 2, r, val)],
                                    out=[(h // 2, 5 + (h // 2) % 2)] if h % 2 and t == TT - 1 else []))
        l_cfg = dict(units=l_units, sems=latt, base=(0, 0), dest=lambda c: H[:, (2, 3, 6, 7)[c], :], scale=1.0)

        def layer_sync(sp):
            sp.wait_ge(att["shifted_max"], 8 * TT)
            sp.dma_start(AUX[:, 0:4, :], A["rotary"]).then_inc(s_tab, 16)
            wait_counted(sp, ew_low, sp.value_load(table_u[0:1, 63:64], min_val=MINB, max_val=MAXB) * 6 + 2)
            sp.wait_ge(y_got[(TT - 1) % 2], 16 * TT)
            with sp.Fori(0, L2) as l:
                sp.dma_start(cols2[:, :], A["cols2"][bass.ds(l, 1)].rearrange("o p n -> p (o n)")).then_inc(s_small, 16)
                sp.dma_start(UKV, A["w_ukv"][bass.ds(l, 1)].rearrange("o p n -> p (o n)")).then_inc(s_small, 16)
                sp.dma_start(UQ[:, 0, :], A["w_uq"][bass.ds(l, 1), 0:P, :].rearrange("o p n -> p (o n)")).then_inc(s_small, 16)
                sp.dma_start(UQ[0:QL - P, 1, :], A["w_uq"][bass.ds(l, 1), P:QL, :].rearrange("o p n -> p (o n)")).then_inc(s_small, 16)
                sp.dma_start(SGW, A["sgu_wT"][bass.ds(l, 1)].rearrange("o q g p -> q (o g) p")).then_inc(s_small, 16)
                for g in range(4):
                    src = A["sgu_b"][bass.ds(l, 1), g:g + 1, :].rearrange("o g p -> o (g p)")
                    sp.dma_start(sgb[64 * (g % 2):64 * (g % 2) + 64, g // 2, :], src.to_broadcast([64, P])).then_inc(s_small, 16)
                uses = layer_uses(l)
                assert len(uses) == N_USES
                for n, (parts, _, _) in enumerate(uses):
                    if n >= RING:
                        sp.wait_ge(*uses[n - RING][1:])
                    for place, src in parts:
                        sp.dma_start(place(ring[n % RING]), src).then_inc(lw[n % RING], 16)
                sp.wait_ge(*uses[3][1:])
                for n in range(len(units)):
                    if n >= 2:
                        sp.wait_ge(wl_done, n - 1)
                    sp.dma_start(raw_half(n), unit_source(l, n)[0]).then_inc(half_landed[n % 2], 16)
                end_of_layer(sp, l)

        def layer_gpsimd(pool):
            with pool.Fori(0, L2) as l:
                st = Steps(pool, l_pool)
                for j in range(FC // 2):
                    for i in range(2):
                        pool.wait_ge(f_silu, 2 * j + i + 1)
                        pool.wait_ge(f_free, 4 * j + 2 + i + 1)
                        b = 2 * (j % 2) + i
                        if j:
                            pool.wait_ge(pl_done, 2 * (j - 1) + i + 1)
                        st.tell(pool.tensor_tensor(QKVG[:, 14 + i, :], QKVG[:, b, :], QKVG[:, 4 + b, :], ALU.mult), f_act)
                st.wait()
                wait_counted(pool, layer_done, 4 * l + 4)
                pool.sem_clear(range(first_cleared, last_cleared + 1))
                pool.sem_inc(layer_go, 1)

        def layer_tensor(pe):
            h = lambda k: H[:, k, :]
            x = lambda k: X[:, k, :]
            pe.wait_ge(s_tab, 16)
            pe.wait_ge(lnin["ready"], DC)
            with pe.Fori(0, L2) as l:
                use = [0]
                landed = [0] * RING

                def slot():
                    n = use[0]
                    use[0] += 1
                    landed[n % RING] += 16
                    pe.wait_ge(lw[n % RING], landed[n % RING])
                    return ring[n % RING]

                read = {}

                def take(b):
                    if b in read:
                        pe.wait_ge(*read[b])

                tiles = [0]

                def tile(mms, count=tiles, done=t_done, free=t_free):
                    n = count[0]
                    if n >= 4:
                        pe.wait_ge(free, n - 3)
                    mms(bank[n % 4]).then_inc(done, 1)
                    count[0] += 1

                def products(w, m0, m, src, rows=slice(0, P), k_tiles=DC):
                    def mms(b):
                        for k in range(k_tiles):
                            mm = pe.matmul(b[rows, :], w[:, k, m0:m0 + m], src(k), start=(k == 0), stop=(k == k_tiles - 1))
                        return mm
                    return mms

                pe.wait_ge(s_small, 16 * 9)
                w = slot()
                for m in range(4):
                    tile(products(w, m * P, P, x))
                w = slot()
                for m in range(3):
                    tile(products(w, m * P, P, x))

                def values(b):
                    for t in range(TT):
                        for k in range(DC):
                            mm = pe.matmul(b[:, t * P:(t + 1) * P], X[:, k, t * P:(t + 1) * P], w[:, k, 3 * P:4 * P], start=(k == 0), stop=(k == DC - 1))
                    return mm
                tile(values)
                w = slot()
                for m in range(4):
                    tile(products(w, m * P, P, x))
                for i in range(3):
                    pe.wait_ge(g_sq, i + 1)
                    pe.matmul(bank[4 + i][:, :], const("pair"), S[:, 4 + i, :], start=True, stop=True).then_inc(g_stat, 1)
                    read[4 + i] = (g_rstd, i + 1)
                w = slot()
                tile(products(w, 0, P, x))
                tile(products(w, P, QL - P, x, slice(0, QL - P)))
                tile(products(w, QL, KVL, x))
                tile(products(w, QL + KVL, ROPE, x, slice(64, HM)))
                pe.wait_ge(m_sq, 2)
                pe.matmul(bank[7][:, :], ones, H[:, 2, :], start=True, stop=False)
                pe.matmul(bank[7][:, :], ones[0:QL - P, :], H[0:QL - P, 3, :], start=False, stop=True).then_inc(m_stat, 1)
                read[7] = (m_rstd, 1)
                pe.wait_ge(m_sq, 3)
                take(4)
                pe.matmul(bank[4][:, :], ones, H[:, 6, :], start=True, stop=True).then_inc(m_stat, 1)
                read[4] = (m_rstd, 2)
                take(5)
                for c in range(GC):
                    pe.wait_ge(t_free, 11 + c)
                    mm = pe.matmul(bank[5][:, :], ones, SV[:, c, :], start=(c == 0), stop=(c == GC - 1))
                mm.then_inc(ln_s["mean"], 1)
                read[5] = (ln_s["centred"], GC)
                for i, b in enumerate((6, 7, 4)):
                    pe.wait_ge(g_n, i + 1)
                    take(b)
                    pe.matmul(bank[b][:, :], const("perm"), (QG[:, 0, :], QG[:, 1, :], KG)[i], start=True, stop=True).then_inc(g_turned, 1)
                    read[b] = (g_rot, i + 1)
                take(5)
                for c in range(GC):
                    pe.wait_ge(ln_s["squared"], c + 1)
                    mm = pe.matmul(bank[5][:, :], ones, H[:, 4 + c, :], start=(c == 0), stop=(c == GC - 1))
                mm.then_inc(ln_s["var"], 1)
                read[5] = (ln_s["rstd"], 1)
                for hh in range(4):
                    def mms(b):
                        pe.wait_ge(m_n, 2)
                        pe.matmul(b[0:HM, :], UQ[:, 0, hh * HM:(hh + 1) * HM], CQ[:, 0, :], start=True, stop=False)
                        return pe.matmul(b[0:HM, :], UQ[0:QL - P, 1, hh * HM:(hh + 1) * HM], CQ[0:QL - P, 1, :], start=False, stop=True)
                    tile(mms)
                for hh in range(4):
                    def mms(b):
                        pe.wait_ge(m_n, 3)
                        return pe.matmul(b[0:64, :], UKV[:, hh * P:hh * P + 64], CKV, start=True, stop=True)
                    tile(mms)
                for half in range(2):
                    def mms(b):
                        for t in range(2):
                            tok = slice((2 * half + t) * P, (2 * half + t + 1) * P)
                            mm = pe.matmul(b[:, t * 256:(t + 1) * 256], CKV[:, tok],
                                           UKV.rearrange("p (h n) -> p h n", h=4)[:, :, 64:128], start=True, stop=True)
                        return mm
                    tile(mms)
                take(6)
                pe.wait_ge(t_free, 16)
                pe.matmul(bank[6][64:HM, :], const("perm96")[64:HM, 64:HM], KR[64:HM, :], start=True, stop=True).then_inc(m_turned, 1)
                read[6] = (m_rot, 1)
                for hh, b in enumerate((7, 4, 5, 6)):
                    take(b)
                    pe.wait_ge(t_free, 17 + hh)
                    pe.matmul(bank[b][0:HM, :], const("perm96")[0:HM, 0:HM], QF[0:HM, hh, :], start=True, stop=True).then_inc(m_turned, 1)
                    read[b] = (m_rot, 2 + hh)
                take(7)
                take(4)
                pe_layernorm(pe, ln_a, lambda c: CV[:, c, :], lambda c: pe.wait_ge(conv_ready, c + 1), lambda c: CSQ[:, c, :])
                read[7], read[4] = (ln_a["centred"], GC), (ln_a["rstd"], 1)
                for c, b in enumerate((5, 6)):
                    take(b)
                    pe.wait_ge(ln_s["ready"], c + 1)
                    for t in range(TT):
                        mm = pe.transpose(bank[b][:, t * P:(t + 1) * P], SV[:, c, t * P:(t + 1) * P], ident)
                    mm.then_inc(svt_done, 1)
                    read[b] = (svt_laid, c + 1)
                pe.wait_ge(svt_laid, GC)
                for c, b in enumerate((7, 4)):
                    take(b)
                    for g in (2 * c, 2 * c + 1):
                        for t in range(TT):
                            mm = pe.matmul(bank[b][64 * (g % 2):64 * (g % 2) + 64, t * P:(t + 1) * P], SVT[:, t, g * 64:(g + 1) * 64],
                                           SGW[:, g, :], start=True, stop=True)
                    mm.then_inc(mix_done, 1)
                    read[b] = (oc_done, c + 1)
                pe.wait_ge(t_free, 26)
                for b in (4, 5, 6):
                    take(b)
                pe.wait_ge(m_rot, 5)
                pe_attention(pe, l_cfg)
                pe.wait_ge(latt["att_out"], 4)
                pe.wait_ge(ln_a["ready"], GC)
                pe.wait_ge(oc_done, 2)
                rt_ = [0]
                res = dict(count=rt_, done=r_done, free=r_free)
                for j in range(2):
                    w = slot()
                    for m in range(4):
                        tile(products(w, m * P, P, h), **res)
                pe_layernorm(pe, ln_m, x, lambda c: pe.wait_ge(r_free, c + 1))
                for n, (kind, a, b) in enumerate(units):
                    ks = k_chunks(n)
                    pe.wait_ge(wl_done, n + 1)
                    w = WHL[n % 2]
                    banks = []
                    for i in range(2):
                        if kind == "up":
                            t = 2 * ups.index(n) + i
                            if t >= 4:
                                pe.wait_ge(f_free, t - 3)
                            banks.append(bank[t % 4])
                        else:
                            t = 2 * downs.index(n) + i
                            if t >= 4:
                                pe.wait_ge(r_free, DC + t - 3)
                            banks.append(bank[4 + t % 4])

                    def products(i, k, first, last):
                        if kind == "up":
                            xs = XH[:, k, :], XL[:, k, :]
                        else:
                            xs = product_parts(PARTS[a][0] + k)
                        m = slice(i * P, (i + 1) * P)
                        for q, (u, v) in enumerate(((0, 0), (0, 1), (1, 0))):
                            mm = pe.matmul(banks[i][:, :], w[:, u, k, m], xs[v], start=first and q == 0, stop=last and q == 2)
                        return mm

                    done = f_done if kind == "up" else r_done
                    if n == 0:
                        for k in range(ks):
                            pe.wait_ge(xl_done, k + 1)
                            mm = [products(i, k, k == 0, k == ks - 1) for i in range(2)]
                            if k == ks - 1:
                                mm[0].then_inc(done, 1)
                                mm[1].then_inc(done, 1)
                    else:
                        for i in range(2):
                            for k in range(ks):
                                if kind == "down" and b == 0 and i == 0:
                                    pe.wait_ge(pl_done, PARTS[a][0] + k + 1)
                                mm = products(i, k, k == 0, k == ks - 1)
                            mm.then_inc(done, 1)
                pe.wait_ge(f_free, 2 * FC)
                pe_layernorm(pe, ln_f, x, lambda c: pe.wait_ge(r_free, DC + 2 * DC + c + 1))
                pe.wait_ge(ln_f["ready"], 2 * DC)
                end_of_layer(pe, l)

        def layer_vector(dve):
            with dve.Fori(0, L2) as l:
                st = Steps(dve, l_dve)
                x = lambda k: X[:, k, :]

                def step(ins):
                    st.do(ins)
                    st.wait()

                dve.wait_ge(s_small, 16 * 9)
                for c in range(GC):
                    dve.wait_ge(t_free, 3 + c)
                    st.do(dve.tensor_tensor(AA[:, c, :], AA[:, c, :], SGA[:, c, :], ALU.mult))
                st.wait()
                last = [None] * GC
                for n, i in enumerate([CONVA // 2] + [i for i in range(CONVA) if i != CONVA // 2]):
                    for c in range(GC):
                        o = i - CONVA // 2
                        w = col2("ca_w", i * GC + c)
                        lo, hi = max(0, -o), T - max(0, o)
                        if n == 0:
                            last[c] = st.do(dve.tensor_scalar(CV[:, c, :], AA[:, c, :], w, col2("ca_b", c), ALU.mult, ALU.add))
                            continue
                        st.wait(last[c])
                        ins = dve.scalar_tensor_tensor(CV[:, c, lo:hi], AA[:, c, lo + o:hi + o], w, CV[:, c, lo:hi], ALU.mult, ALU.add)
                        last[c] = st.tell(ins, conv_ready) if n == CONVA - 1 else st.do(ins)
                qk = (QG[:, 0, :], QG[:, 1, :], KG)
                for i in range(3):
                    dve.wait_ge(g_rstd, i + 1)
                    st.tell(dve.scalar_tensor_tensor(qk[i], qk[i], col2("kn" if i == 2 else "qn"), GR[:, i, :], ALU.mult, ALU.mult), g_n)
                dve_centre(dve, st, ln_s, lambda c: SV[:, c, :])
                for i, (a, p) in enumerate(((CQ[:, 0, :], P), (CQ[:, 1, :], QL - P), (CKV, P))):
                    dve.wait_ge(m_rstd, 1 + i // 2)
                    w = col2("mkv") if i == 2 else col2("mq", i, p)
                    st.tell(dve.scalar_tensor_tensor(a[0:p], a[0:p], w, GR[0:p, 3 + i // 2, :], ALU.mult, ALU.mult), m_n)

                def rotate(a, b, r, cos, sin, done, i):
                    step(dve.tensor_tensor(ROT[r, i % 3, :], bank[b][r, :], sin[r], ALU.mult))
                    step(dve.tensor_tensor(a[r], a[r], cos[r], ALU.mult))
                    ins = dve.tensor_tensor(a[r], a[r], ROT[r, i % 3, :], ALU.add)
                    st.tell(ins, done) if done else st.do(ins)
                    st.wait()

                for i, b in enumerate((6, 7, 4)):
                    dve.wait_ge(g_turned, i + 1)
                    rotate(qk[i], b, slice(0, P), cos64, sin64, g_rot, i)
                for kv in range(2):
                    for half in range(2):
                        st.do(dve.tensor_copy(K2[64 * half:64 * half + 64, kv, :], KG[64 * kv:64 * kv + 64, :]))
                dve_scale(dve, st, ln_s, lambda c: SV[:, c, :], lambda c: col2("sg_g", c), r_sgu)
                dve.wait_ge(m_turned, 1)
                rotate(KR, 6, slice(64, HM), cos96, sin96, None, 0)
                for hh in range(3):
                    st.do(dve.tensor_copy(KF[64:HM, hh, :], KR[64:HM, :]))
                st.tell(dve.tensor_copy(KF[64:HM, 3, :], KR[64:HM, :]), m_rot)
                for hh, b in enumerate((7, 4, 5, 6)):
                    dve.wait_ge(m_turned, 2 + hh)
                    rotate(QF[:, hh, :], b, slice(0, HM), cos96, sin96, m_rot, 1 + hh)
                dve_layernorm(dve, st, ln_a, lambda c: CV[:, c, :], lambda c: col2("la_g", c), r_conv)
                for c, b in enumerate((7, 4)):
                    dve.wait_ge(mix_done, c + 1)
                    hb = H[:, 4 + c, :].rearrange("p (t n) -> p t n", t=TT)
                    step(dve.tensor_tensor(hb, bank[b][:, :].rearrange("p (t n) -> p t n", t=TT),
                                           sgb[:, c, None, :].to_broadcast([P, TT, P]), ALU.add))
                    st.tell(dve.tensor_tensor(H[:, 4 + c, :], H[:, 4 + c, :], U[:, c, :], ALU.mult), oc_done)
                dve_attention(dve, st, l_cfg)

                for m in range(DC):
                    dve.wait_ge(r_done, m + 1)
                    st.tell(dve.scalar_tensor_tensor(X[:, m, :], X[:, m, :], ALPHA, bank[m % 4][:, :], ALU.mult, ALU.add), r_free)

                added = {}

                def weights_low(n):
                    ks = k_chunks(n)
                    dve.wait_ge(wh_done, n + 1)
                    st.tell(dve.tensor_tensor(WHL[n % 2][:, 1, 0:ks, :], raw_half(n), as_f32(WHL[n % 2][:, 0, 0:ks, :]), ALU.subtract), wl_done)

                def product_low(j):
                    for i in range(2):
                        c = 2 * j + i
                        high, low = product_parts(c)
                        dve.wait_ge(ph_done, c + 1)
                        st.tell(dve.tensor_tensor(low, QKVG[:, 14 + i, :], as_f32(high), ALU.subtract), pl_done)

                weights_low(0)
                dve_centre(dve, st, ln_m, x)
                weights_low(1)
                dve_scale(dve, st, ln_m, x, lambda c: col2("mix_g", c))
                for c in range(DC):
                    dve.wait_ge(xh_done, c + 1)
                    st.tell(dve.scalar_tensor_tensor(XL[:, c, :], X[:, c, :], col2("mix_b", c), as_f32(XH[:, c, :]), ALU.add, ALU.subtract), xl_done)

                def convolve(j, m):
                    n = 4 * j + m
                    b = 4 * (m // 2) + 2 * (j % 2) + m % 2
                    f = FC * (m // 2) + 2 * j + m % 2
                    src, dst = bank[n % 4], QKVG[:, b, :]
                    dve.wait_ge(f_done, n + 1)
                    if j >= 2:
                        dve.wait_ge(f_act, 2 * (j - 2) + m % 2 + 1)
                    tap = lambda i: col2("fc_w", i * 2 * FC + f)
                    step(dve.tensor_scalar(dst, src[:, :], tap(1), col2("fc_b", f), ALU.mult, ALU.add))
                    step(dve.scalar_tensor_tensor(dst[:, 1:T], src[:, 0:T - 1], tap(0), dst[:, 1:T], ALU.mult, ALU.add))
                    st.tell(dve.scalar_tensor_tensor(dst[:, 0:T - 1], src[:, 1:T], tap(2), dst[:, 0:T - 1], ALU.mult, ALU.add), f_free)

                for n, (kind, a, b) in enumerate(units):
                    pair = units[n - 1][1] if n and units[n - 1][0] == "up" and units[n - 1][2] else None
                    last_part = pair == FC // 2 - 1
                    if last_part:
                        product_low(pair)
                    for i in range(2):
                        if kind == "up":
                            convolve(a, 2 * b + i)
                        else:
                            m, t = 2 * b + i, 2 * downs.index(n) + i
                            dve.wait_ge(r_done, DC + t + 1)
                            out_bank = bank[4 + t % 4][:, :]
                            if a == 0:
                                dve.wait_ge(ln_m["ready"], DC)
                                ins = dve.scalar_tensor_tensor(X[:, m, :], X[:, m, :], ALPHA, out_bank, ALU.mult, ALU.add)
                            else:
                                st.wait(added[m])
                                ins = dve.tensor_tensor(X[:, m, :], X[:, m, :], out_bank, ALU.add)
                            added[m] = st.tell(ins, r_free)
                        if i == 0 and pair is not None and not last_part:
                            product_low(pair)
                    if n + 2 < len(units):
                        weights_low(n + 2)
                dve_layernorm(dve, st, ln_f, x, lambda c: col2("ffn_g", c))
                st.wait()
                end_of_layer(dve, l)

        def layer_scalar(act):
            with act.Fori(0, L2) as l:
                st = Steps(act, l_act)
                n = [0]
                act.wait_ge(s_small, 16 * 9)

                def evac(dst, rows=slice(0, P), func=ACT.Copy):
                    act.wait_ge(t_done, n[0] + 1)
                    st.tell(act.activation(dst, bank[n[0] % 4][rows, :], func), t_free)
                    n[0] += 1

                def rms(i, b, scale, done):
                    st.do(act.activation(GR[:, i, :], bank[b][:, :], ACT.Ln, scale=scale, bias=eps[:, 0:1])); st.wait()
                    st.tell(act.activation(GR[:, i, :], GR[:, i, :], ACT.Exp, scale=-0.5), done)

                for c in range(2):
                    evac(AA[:, c, :])
                for c in range(2):
                    evac(SGA[:, c, :], func=ACT.Sigmoid)
                qk = (QG[:, 0, :], QG[:, 1, :], KG)
                for i in range(3):
                    evac(qk[i])
                    st.wait()
                    st.tell(act.activation(S[:, 4 + i, :], qk[i], ACT.Square), g_sq)
                evac(VG.rearrange("p t n -> p (t n)"))
                for c in range(2):
                    evac(U[:, c, :], func=ACT.Gelu_apprx_tanh)
                for c in range(2):
                    evac(SV[:, c, :], func=ACT.Gelu_apprx_tanh)
                for i in range(3):
                    act.wait_ge(g_stat, i + 1)
                    rms(i, 4 + i, 1.0 / 64, g_rstd)
                for a, sq, p in ((CQ[:, 0, :], H[:, 2, :], P), (CQ[:, 1, :], H[:, 3, :], QL - P), (CKV, H[:, 6, :], P)):
                    evac(a[0:p], slice(0, p))
                    st.wait()
                    st.tell(act.activation(sq[0:p], a[0:p], ACT.Square), m_sq)
                evac(KR[64:HM, :], slice(64, HM))
                for i in range(2):
                    act.wait_ge(m_stat, i + 1)
                    rms(3 + i, (7, 4)[i], 1.0 / (QL, KVL)[i], m_rstd)
                act_variance(act, st, ln_s, lambda c: SV[:, c, :], lambda c: H[:, 4 + c, :], r_sgu)
                for hh in range(4):
                    evac(QF[0:HM, hh, :], slice(0, HM))
                for hh in range(4):
                    evac(KF[0:64, hh, :], slice(0, 64))
                for half in range(2):
                    evac(VF[:, 2 * half:2 * half + 2, :].rearrange("p t n -> p (t n)"))
                act_variance(act, st, ln_a, lambda c: CV[:, c, :], lambda c: CSQ[:, c, :], r_conv)
                act_shift(act, st, ln_s, lambda c: SV[:, c, :], lambda c: SV[:, c, :], lambda c: col2("sg_b", c))
                for c, b in enumerate((5, 6)):
                    act.wait_ge(svt_done, c + 1)
                    st.tell(act.activation(SVT[:, :, c * P:(c + 1) * P], bank[b][:, :].rearrange("p (t n) -> p t n", t=TT), ACT.Copy), svt_laid)
                act_shift(act, st, ln_a, lambda c: CV[:, c, :], lambda c: H[:, c, :], lambda c: col2("la_b", c), ACT.Silu)
                act_attention(act, st, l_cfg)
                x, h = (lambda k: X[:, k, :]), (lambda k: H[:, k, :])
                act.wait_ge(r_done, DC)


                def weights_high(n):
                    ks = k_chunks(n)
                    act.wait_ge(half_landed[n % 2], 16 * (n // 2 + 1))
                    if n >= 2:
                        act.wait_ge(*unit_used(n - 2))
                    st.tell(act.activation(WHL[n % 2][:, 0, 0:ks, :], raw_half(n), ACT.Copy), wh_done)

                def product_high(j):
                    for i in range(2):
                        c = 2 * j + i
                        if c == PARTS[2][0]:
                            act.wait_ge(r_done, DC + DC)
                        act.wait_ge(f_act, c + 1)
                        st.tell(act.activation(product_parts(c)[0], QKVG[:, 14 + i, :], ACT.Copy), ph_done)

                weights_high(0)
                weights_high(1)
                act_variance(act, st, ln_m, x, h)
                for c in range(DC):
                    act.wait_ge(ln_m["scaled"], c + 1)
                    st.tell(act.activation(XH[:, c, :], X[:, c, :], ACT.Identity, bias=col2("mix_b", c)), xh_done)
                for c in range(DC):
                    act.wait_ge(xl_done, c + 1)
                    st.tell(act.activation(X[:, c, :], X[:, c, :], ACT.Identity, bias=col2("mix_b", c)), ln_m["ready"])
                for n, (kind, a, b) in enumerate(units):
                    if n and units[n - 1][0] == "up" and units[n - 1][2]:
                        product_high(units[n - 1][1])
                    if kind == "up" and b:
                        for i in range(2):
                            act.wait_ge(f_free, 4 * a + i + 1)
                            q = QKVG[:, 2 * (a % 2) + i, :]
                            st.tell(act.activation(q, q, ACT.Silu), f_silu)
                    if n + 2 < len(units):
                        weights_high(n + 2)
                act.wait_ge(*unit_used(len(units) - 1))
                act_layernorm(act, st, ln_f, x, h, x, lambda c: col2("ffn_b", c))
                st.wait()
                end_of_layer(act, l)
            act.dma_start(out.rearrange("(k p) t -> p k t", p=P), X[:, :, :]).then_inc(s_out, 16)
            act.wait_ge(s_out, 16)

        block = ctx.enter_context(nc.Block())

        @block.sync
        def _(sp):
            sp.dma_start(konst[:, :], A["konst"]).then_inc(s_const, 16)
            sp.dma_start(cols[:, :], A["cols"]).then_inc(s_const, 16)
            sp.dma_start(MT, A["memT"].rearrange("(k p) m -> p k m", p=P)).then_inc(s_mem, 16)
            for n, (src, _, _) in enumerate(first_uses):
                if n == 2:
                    sp.dma_start(X[:, :, :], A["xT"].rearrange("(k p) t -> p k t", p=P)).then_inc(s_x, 16)
                if n >= RING:
                    sp.wait_ge(*first_uses[n - RING][1:])
                sp.dma_start(ring[n % RING][:, :, :], src).then_inc(w_landed[n % RING], 16)
            moe_sync(sp)
            layer_sync(sp)

        @block.gpsimd
        def _(pool):
            st = Steps(pool, pool_own)
            st.do(pool.memset(gatew[:, :, :, :], 0.0))
            st.do(pool.memset(ext[:, :], 0.0))
            st.wait()
            for g, w in enumerate(("rnn_wa", "rnn_wx")):
                for half in range(2):
                    pool.dma_start(gatew[64 * half:64 * half + 64, g, :, 64 * half:64 * half + 64],
                                   A[w].rearrange("(c h) i o -> h i c o", h=2)[half]).then_inc(s_gates, 16)
            pool.dma_start(ext[:, NEXT - 2 * CLIP:], A["rel_rev"][:, 0:2 * CLIP]).then_inc(s_biasd, 16)
            pool.wait_ge(s_biasd, 16)
            st.do(pool.tensor_copy(ext[:, 0:NEXT - 2 * CLIP],
                                   ext[:, NEXT - 2 * CLIP:NEXT - 2 * CLIP + 1].to_broadcast([HEADS, NEXT - 2 * CLIP])))
            st.wait()
            pool.dma_start(ext_dram, ext[:, :]).then_inc(s_biasd, 16)
            pool.wait_ge(s_biasd, 32)
            pool.dma_start(ext_copies, bass.AP(ext_dram.tensor, 0, [[0, P], [NEXT, HEADS], [1, NEXT]])).then_inc(s_biasd, 16)
            pool.wait_ge(s_biasd, 48)
            pool.dma_start(AUX[:, :, :], bass.AP(ext_copies.tensor, P - 1, [[HEADS * NEXT - 1, P], [NEXT, HEADS], [1, T]])).then_inc(s_biasd, 16)
            pool.wait_ge(s_biasd, 64)
            pool.memset(AUX[0:CHUNK, :, T - CHUNK:T], NEG).then_inc(s_bias, 1)
            moe_gpsimd(pool, st)
            layer_gpsimd(pool)

        def pe_stats(pe, name, src, n=T, acc=bank[7]):
            i, before, chunks = chunks_before[name]
            if i:
                pe.wait_ge(rstd_done, i)
            for c in range(chunks):
                pe.wait_ge(sq_done, before + c + 1)
                mm = pe.matmul(acc[:, 0:n], ones, src(c), start=(c == 0), stop=(c == chunks - 1))
            mm.then_inc(stat_done, 1)

        def pe_attention(pe, cfg):
            s, units = cfg["sems"], cfg["units"]
            before, outs = cfg["base"]
            for step in range(len(units) + 3):
                u = step
                if u < len(units):
                    x = units[u]
                    if u >= 3:
                        pe.wait_ge(s["shifted"], before + u - 2)
                    for i, (q, k) in enumerate(x["scores"]):
                        mm = pe.matmul(bank[u % 3][:, 0:x["keys"]], q, k, start=(i == 0), stop=(i == len(x["scores"]) - 1))
                    mm.then_inc(s["scored"], 1)
                u = step - 2
                if 0 <= u < len(units):
                    x = units[u]
                    pe.wait_ge(s["normed"], before + u + 1)
                    if u >= 2:
                        pe.wait_ge(s["laid"], before + u - 1)
                    for kt in range(x["keys"] // P):
                        mm = pe.transpose(bank[3 + u % 2][:, kt * P:(kt + 1) * P], SS[:, u % 3, kt * P:(kt + 1) * P], ident)
                    mm.then_inc(s["turned"], 1)
                u = step - 3
                if 0 <= u < len(units):
                    x = units[u]
                    t = slice(x["t"] * P, (x["t"] + 1) * P)
                    pe.wait_ge(s["laid"], before + u + 1)
                    need = outs_before(cfg, u)
                    need -= len(x["values"]) == 1
                    if x["t"] == 0 and need > 0:
                        pe.wait_ge(s["att_out"], outs + need)
                    for b, r, v in x["values"]:
                        last = x["keys"] // P - 1
                        for kt in range(last + 1):
                            mm = pe.matmul(bank[b][r, t], v(kt), PT[:, x["pt"], kt, t], start=(kt == 0), stop=(kt == last))
                    mm.then_inc(s["summed"], 1)

        def dve_attention(dve, st, cfg):
            s, units = cfg["sems"], cfg["units"]
            before, outs = cfg["base"]
            for step in range(len(units) + 1):
                u = step
                if u < len(units):
                    x = units[u]
                    n = x["keys"]
                    dve.wait_ge(s["scored"], before + u + 1)
                    if u >= 3:
                        dve.wait_ge(s["turned"], before + u - 2)
                    if x["bias"]:
                        aux, h = x["bias"]
                        st.tell(dve.tensor_tensor(SS[:, u % 3, 0:n], bank[u % 3][:, 0:n], aux[:, h, T - n:T], ALU.add), s["shifted"])
                        st.wait()
                        st.tell(dve.tensor_reduce(stats[:, 0, u:u + 1], SS[:, u % 3, 0:n], AX.X, ALU.max, negate=True), s["shifted_max"])
                    else:
                        st.tell(dve.tensor_scalar(SS[:, u % 3, 0:n], bank[u % 3][:, 0:n], -x.get("scale", cfg["scale"]), None, ALU.mult, ALU.min,
                                                  accum_out=stats[:, 0, u:u + 1]), s["shifted"])
                u = step - 1
                if 0 <= u:
                    n = units[u]["keys"]
                    dve.wait_ge(s["expd"], before + u + 1)
                    st.do(dve.reciprocal(stats[:, 2, u:u + 1], stats[:, 1, u:u + 1]))
                    st.wait()
                    st.tell(dve.tensor_scalar(SS[:, u % 3, 0:n], SS[:, u % 3, 0:n], stats[:, 2, u:u + 1], None, ALU.mult), s["normed"])

        def act_attention(act, st, cfg, extra=lambda u: None):
            s, units = cfg["sems"], cfg["units"]
            before, outs = cfg["base"]
            for step in range(len(units) + 3):
                u = step
                if u < len(units):
                    x = units[u]
                    n = x["keys"]
                    act.wait_ge(s["shifted_max"] if x["bias"] else s["shifted"], before + u + 1)
                    st.tell(act.activation(SS[:, u % 3, 0:n], SS[:, u % 3, 0:n], ACT.Exp, bias=stats[:, 0, u:u + 1],
                                           scale=1.0 if x["bias"] else -1.0, accum_out=stats[:, 1, u:u + 1]), s["expd"])
                u = step - 2
                if 0 <= u < len(units):
                    x = units[u]
                    n = x["keys"]
                    act.wait_ge(s["turned"], before + u + 1)
                    if u >= 2 * TT:
                        act.wait_ge(s["summed"], before + u - 2 * TT + 1)
                    st.tell(act.activation(PT[:, x["pt"], 0:n // P, x["t"] * P:(x["t"] + 1) * P],
                                           bank[3 + u % 2][:, 0:n].rearrange("p (k t) -> p k t", t=P), ACT.Copy), s["laid"])
                u = step - 3
                if 0 <= u and units[u]["out"]:
                    act.wait_ge(s["summed"], before + u + 1)
                    for c, b in units[u]["out"]:
                        st.tell(act.activation(cfg["dest"](c), bank[b][:, :], ACT.Copy), s["att_out"])


        @block.tensor
        def _(pe):
            uses = [0]

            def slot():
                n = uses[0]
                uses[0] += 1
                pe.wait_ge(w_landed[n % RING], 16 * (n // RING + 1))
                return ring[n % RING]


            tiles = [0]

            def tile(mms, done=tile_done, free=tile_free, count=tiles, banks=4):
                n = count[0]
                if n >= banks:
                    pe.wait_ge(free, n - banks + 1)
                mms(bank[n % banks]).then_inc(done, 1)
                count[0] += 1

            def project(src, n=T, hwait=None, chunks=4, after=None, **kw):
                w = slot()
                for m in range(chunks):
                    def mms(b):
                        for k in range(DC):
                            if hwait is not None and m == 0:
                                pe.wait_ge(h_done, hwait + k + 1)
                            mm = pe.matmul(b[:, 0:n], w[:, k, m * P:(m + 1) * P], src(k), start=(k == 0), stop=(k == DC - 1))
                        return mm
                    tile(mms, **kw)
                    if after:
                        after(m)

            def tokens(src, tt):
                w = slot()
                for t in range(tt):
                    def mms(b):
                        for k in range(DC):
                            mm = pe.matmul(b[:, :], src(k)[:, t * P:(t + 1) * P], w[:, k, :], start=(k == 0), stop=(k == DC - 1))
                        return mm
                    tile(mms)

            pe.wait_ge(s_const, 32)
            pe_stats(pe, "mem", lambda c: S[:, 12 + c // 2, (c % 2) * MEM:(c % 2) * MEM + MEM], MEM)
            pe_stats(pe, "ln1", lambda c: H[:, c, :])
            mt = lambda k: MT[:, k, :]
            h = lambda k: H[:, k, :]
            project(mt, MEM, hwait=0)
            project(mt, MEM)
            tokens(mt, 2)
            tokens(mt, 2)
            project(h, hwait=chunks_before["ln1"][1])
            project(h)
            pe.wait_ge(s_gates, 64)

            def gates(m):
                pe.wait_ge(xc_done, m + 1)
                if m:
                    pe.wait_ge(gate_free, 2 * m)
                for g in range(2):
                    pe.matmul(bank[5 + g][:, :], gatew[:, g, m, :], XC[:, m, :], start=True, stop=True).then_inc(gate_done, 1)

            project(h, after=gates)
            project(h)
            tokens(h, TT)
            pe.wait_ge(tile_free, tiles[0])
            pe_attention(pe, att_cfg[0])
            pe_stats(pe, "gn_rnn", lambda c: S[:, c, :])
            pe_stats(pe, "gn_att", lambda c: S[:, 4 + c, :])
            rt = [0]
            res = dict(done=res_done, free=res_free, count=rt)
            project(h, hwait=chunks_before["gn_rnn"][1], **res)
            project(h, **res)
            pe_stats(pe, "ln2", h)
            pe.wait_ge(res_free, rt[0])
            project(h, hwait=chunks_before["ln2"][1])
            project(h)
            pe.wait_ge(tile_free, tiles[0])
            pe_attention(pe, att_cfg[1])
            pe.wait_ge(att["att_out"], HEADS // 2 + 8)
            project(h, **res)
            project(h, **res)
            pe_stats(pe, "ln3", h)
            moe_tensor(pe)

        def dve_norm(dve, st, name, src, dst, w=None, n=T):
            i, before, chunks = chunks_before[name]
            dve.wait_ge(rstd_done, i + 1)
            for c in range(chunks):
                st.tell(dve.scalar_tensor_tensor(dst(c), src(c), col(w or name, c), rstd[:, 0:n], ALU.mult, ALU.mult), h_done)

        def dve_residual(dve, st, first, scale=None):
            for m in range(DC):
                dve.wait_ge(res_done, first + m + 1)
                st.tell(dve.tensor_tensor(X[:, m, :], X[:, m, :], bank[(first + m) % 4][:, :], ALU.add), res_free)

        @block.vector
        def _(dve):
            st = Steps(dve, dve_own)
            st.do(dve.memset(eps[:, 0:1], EPS))
            st.do(dve.memset(eps[:, 1:2], LN_EPS))
            st.do(dve.memset(eps[:, 2:3], 1e-30))
            st.do(dve.memset(eps[:, 3:4], 1.0))
            dve.wait_ge(s_mem, 16)
            dve_norm(dve, st, "mem", lambda c: MT[:, c, :], lambda c: MT[:, c, :], n=MEM)
            dve.wait_ge(s_x, 16)
            dve_norm(dve, st, "ln1", lambda c: X[:, c, :], lambda c: H[:, c, :])
            lam = cols[:, C1["lam"]:C1["lam"] + HC]
            sm = lambda i: small[:, 4 * i:4 * i + 4]
            dve.wait_ge(rg_done, 1)
            dve.wait_ge(rg_done, 2)
            st.do(dve.tensor_scalar(sm(3), sm(1), 1.0, None, ALU.add)); st.wait()
            st.do(dve.reciprocal(sm(4), sm(3)))
            st.do(dve.tensor_scalar(sm(5), sm(3), -1.0, None, ALU.add)); st.wait()
            st.do(dve.tensor_tensor(sm(5), sm(1), sm(5), ALU.subtract)); st.wait()
            st.do(dve.tensor_tensor(sm(5), sm(5), sm(4), ALU.mult)); st.wait()
            st.do(dve.tensor_tensor(sm(5), sm(5), sm(2), ALU.add)); st.wait()
            st.do(dve.tensor_scalar(sm(6), lam, -1.0, 0.0, ALU.mult, ALU.max)); st.wait()
            st.do(dve.tensor_tensor(sm(5), sm(5), sm(6), ALU.add)); st.wait()
            st.do(dve.tensor_scalar(sm(7), sm(5), 8.0, None, ALU.mult))
            st.do(dve.tensor_scalar(sm(8), sm(5), -8.0, None, ALU.mult))
            for c in range(HC):
                dve.wait_ge(tile_free, 12 + c + 1)
                tap = lambda i: col("conv_w", i * HC + c)
                st.do(dve.tensor_scalar(XC[:, c, :], XR[:, c, :], tap(3), col("conv_b", c), ALU.mult, ALU.add))
                for i in (2, 1, 0):
                    o = 3 - i
                    st.wait()
                    ins = dve.scalar_tensor_tensor(XC[:, c, o:T], XR[:, c, 0:T - o], tap(i), XC[:, c, o:T], ALU.mult, ALU.add)
                    st.tell(ins, xc_done) if i == 0 else st.do(ins)
            for c in range(HC):
                dve.wait_ge(rg_done, 2 + 2 * c + 2)
                st.do(dve.tensor_tensor(IG[:, c, :], IG[:, c, :], XC[:, c, :], ALU.mult))
            for c in range(HC):
                dve.wait_ge(ia_done, 2 * c + 2)
                st.do(dve.tensor_tensor(XR[:, c, :], AD[:, c, :], AD[:, c, :], ALU.mult)); st.wait()
                st.tell(dve.scalar_tensor_tensor(RG[:, c, :], XR[:, c, :], 1.0, RG[:, c, :], ALU.add, ALU.mult), y_rnn)
            for c in range(HC):
                dve.wait_ge(nh_done, c + 1)
                st.do(dve.tensor_tensor(IG[:, c, :], IG[:, c, :], RG[:, c, :], ALU.mult)); st.wait()
                st.do(dve.tensor_tensor_scan(XC[:, c, :], AD[:, c, :], IG[:, c, :], 0.0, ALU.mult, ALU.add)); st.wait()
                st.tell(dve.tensor_tensor(G[:, c, :], G[:, c, :], XC[:, c, :], ALU.mult), y_rnn)
            dve.wait_ge(s_bias, 1)
            dve_attention(dve, st, att_cfg[0])
            dve_norm(dve, st, "gn_rnn", lambda c: G[:, c, :], lambda c: H[:, c, :])
            dve_norm(dve, st, "gn_att", lambda c: S[:, 12 + c, :], lambda c: H[:, 4 + c, :])
            dve_residual(dve, st, 0)
            dve_norm(dve, st, "ln2", lambda c: X[:, c, :], lambda c: H[:, c, :])
            dve_attention(dve, st, att_cfg[1])
            dve_residual(dve, st, 8)
            dve_norm(dve, st, "ln3", lambda c: X[:, c, :], lambda c: H[:, c, :])
            moe_vector(dve, st)

        def act_squares(act, st, name, src, dst):
            for c in range(chunks_before[name][2]):
                st.tell(act.activation(dst(c), src(c), ACT.Square), sq_done)

        def act_rstd(act, st, name, n=T, acc=bank[7], size=None, e=0):
            i, before, chunks = chunks_before[name]
            act.wait_ge(stat_done, i + 1)
            if before:
                act.wait_ge(h_done, before)
            st.do(act.activation(rstd[:, 0:n], acc[:, 0:n], ACT.Ln, scale=1.0 / (chunks * P), bias=eps[:, e:e + 1])); st.wait()
            st.tell(act.activation(rstd[:, 0:n], rstd[:, 0:n], ACT.Exp, scale=-0.5), rstd_done)

        @block.scalar
        def _(act):
            st = Steps(act, act_own)
            act.wait_ge(s_mem, 16)
            act_squares(act, st, "mem", lambda c: MT[:, c, :], lambda c: S[:, 12 + c // 2, (c % 2) * MEM:(c % 2) * MEM + MEM])
            act.wait_ge(s_x, 16)
            act_squares(act, st, "ln1", lambda c: X[:, c, :], lambda c: H[:, c, :])
            act.wait_ge(dve_own, 4)
            act_rstd(act, st, "mem", MEM)
            act_rstd(act, st, "ln1")
            act.wait_ge(s_const, 32)
            lam = cols[:, C1["lam"]:C1["lam"] + HC]
            sm = lambda i: small[:, 4 * i:4 * i + 4]
            st.do(act.activation(sm(0), lam, ACT.Abs)); st.wait()
            st.tell(act.activation(sm(1), sm(0), ACT.Exp, scale=-1.0), rg_done); st.wait()
            st.tell(act.activation(sm(2), sm(1), ACT.Ln, bias=eps[:, 3:4]), rg_done)

            n = [0]

            def evac(dst, src, func=ACT.Copy, scale=1.0):
                act.wait_ge(tile_done, n[0] + 1)
                st.tell(act.activation(dst, src(bank[n[0] % 4]), func, scale=scale), tile_free)
                n[0] += 1

            for m in range(DC):
                evac(KM[:, m, :], lambda b: b[:, 0:MEM])
            for j in range(2):
                for t in range(2):
                    evac(VM[:, t, j * 512:(j + 1) * 512], lambda b: b[:, :])
            full = lambda b: b[:, :]
            for c in range(HC):
                evac(XR[:, c, :], full)
            for c in range(HC):
                evac(G[:, c, :], full, ACT.Gelu_apprx_tanh)
            for c in range(HC):
                evac(Q[:, c, :], full, scale=HD ** -0.5)
                for g, (dst, b) in enumerate(((RG, "ba"), (IG, "bx"))):
                    act.wait_ge(gate_done, 2 * c + g + 1)
                    st.tell(act.activation(dst[:, c, :], bank[5 + g][:, :], ACT.Sigmoid, bias=col(b, c)), gate_free)
                st.told.setdefault(rg_done.name, 0)
                st.wait()
                act.sem_inc(rg_done, 2)
            act.wait_ge(dve_own, 4 + 10)
            for c in range(HC):
                evac(K[:, c, :], full)
                st.tell(act.activation(AD[:, c, :], RG[:, c, :], ACT.Exp, scale=small[:, 32 + c:33 + c]), ia_done)
                st.tell(act.activation(RG[:, c, :], RG[:, c, :], ACT.Tanh, scale=small[:, 28 + c:29 + c]), ia_done)
            for t in range(TT):
                evac(V[:, t, :], full)
                act.wait_ge(y_rnn, t + 1)
                st.tell(act.activation(RG[:, t, :], RG[:, t, :], ACT.Sqrt, bias=eps[:, 2:3]), nh_done)
            act.wait_ge(y_rnn, 8)
            act_attention(act, st, att_cfg[0])
            for c in range(HC):
                st.tell(act.activation(S[:, c, :], G[:, c, :], ACT.Square), sq_done)
            act_rstd(act, st, "gn_rnn")
            act.wait_ge(att["summed"], 32)
            act.wait_ge(att["att_out"], 4)
            for c in range(HC):
                st.tell(act.activation(S[:, 4 + c, :], S[:, 12 + c, :], ACT.Square), sq_done)
            act_rstd(act, st, "gn_att")
            act.wait_ge(res_done, 8)
            for c in range(DC):
                act.wait_ge(res_free, c + 1)
                st.tell(act.activation(H[:, c, :], X[:, c, :], ACT.Square), sq_done)
            act_rstd(act, st, "ln2")
            for c in range(DC):
                evac(QX[:, c, :], full)
            act_attention(act, st, att_cfg[1])
            act.wait_ge(res_done, 16)
            for c in range(DC):
                act.wait_ge(res_free, 8 + c + 1)
                st.tell(act.activation(H[:, c, :], X[:, c, :], ACT.Square), sq_done)
            act_rstd(act, st, "ln3")
            moe_scalar(act, st)
def layouts(i):
    f = np.float32

    def column(v):
        v = np.asarray(v, f).reshape(-1)
        if v.size % P:
            v = np.concatenate([v, np.zeros(P - v.size % P, f)])
        return v.reshape(-1, P).T

    r = {}
    r["xT"] = np.asarray(i["x"])[0].T
    r["memT"] = np.asarray(i["mem"])[0].T
    parts = [i["ln1_w"], i["conv_w"], i["conv_b"], i["rnn_ba"], i["rnn_bx"], i["rnn_lambda"], i["gn_rnn_w"],
             i["gn_att_w"], i["ln2_w"], i["mem_norm_w"], i["ln3_w"], i["final_norm_w"], i["ln_in_g_2"], i["ln_in_b_2"]]
    r["cols"] = np.concatenate([column(v) for v in parts], axis=1)
    for w in ("w_in", "w_out", "xq_w", "xk_w", "xv_w", "xo_w", "rnn_wa", "rnn_wx"):
        r[w] = np.asarray(i[w])[0]
    r["router_w"] = np.concatenate([np.asarray(i["router_group_w"])[0], np.asarray(i["router_expert_w"])[0].transpose(1, 0, 2).reshape(D, EXPERTS)], axis=1)
    r["router_b"] = np.concatenate([np.asarray(i["router_group_b"])[0], np.asarray(i["router_expert_b"])[0].reshape(-1)])
    for w in ("expert_gate_w", "expert_up_w", "expert_down_w"):
        r[w] = np.asarray(i[w])[0]
    r["rel_rev"] = np.asarray(i["rel_bias"])[0][:, ::-1]
    k = np.arange(P)
    pair = (k[:, None] // 64 == k[None, :] // 64)

    def perm(rows):
        m = np.zeros((P, P), f)
        for d in rows:
            if d % 32 < 16:
                m[d + 16, d] = -1.0
            else:
                m[d - 16, d] = 1.0
        return m

    half = [d for d in range(P)]
    def perm_mla():
        m = np.zeros((P, P), f)
        for d in range(64, HM):
            if d % 16 < 8:
                m[d + 8, d] = -1.0
            else:
                m[d - 8, d] = 1.0
        return m
    r["konst"] = np.concatenate([np.eye(P), np.ones((P, P)), k[:, None] < k[None, :], pair, perm(half), perm_mla(),
                                 np.tile(np.arange(EPG, 0, -1), (P, 1)), np.tile(np.arange(TABLE), (P, 1))],
                                axis=1).astype(f)
    l2 = {n[:-2]: np.asarray(v) for n, v in i.items() if n.endswith("_2")}
    names = ["conv_a_w", "conv_a_b", "ln_a_g", "ln_a_b", "qk_norm_q", "qk_norm_k", "sgu_ln_g", "sgu_ln_b", "mla_q_norm",
             "mla_kv_norm", "ln_mix_g", "ln_mix_b", "ffn_conv_w", "ffn_conv_b", "ln_ffn_g", "ln_ffn_b"]

    def vectors(l):
        return [np.tile(l2[n][l], 2) if n.startswith("qk_norm") else l2[n][l] for n in names]
    r["cols2"] = np.stack([np.concatenate([column(v) for v in vectors(l)], axis=1) for l in range(L2)])
    r["w_in_2"], r["w_out_2"] = l2["w_in"], l2["w_out"]
    r["ffn_w_up"], r["ffn_w_down"] = l2["ffn_w_up"], l2["ffn_w_down"]
    r["w_uq"], r["w_ukv"] = l2["mla_w_uq"], l2["mla_w_ukv"]
    r["sgu_wT"] = l2["sgu_w"].transpose(0, 3, 1, 2)
    r["sgu_b"] = l2["sgu_b"]
    t = np.arange(T)
    row, colm = (t // 64).astype(f), (t % 64).astype(f)

    def angles(dims, half):
        freq = (f(10000.0) ** (-np.arange(half, dtype=f) / f(half))).astype(f)
        return np.stack([(row if (d % (4 * half)) < 2 * half else colm) * freq[d % half] for d in range(dims)]).astype(f)
    a64 = angles(P, 16)
    a96 = np.zeros((P, T), f)
    a96[64:HM] = angles(ROPE, 8)
    r["rotary"] = np.stack([np.cos(a64), np.sin(a64), np.cos(a96), np.sin(a96)], axis=1).astype(f)
    return r


def kernel(**inputs):
    import numpy as _np
    import concourse.bacc as _bacc
    from concourse import mybir as _mybir
    from concourse.bass_utils import run_bass_kernel_spmd as _run

    nc = _bacc.Bacc("TRN2", target_bir_lowering=False, num_devices=1)
    arrays, A = {}, {}
    for name, a in layouts(inputs).items():
        a = _np.ascontiguousarray(a)
        arrays[f"in_{name}"] = a
        A[name] = nc.dram_tensor(f"in_{name}", a.shape, _mybir.dt.from_np(a.dtype), kind="ExternalInput").ap()
    out = nc.dram_tensor("out_0", (D, T), F32, kind="ExternalOutput").ap()
    build(nc, A, out)
    r = _run(nc, [arrays], core_ids=[0])
    return r.results[0]["out_0"].T.reshape(1, T, D)
```
